# Optimizing a Trainium2 kernel written in Bass

```python
import functools
import jax
import jax.numpy as jnp
from jax import lax
import numpy as np

D_MODEL = 1024
BATCH = 1
SEQ = 256
DEPTH = 1
DEC_BATCH = 8
DEC_SEQ = 4
PAST_LEN = 1024
PAGE_SIZE = 128

HEAD_DIM = 64
SB_HEADS = D_MODEL // (2 * HEAD_DIM)
MB_HEADS = D_MODEL // (2 * HEAD_DIM)
SB_WIDTH = SB_HEADS * HEAD_DIM
MB_WIDTH = MB_HEADS * HEAD_DIM
Q_BLOCK = 128
MOBA_BLOCK = 256
MOBA_TOPK = 3
ROPE_THETA = 10000.0
N_EXPERTS = 32
TOP_K = 4
D_FF = D_MODEL
SWIGLU_LIMIT = 7.0
SWIGLU_ALPHA = 1.702
ROUTE_BLOCK = 128
NORM_EPS = 1e-6
N_MOD = 6
ATTN_SCALE = HEAD_DIM ** -0.5
IN_SPLITS = (SB_WIDTH, SB_WIDTH, SB_WIDTH, MB_WIDTH, MB_WIDTH, MB_WIDTH, D_MODEL, D_MODEL)
IN_COLS = sum(IN_SPLITS)

kernel_name = 'hybrid_stickbreak_moba_moe_step'

def rms_norm(x, g):
    xf = x.astype(jnp.float32)
    y = xf * lax.rsqrt(jnp.mean(xf * xf, axis=-1, keepdims=True) + NORM_EPS)
    return (y * g.astype(jnp.float32)).astype(x.dtype)

def rope(x, pos):
    inv_freq = ROPE_THETA ** (-jnp.arange(0, HEAD_DIM, 2, dtype=jnp.float32) / HEAD_DIM)
    ang = pos.astype(jnp.float32)[:, None] * inv_freq[None, :]
    cos = jnp.cos(ang)[None, :, None, :]
    sin = jnp.sin(ang)[None, :, None, :]
    x1, x2 = jnp.split(x.astype(jnp.float32), 2, axis=-1)
    return jnp.concatenate([x1 * cos - x2 * sin, x2 * cos + x1 * sin], axis=-1).astype(x.dtype)

def adaln(c, w_ada, b_ada):
    mod = jax.nn.silu(c) @ w_ada + b_ada
    return jnp.split(mod[:, None, :], N_MOD, axis=-1)

def modulate(x, g, shift, scale):
    return rms_norm(x, g) * (1.0 + scale) + shift

def project_mixer_inputs(h, pos, w_in, q_norm_g, k_norm_g):
    b, t, _ = h.shape
    p = h @ w_in
    bounds = np.cumsum(IN_SPLITS)[:-1].tolist()
    q_sb, k_sb, v_sb, q_mb, k_mb, v_mb, g_sb, g_mb = jnp.split(p, bounds, axis=-1)
    heads = lambda z: z.reshape(b, t, -1, HEAD_DIM)
    q_mb = rope(rms_norm(heads(q_mb), q_norm_g), pos)
    k_mb = rope(rms_norm(heads(k_mb), k_norm_g), pos)
    return heads(q_sb), heads(k_sb), heads(v_sb), q_mb, k_mb, heads(v_mb), g_sb, g_mb

def stick_breaking_weights(z, allowed):
    log_keep = jnp.where(allowed, jax.nn.log_sigmoid(-z), 0.0)
    later = lax.cumsum(log_keep, axis=z.ndim - 1, reverse=True) - log_keep
    return jnp.where(allowed, jnp.exp(jax.nn.log_sigmoid(z) + later), 0.0)

def sb_prompt(q, k, v):
    b, s, h, d = q.shape
    n_qb = s // Q_BLOCK
    k_pos = jnp.arange(s)
    q_blocks = q.reshape(b, n_qb, Q_BLOCK, h, d).swapaxes(0, 1)

    def one_block(args):
        q_blk, start = args
        q_pos = start + jnp.arange(Q_BLOCK)
        z = jnp.einsum('bthd,bshd->bhts', q_blk, k).astype(jnp.float32) * ATTN_SCALE
        a = stick_breaking_weights(z, k_pos[None, :] < q_pos[:, None])
        return jnp.einsum('bhts,bshd->bthd', a.astype(v.dtype), v)

    out = lax.map(one_block, (q_blocks, jnp.arange(n_qb) * Q_BLOCK))
    return out.swapaxes(0, 1).reshape(b, s, h * d)

def sb_sample(q, k_past, v_past, k_new, v_new):
    b, t, h, d = q.shape
    past = k_past.shape[1]
    q_pos = past + jnp.arange(t)
    k_pos = jnp.arange(past + t)
    z = jnp.concatenate([jnp.einsum('bthd,bshd->bhts', q, k_past),
                         jnp.einsum('bthd,bshd->bhts', q, k_new)], axis=-1)
    z = z.astype(jnp.float32) * ATTN_SCALE
    a = stick_breaking_weights(z, k_pos[None, :] < q_pos[:, None]).astype(v_past.dtype)
    out = (jnp.einsum('bhts,bshd->bthd', a[..., :past], v_past)
           + jnp.einsum('bhts,bshd->bthd', a[..., past:], v_new))
    return out.reshape(b, t, h * d)

def pad_blocks(x):
    pad = (-x.shape[1]) % MOBA_BLOCK
    return jnp.pad(x, ((0, 0), (0, pad), (0, 0), (0, 0)))

def block_means(k):
    b, l, h, d = k.shape
    kb = k.reshape(b, l // MOBA_BLOCK, MOBA_BLOCK, h, d).astype(jnp.float32)
    return jnp.mean(kb, axis=2).astype(k.dtype)

def moba_group(q, q_pos, k, v, k_mean):
    n_kb, h, _ = k_mean.shape
    t = q.shape[0]
    k_sel = min(MOBA_TOPK, n_kb)
    own = q_pos[0] // MOBA_BLOCK
    gate = jnp.einsum('thd,nhd->htn', q, k_mean).astype(jnp.float32)
    gate = jnp.where(jnp.arange(n_kb) < own, gate, -jnp.inf)
    _, sel = lax.top_k(gate, k_sel)
    sel_ok = jnp.arange(k_sel) < own
    k_blocks = k.reshape(n_kb, MOBA_BLOCK, h, HEAD_DIM).transpose(2, 0, 1, 3)
    v_blocks = v.reshape(n_kb, MOBA_BLOCK, h, HEAD_DIM).transpose(2, 0, 1, 3)
    h_idx = jnp.arange(h)[:, None, None]
    k_g = k_blocks[h_idx, sel]
    v_g = v_blocks[h_idx, sel]
    s_sel = jnp.einsum('thd,htkbd->htkb', q, k_g).astype(jnp.float32) * ATTN_SCALE
    s_sel = jnp.where(sel_ok[:, None], s_sel, -jnp.inf).reshape(h, t, k_sel * MOBA_BLOCK)
    own_start = own * MOBA_BLOCK
    own_k = lax.dynamic_slice_in_dim(k, own_start, MOBA_BLOCK, axis=0)
    own_v = lax.dynamic_slice_in_dim(v, own_start, MOBA_BLOCK, axis=0)
    own_pos = own_start + jnp.arange(MOBA_BLOCK)
    s_own = jnp.einsum('thd,bhd->htb', q, own_k).astype(jnp.float32) * ATTN_SCALE
    s_own = jnp.where(own_pos[None, :] <= q_pos[:, None], s_own, -jnp.inf)
    p = jax.nn.softmax(jnp.concatenate([s_sel, s_own], axis=-1), axis=-1).astype(v.dtype)
    p_sel = p[..., :k_sel * MOBA_BLOCK].reshape(h, t, k_sel, MOBA_BLOCK)
    p_own = p[..., k_sel * MOBA_BLOCK:]
    return (jnp.einsum('htkb,htkbd->thd', p_sel, v_g)
            + jnp.einsum('htb,bhd->thd', p_own, own_v))

def moba_prompt(q, k, v):
    b, s, h, d = q.shape
    kp, vp = pad_blocks(k), pad_blocks(v)
    km = block_means(kp)
    n_qb = s // Q_BLOCK
    q_items = q.reshape(b * n_qb, Q_BLOCK, h, d)
    item = jnp.arange(b * n_qb)
    b_idx = item // n_qb
    starts = (item % n_qb) * Q_BLOCK

    def one_item(args):
        q_blk, bi, start = args
        return moba_group(q_blk, start + jnp.arange(Q_BLOCK), kp[bi], vp[bi], km[bi])

    out = lax.map(one_item, (q_items, b_idx, starts))
    return out.reshape(b, s, h * d)

def moba_sample(q, k_past, v_past, k_new, v_new):
    b, t, h, d = q.shape
    past = k_past.shape[1]
    kf = pad_blocks(jnp.concatenate([k_past, k_new], axis=1))
    vf = pad_blocks(jnp.concatenate([v_past, v_new], axis=1))
    km = block_means(kf)
    q_pos = past + jnp.arange(t)
    out = jax.vmap(moba_group, in_axes=(0, None, 0, 0, 0))(q, q_pos, kf, vf, km)
    return out.reshape(b, t, h * d)

def merge_branches(o_sb, o_mb, g_sb, g_mb, w_br_sb, w_br_mb, w_out):
    u = jax.nn.sigmoid(g_sb) * (o_sb @ w_br_sb) + jax.nn.sigmoid(g_mb) * (o_mb @ w_br_mb)
    return u @ w_out

def moe_ffn(x, w_router, b_router, w_gu, b_gu, w_down, b_down):
    n, d = x.shape
    logits = (x @ w_router).astype(jnp.float32) + b_router.astype(jnp.float32)
    top_logit, top_e = lax.top_k(logits, TOP_K)
    gate = jax.nn.softmax(top_logit, axis=-1).astype(x.dtype)
    nk = n * TOP_K
    flat_e = top_e.reshape(-1)
    order = jnp.argsort(flat_e)
    e_sorted = flat_e[order]
    tok_sorted = order // TOP_K
    counts = jnp.bincount(flat_e, length=N_EXPERTS)
    padded = (counts + ROUTE_BLOCK - 1) // ROUTE_BLOCK * ROUTE_BLOCK
    start = jnp.cumsum(counts) - counts
    pend = jnp.cumsum(padded)
    pstart = pend - padded
    dest = pstart[e_sorted] + jnp.arange(nk) - start[e_sorted]
    n_blocks = (nk + N_EXPERTS * (ROUTE_BLOCK - 1) + ROUTE_BLOCK - 1) // ROUTE_BLOCK
    rows = n_blocks * ROUTE_BLOCK
    row_tok = jnp.full((rows,), n, jnp.int32).at[dest].set(tok_sorted.astype(jnp.int32))
    row_gate = jnp.zeros((rows,), x.dtype).at[dest].set(gate.reshape(-1)[order])
    block_e = jnp.minimum(
        jnp.searchsorted(pend, jnp.arange(n_blocks) * ROUTE_BLOCK, side='right'), N_EXPERTS - 1)
    x_rows = jnp.concatenate([x, jnp.zeros((1, d), x.dtype)], axis=0)[row_tok]
    x_rows = x_rows.reshape(n_blocks, ROUTE_BLOCK, d)

    def expert_block(args):
        xb, e = args
        gu = xb @ w_gu[e] + b_gu[e]
        g, u = jnp.split(gu, 2, axis=-1)
        g = jnp.minimum(g, SWIGLU_LIMIT)
        u = jnp.clip(u, -SWIGLU_LIMIT, SWIGLU_LIMIT)
        glu = g * jax.nn.sigmoid(SWIGLU_ALPHA * g)
        return ((u + 1.0) * glu) @ w_down[e] + b_down[e]

    y_rows = lax.map(expert_block, (x_rows, block_e)).reshape(rows, d)
    y = jax.ops.segment_sum(y_rows * row_gate[:, None], row_tok, num_segments=n + 1)
    return y[:n]

def decoder_layer(x, c, pos, attend, w_ada, b_ada, g_norm1, g_norm2, w_in, q_norm_g,
                  k_norm_g, w_br_sb, w_br_mb, w_out, w_router, b_router, w_gu, b_gu,
                  w_down, b_down):
    sh1, sc1, ga1, sh2, sc2, ga2 = adaln(c, w_ada, b_ada)
    h = modulate(x, g_norm1, sh1, sc1)
    q_sb, k_sb, v_sb, q_mb, k_mb, v_mb, g_sb, g_mb = project_mixer_inputs(
        h, pos, w_in, q_norm_g, k_norm_g)
    o_sb, o_mb = attend(q_sb, k_sb, v_sb, q_mb, k_mb, v_mb)
    x = x + ga1 * merge_branches(o_sb, o_mb, g_sb, g_mb, w_br_sb, w_br_mb, w_out)
    h2 = modulate(x, g_norm2, sh2, sc2)
    b, t, dm = h2.shape
    ffn = moe_ffn(h2.reshape(b * t, dm), w_router, b_router, w_gu, b_gu, w_down, b_down)
    x = x + ga2 * ffn.reshape(b, t, dm)
    return x, (k_sb, v_sb, k_mb, v_mb)

def prompt_attend(q_sb, k_sb, v_sb, q_mb, k_mb, v_mb):
    return sb_prompt(q_sb, k_sb, v_sb), moba_prompt(q_mb, k_mb, v_mb)

def sample_attend(past_rows, q_sb, k_sb, v_sb, q_mb, k_mb, v_mb):
    sb_k_past, sb_v_past, mb_k_past, mb_v_past = past_rows
    return (sb_sample(q_sb, sb_k_past, sb_v_past, k_sb, v_sb),
            moba_sample(q_mb, mb_k_past, mb_v_past, k_mb, v_mb))

def gather_pages(cache, layer, page_table):
    rows = cache[layer, page_table]
    db, n_p, ps, h, d = rows.shape
    return rows.reshape(db, n_p * ps, h, d)

def setup_inputs(seed: int = 0) -> dict:
    key = jax.random.key(seed)
    ks = jax.random.split(key, 26)
    f32 = jnp.float32

    def nrm(k, shape, scale=1.0):
        return jax.random.normal(k, shape, f32) * scale

    n_pages = PAST_LEN // PAGE_SIZE
    n_used = DEC_BATCH * n_pages
    n_phys = (5 * n_used + 3) // 4
    page_table = jax.random.permutation(ks[8], n_phys)[:n_used].reshape(
        DEC_BATCH, n_pages).astype(jnp.int32)
    sb_cache = (DEPTH, n_phys, PAGE_SIZE, SB_HEADS, HEAD_DIM)
    mb_cache = (DEPTH, n_phys, PAGE_SIZE, MB_HEADS, HEAD_DIM)
    L = DEPTH
    return {
        'x_prompt': nrm(ks[0], (BATCH, SEQ, D_MODEL)),
        'x_sample': nrm(ks[1], (DEC_BATCH, DEC_SEQ, D_MODEL)),
        'c_prompt': nrm(ks[2], (BATCH, D_MODEL)),
        'c_sample': nrm(ks[3], (DEC_BATCH, D_MODEL)),
        'cache_sb_k': nrm(ks[4], sb_cache),
        'cache_sb_v': nrm(ks[5], sb_cache),
        'cache_mb_k': nrm(ks[6], mb_cache),
        'cache_mb_v': nrm(ks[7], mb_cache),
        'page_table': page_table,
        'w_ada': nrm(ks[9], (L, D_MODEL, N_MOD * D_MODEL), D_MODEL ** -0.5),
        'b_ada': nrm(ks[10], (L, N_MOD * D_MODEL), 0.02),
        'g_norm1': 1.0 + nrm(ks[11], (L, D_MODEL), 0.02),
        'g_norm2': 1.0 + nrm(ks[12], (L, D_MODEL), 0.02),
        'w_in': nrm(ks[13], (L, D_MODEL, IN_COLS), D_MODEL ** -0.5),
        'q_norm_g': 1.0 + nrm(ks[14], (L, HEAD_DIM), 0.02),
        'k_norm_g': 1.0 + nrm(ks[15], (L, HEAD_DIM), 0.02),
        'w_br_sb': nrm(ks[16], (L, SB_WIDTH, D_MODEL), SB_WIDTH ** -0.5),
        'w_br_mb': nrm(ks[17], (L, MB_WIDTH, D_MODEL), MB_WIDTH ** -0.5),
        'w_out': nrm(ks[18], (L, D_MODEL, D_MODEL), D_MODEL ** -0.5),
        'w_router': nrm(ks[19], (L, D_MODEL, N_EXPERTS), D_MODEL ** -0.5),
        'b_router': nrm(ks[20], (L, N_EXPERTS), 0.01),
        'w_gu': nrm(ks[21], (L, N_EXPERTS, D_MODEL, 2 * D_FF), D_MODEL ** -0.5),
        'b_gu': nrm(ks[22], (L, N_EXPERTS, 2 * D_FF), 0.02),
        'w_down': nrm(ks[23], (L, N_EXPERTS, D_FF, D_MODEL), D_FF ** -0.5),
        'b_down': nrm(ks[24], (L, N_EXPERTS, D_MODEL), 0.02),
    }

def reference(x_prompt, x_sample, c_prompt, c_sample, cache_sb_k, cache_sb_v, cache_mb_k,
              cache_mb_v, page_table, w_ada, b_ada, g_norm1, g_norm2, w_in, q_norm_g,
              k_norm_g, w_br_sb, w_br_mb, w_out, w_router, b_router, w_gu, b_gu, w_down,
              b_down):
    seq = x_prompt.shape[1]
    past = page_table.shape[1] * cache_sb_k.shape[2]
    pos_prompt = jnp.arange(seq, dtype=jnp.int32)
    pos_sample = past + jnp.arange(x_sample.shape[1], dtype=jnp.int32)
    y_prompt, y_sample = x_prompt, x_sample
    rows_prompt, rows_sample = [], []
    for layer in range(DEPTH):
        lw = (w_ada[layer], b_ada[layer], g_norm1[layer], g_norm2[layer], w_in[layer],
              q_norm_g[layer], k_norm_g[layer], w_br_sb[layer], w_br_mb[layer],
              w_out[layer], w_router[layer], b_router[layer], w_gu[layer], b_gu[layer],
              w_down[layer], b_down[layer])
        y_prompt, new_p = decoder_layer(y_prompt, c_prompt, pos_prompt, prompt_attend, *lw)
        past_rows = (gather_pages(cache_sb_k, layer, page_table),
                     gather_pages(cache_sb_v, layer, page_table),
                     gather_pages(cache_mb_k, layer, page_table),
                     gather_pages(cache_mb_v, layer, page_table))
        y_sample, new_s = decoder_layer(y_sample, c_sample, pos_sample,
                                        functools.partial(sample_attend, past_rows), *lw)
        rows_prompt.append(new_p)
        rows_sample.append(new_s)
    sb_k_prompt = jnp.stack([r[0] for r in rows_prompt])
    sb_v_prompt = jnp.stack([r[1] for r in rows_prompt])
    mb_k_prompt = jnp.stack([r[2] for r in rows_prompt])
    mb_v_prompt = jnp.stack([r[3] for r in rows_prompt])
    sb_k_sample = jnp.stack([r[0] for r in rows_sample])
    sb_v_sample = jnp.stack([r[1] for r in rows_sample])
    mb_k_sample = jnp.stack([r[2] for r in rows_sample])
    mb_v_sample = jnp.stack([r[3] for r in rows_sample])
    return (y_prompt, y_sample, sb_k_prompt, sb_v_prompt, mb_k_prompt, mb_v_prompt,
            sb_k_sample, sb_v_sample, mb_k_sample, mb_v_sample)


_drawn_inputs = setup_inputs


def setup_inputs(seed=0):
    import zlib

    import numpy as np

    out = dict(_drawn_inputs(seed))
    spreads = {}
    factors = {'g_norm1': 2.856,
     'q_norm_g': 6.342,
     'k_norm_g': 3.009,
     'b_router': 2.83,
     'b_gu': 6.609,
     'b_down': 8.0}
    for name, (base, spread) in spreads.items():
        noise = np.random.default_rng([zlib.crc32(name.encode()), seed]).standard_normal(out[name].shape)
        drawn = base * np.exp(spread * noise) if base else spread * noise
        out[name] = jnp.asarray(drawn.astype(out[name].dtype))
    for name, factor in factors.items():
        out[name] = (out[name] * factor).astype(out[name].dtype)
    return out
```

```python
from contextlib import ExitStack

import concourse.bass as bass
import numpy as np
from concourse import mybir

F32 = mybir.dt.float32
F32R = mybir.dt.float32r
I32 = mybir.dt.int32
U32 = mybir.dt.uint32
ALU = mybir.AluOpType
ACT = mybir.ActivationFunctionType
AX = mybir.AxisListType

P = 128
D = 1024
DT = D // P
HD = 64
HEADS = 8
BW = HEADS * HD
PAIRS = BW // P
NPR = 256
NSEQ, NNEW = 8, 4
NSM = NSEQ * NNEW
NTOK = NPR + NSM
TILES = [(0, P), (P, P), (NPR, NSM)]
NT = len(TILES)
PAST = 1024
PAGES = PAST // P
HALF = PAGES // 2
MOBA = 256
NMB = PAST // MOBA
MTOP = 3
NE, TOPK = 32, 4
FF = 1024
CAP = P
LIMIT, ALPHA = 7.0, 1.702
EPS = 1e-6
SCALE = HD ** -0.5
NMOD = 6
SLOTS = 4
SLOTW = 2048
SPLITW = 1024
SPLITS = 6
POOL_EVERY = 4
OFF = float(1 << 20)
NEG = -1e30

CONST = {}
_at = 0
for _name, _n in (("ident", P), ("ones", P), ("below", P), ("iota", P), ("strict", P), ("causal", P),
                  ("cos", NT * HD // 2), ("sin", NT * HD // 2), ("newsb", 2 * NSM), ("newmb", 2 * NSM),
                  ("row4", NT)):
    CONST[_name] = (_at, _at + _n)
    _at += _n
NCONST = _at


def constants():
    c = np.zeros((P, NCONST), np.float32)

    def put(name, x):
        a, b = CONST[name]
        c[:, a:b] = x

    i = np.arange(P)
    put("ident", np.eye(P))
    put("ones", 1.0)
    put("below", i[:, None] < i[None, :])
    put("iota", i[None, :])
    put("strict", i[None, :] < i[:, None])
    put("causal", np.where(i[None, :] <= i[:, None], 0.0, NEG))
    inv = (np.float32(10000.0) ** (-np.arange(0, HD, 2, dtype=np.float32) / np.float32(HD))).astype(np.float32)
    pos = np.zeros((NT, P), np.float32)
    pos[0], pos[1] = i, P + i
    pos[2, :NSM] = PAST + np.arange(NSM) % NNEW
    ang = (pos[:, :, None] * inv).astype(np.float32)
    put("cos", np.cos(ang).transpose(1, 0, 2).reshape(P, -1))
    put("sin", np.sin(ang).transpose(1, 0, 2).reshape(P, -1))
    b, t = i // (HEADS * NNEW), i % NNEW
    kb, kt = np.arange(NSM) // NNEW, np.arange(NSM) % NNEW
    same = [(b[:, None] + 4 * g) == kb[None, :] for g in range(2)]
    put("newsb", np.concatenate([s & (kt[None, :] < t[:, None]) for s in same], 1))
    put("newmb", np.concatenate([np.where(s & (kt[None, :] <= t[:, None]), 0.0, NEG) for s in same], 1))
    put("row4", TOPK * (i[:, None] + np.array([a for a, _ in TILES])[None, :]) - OFF)
    return c


def build(nc, t, o):
    ctx = ExitStack()
    with ctx:
        def sb(name, shape, dt=F32):
            return ctx.enter_context(nc.sbuf_tensor(name, shape, dt))

        def sem(name):
            return ctx.enter_context(nc.semaphore(name))

        PS = ctx.enter_context(nc.psum_tensor("PS", [P, 8, 512], F32))
        ring = sb("ring", [P, SLOTS, SLOTW])
        WH, WL = sb("WH", [P, SPLITS, SPLITW], F32R), sb("WL", [P, SPLITS, SPLITW], F32R)
        XH, XL = sb("XH", [P, DT, P], F32R), sb("XL", [P, DT, P], F32R)
        HH, HL = sb("HH", [P, DT, P], F32R), sb("HL", [P, DT, P], F32R)
        xT = sb("xT", [P, DT, NTOK])
        hT = sb("hT", [P, DT, NTOK])
        modT = sb("modT", [P, NMOD * DT, 1 + NSEQ])
        gs = sb("gs", [P, 2, DT, 1 + NSEQ])
        cst = sb("cst", [P, NCONST])
        small = sb("small", [P, 1600])
        ptab = sb("ptab", [1, NSEQ * PAGES], I32)
        cnt_i = sb("cnt_i", [1, 1], I32)
        idx_cur = sb("idx_cur", [P, 1], U32)
        i8 = sb("i8", [P, NT, 8], U32)
        arena = sb("arena", [P, 19600])

        cursor = [0]

        def carve(width, start=None):
            if start is not None:
                cursor[0] = start
            a = cursor[0]
            cursor[0] += width
            assert cursor[0] <= 19600, cursor[0]
            return arena[:, a:a + width]

        def c3(ap, b):
            return ap.rearrange("p (a b) -> p a b", b=b)

        qT = [c3(carve(PAIRS * NTOK, 0 if r == 0 else None), NTOK) for r in range(2)]
        kT = [c3(carve(PAIRS * NTOK), NTOK) for _ in range(2)]
        vn_at = cursor[0]
        vn = [c3(carve(NT * BW), BW) for _ in range(2)]
        oT = [c3(carve(PAIRS * NTOK), NTOK) for _ in range(2)]
        QP = carve(NSEQ * PAIRS * 32).rearrange("p (b a c) -> p b a c", a=PAIRS, c=32)
        KT_at = cursor[0]
        KT = carve(2 * PAIRS * 512).rearrange("p (s a c) -> p s a c", a=PAIRS, c=512)
        ROWW = PAST + NSM
        Z, T1, T2 = carve(ROWW), carve(ROWW), carve(ROWW)
        W_at = cursor[0] - 3 * ROWW
        AT = c3(carve((PAGES + 1) * P), P)
        pv_rows = AT[:, 0:PAIRS, :].rearrange("p a b -> p (a b)")
        W_end = cursor[0]
        mod_rows = c3(carve(2 * SLOTW, vn_at), SLOTW)
        cursor[0] = W_end
        xn = c3(carve(NT * D, KT_at), D)
        nat = [c3(carve(NT * BW, KT_at), BW), c3(carve(NT * BW), BW)]
        natks = c3(carve(NT * BW), BW)
        PW = 2 * 3 * P
        pt1 = [carve(PW, W_at).rearrange("p (h c) -> p h c", h=2), carve(PW).rearrange("p (h c) -> p h c", h=2)]
        pt2 = [carve(PW).rearrange("p (h c) -> p h c", h=2), carve(PW).rearrange("p (h c) -> p h c", h=2)]
        pAT = AT[:, 0:6, :].rearrange("p (h c) k -> p h (c k)", h=2)
        uT = c3(carve(DT * NTOK, KT_at), NTOK)
        sg = c3(carve(4 * NTOK), NTOK)
        h2n = c3(carve(NT * D, 0), D)
        acc = c3(carve(NT * D), D)
        ga2n = c3(carve(2 * D), D)
        last_at = cursor[0]
        bb = carve(2 * FF)
        g1, u1, e1 = carve(512), carve(512), carve(512)
        hb = carve(FF)
        last_rows = carve(TOPK * D, last_at)
        yb = carve(D)
        bdn = carve(D)
        onehot = c3(carve(NT * P), P)
        bgrow = carve(2 * FF)
        gx = c3(carve(DT * NSM), NSM)
        MOE_END = cursor[0]

        scur = [0]

        def tiny(n, w=None):
            a = scur[0]
            scur[0] += n
            assert scur[0] <= 1600
            ap = small[:, a:a + n]
            return ap if w is None else c3(ap, w)

        badaT = tiny(NMOD * DT)
        gT = tiny(2 * DT)
        sT = tiny(DT * 9, 9)
        rst = tiny(NTOK)
        qkg = tiny(2 * HD, HD)
        ssh_at = scur[0]
        ssh = tiny(NT * HEADS * 2).rearrange("p (r a b) -> p r a b", r=2, b=HEADS)
        mx = tiny(4, 2)
        ls = tiny(4, 2)
        gt8, m8d, f8d, sel8 = tiny(8), tiny(8), tiny(8), tiny(8)
        dmx, dls = tiny(1), tiny(1)
        LG = tiny(NT * NE, NE)
        m8 = tiny(NT * 8, 8)
        f8 = tiny(NT * 8, 8)
        gt4 = tiny(NT * TOPK, TOPK)
        gls = tiny(NT)
        ngm = tiny(NT)
        oh = tiny(NT * NE, NE)
        msk = tiny(NT * NE, NE)
        gD = tiny(NT * NE, NE)
        pos = tiny(NT * (NE + 1), NE + 1)
        val = tiny(NT * (NE + 1) * 2).rearrange("p (a e c) -> p a e c", a=NT, c=2)
        cnt = tiny(1)
        infos = tiny((NE + 1) * 2, 2)
        gcur = tiny(1)
        brt = tiny(NE)
        wr = sb("wr", [P, DT, NE])
        GT = sb("GT", [NE, NTOK])
        cn = carve(D, 15700)
        ce = carve(D)
        ban = carve(P)
        gn = carve(P)

        def K(name, rows=P):
            a, b = CONST[name]
            return cst[0:rows, a:b]

        ident, ones, below, iota = K("ident"), K("ones"), K("below"), K("iota")
        strict, causal = K("strict"), K("causal")
        cosv, sinv = c3(K("cos"), HD // 2), c3(K("sin"), HD // 2)
        newsb, newmb = c3(K("newsb"), NSM), c3(K("newmb"), NSM)
        row4 = K("row4")

        Y4 = nc.dram_tensor("choice_rows", (NTOK * TOPK, D), F32, kind="Internal").ap()

        in_const, in_c, in_x, in_misc, in_pt = sem("in_const"), sem("in_c"), sem("in_x"), sem("in_misc"), sem("in_pt")
        landed = [sem(f"landed{s}") for s in range(SLOTS)]
        used = sem("used")
        c_sig, c_silu = sem("c_sig"), sem("c_silu")
        set_fill, set_copy = sem("set_fill"), sem("set_copy")
        sq_ready, ssq_done, ms_ready, rstd_ready = sem("sq_ready"), sem("ssq_done"), sem("ms_ready"), sem("rstd_ready")
        h_ready = sem("h_ready")
        proj_free = sem("proj_free")
        nat_ready = sem("nat_ready")
        nat_ms, nat_rs = sem("nat_ms"), sem("nat_rs")
        tr_fill, tr_free = sem("tr_fill"), sem("tr_free")
        qp_zero, qp_ready = sem("qp_zero"), sem("qp_ready")
        out_rows = sem("out_rows")
        pz_fill, pz_free, pl_ready, pd_ready, pe_ready, pw_ready = (
            sem("pz_fill"), sem("pz_free"), sem("pl_ready"), sem("pd_ready"), sem("pe_ready"), sem("pw_ready"))
        at_fill, at_copy, po_fill, po_copy = sem("at_fill"), sem("at_copy"), sem("po_fill"), sem("po_copy")
        kt_fill, kt_act, kt_dve = sem("kt_fill"), sem("kt_act"), sem("kt_dve")
        s_fill, z_copy, dl_ready, dd_ready, de_ready, aw_ready = (
            sem("s_fill"), sem("z_copy"), sem("dl_ready"), sem("dd_ready"), sem("de_ready"), sem("aw_ready"))
        aw_fill, aw_copy, pv_copy = sem("aw_fill"), sem("aw_copy"), sem("pv_copy")
        pt_fill, oh_copy = sem("pt_fill"), sem("oh_copy")
        mod_copy, mod_fill, mod_ready = sem("mod_copy"), sem("mod_fill"), sem("mod_ready")
        gate_ready, b_free = sem("gate_ready"), sem("b_free")
        x1_ready = sem("x1_ready")
        gx_ready = sem("gx_ready")
        rt_fill, rt_copy = sem("rt_fill"), sem("rt_copy")
        lg_fill, mask_ready, rank_fill, rank_read, gl_ready, ge_ready = (
            sem("lg_fill"), sem("mask_ready"), sem("rank_fill"), sem("rank_read"), sem("gl_ready"), sem("ge_ready"))
        gT_fill, gT_copy, bd_fill, acc_ready = sem("gT_fill"), sem("gT_copy"), sem("bd_fill"), sem("acc_ready")
        oh_ready, gathered, info_fill, info_ready = sem("oh_ready"), sem("gathered"), sem("info_fill"), sem("info_ready")
        high_ready, low_dve, low_pool, parts_used = sem("high_ready"), sem("low_dve"), sem("low_pool"), sem("parts_used")
        xh_ready, xl_ready, hh_ready, hl_ready = sem("xh_ready"), sem("xl_ready"), sem("hh_ready"), sem("hl_ready")
        g1_ready, e_ready, hb_ready = sem("g1_ready"), sem("e_ready"), sem("hb_ready")
        hg_fill, y_scaled = sem("hg_fill"), sem("y_scaled")
        cur_ready, scattered, rows_out = sem("cur_ready"), sem("scattered"), sem("rows_out")
        brow_in, bb_ready, bb_used = sem("brow_in"), sem("bb_ready"), sem("bb_used")
        back_in, y_ready, y_out, in_bd = sem("back_in"), sem("y_ready"), sem("y_out"), sem("in_bd")
        back = [sem(f"back{i}") for i in range(NT)]
        dve_done, act_done, pool_done = sem("dve_done"), sem("act_done"), sem("pool_done")
        dve_loop, pool_step, sp_step = sem("dve_loop"), sem("pool_step"), sem("sp_step")

        cache_k = [t["cache_sb_k"], t["cache_mb_k"]]
        cache_v = [t["cache_sb_v"], t["cache_mb_v"]]
        w_ada = t["w_ada"][0].rearrange("(k p) n -> p k n", p=P)
        w_in = t["w_in"][0].rearrange("(k p) n -> p k n", p=P)
        w_out = t["w_out"][0].rearrange("(k p) n -> p k n", p=P)
        w_br = [t["w_br_sb"][0].rearrange("(k p) n -> p k n", p=P), t["w_br_mb"][0].rearrange("(k p) n -> p k n", p=P)]
        stream = []
        for c in range(3):
            for k in range(DT):
                stream.append(("w", w_ada[:, k, c * SLOTW:(c + 1) * SLOTW]))

        def add_cols(w, col):
            for kh in range(w.shape[1] // 4):
                stream.append(("w4", w[:, 4 * kh:4 * kh + 4, col:col + 512]))

        for c in range(6):
            add_cols(w_in, 512 * c)
        pages_at = {}
        for kind, gi in (("k", 0), ("k", 1), ("v", 0), ("k", 2), ("v", 1), ("k", 3), ("v", 2), ("v", 3)):
            r, g = divmod(gi, 2)
            pages_at[kind, gi] = len(stream)
            for b in range(4 * g, 4 * g + 4):
                for hf in range(2):
                    stream.append(("pages", (cache_k if kind == "k" else cache_v)[r], b * PAGES + hf * HALF))
        for c in range(2):
            for r in range(2):
                add_cols(w_in, 6 * BW + r * D + 512 * c)
                add_cols(w_br[r], 512 * c)
        for c in range(2):
            add_cols(w_out, 512 * c)
        NSTREAM = len(stream)
        lands, total = [], [0] * SLOTS
        for n, item in enumerate(stream):
            total[n % SLOTS] += 16 * (HALF if item[0] == "pages" else 1)
            lands.append(total[n % SLOTS])

        def slot(n):
            return ring[:, n % SLOTS, :]

        def slot4(n):
            return c3(ring[:, n % SLOTS, :], 512)

        def await_chunk(eng, n):
            eng.wait_ge(landed[n % SLOTS], lands[n])

        MOD_END = [DT * (c + 1) for c in range(3)]
        PROJ_END = [MOD_END[-1] + 2 * (c + 1) for c in range(6)]
        att = PROJ_END[-1] + 64
        GATE_END = [att + 3 * s + 2 for s in range(4)]
        BRANCH_END = [att + 3 * s + 3 for s in range(4)]
        OUT_END = [att + 12 + 2 * (c + 1) for c in range(2)]
        assert OUT_END[-1] == NSTREAM
        EXP_CHUNKS = 12
        PARTS = EXP_CHUNKS * SLOTW // SPLITW
        assert NSTREAM % SLOTS == 0 and EXP_CHUNKS % SLOTS == 0 and PARTS % SPLITS == 0 and PARTS % POOL_EVERY == 0

        def of_pool(q):
            return q % POOL_EVERY == POOL_EVERY - 1

        def pool_lows(it, q):
            return it * (PARTS // POOL_EVERY) + ((q + 1) // POOL_EVERY)

        def dve_lows(it, q):
            return it * (PARTS - PARTS // POOL_EVERY) + (q + 1 - (q + 1) // POOL_EVERY)

        def raw_part(q):
            at = q % 2 * SPLITW
            return slot(q // 2)[:, at:at + SPLITW]
        w_gu = t["w_gu"][0].rearrange("e (k p) (j n) -> e p k j n", p=P, j=4)
        w_dn = t["w_down"][0].rearrange("e (k p) n -> e p k n", p=P)

        GU = [(h, kh, j) for h in range(2) for kh in range(2) for j in range(2)]

        def proj_bank(c):
            return 4 - 4 * (c % 2)

        block = ctx.enter_context(nc.Block())

        @block.sync
        def _(sp):
            for n, item in enumerate(stream):
                if item[0] == "pages" and stream[n - 1][0] != "pages":
                    sp.wait_ge(in_pt, 16)
                if n >= SLOTS:
                    sp.wait_ge(used, n - SLOTS + 1)
                if item[0] == "w":
                    sp.dma_start(slot(n), item[1]).then_inc(landed[n % SLOTS], 16)
                elif item[0] == "w4":
                    sp.dma_start(slot4(n), item[1]).then_inc(landed[n % SLOTS], 16)
                else:
                    _, cache, at = item
                    for j in range(HALF):
                        page = sp.value_load(ptab[0:1, at + j:at + j + 1], min_val=0, max_val=cache.shape[1] - 1)
                        src = cache[0, bass.ds(page, 1)].rearrange("a p h d -> (a p) (h d)")
                        sp.dma_start(slot4(n)[:, j, :], src).then_inc(landed[n % SLOTS], 16)

            def load_expert_chunk(tp, it, e, j):
                if not isinstance(it, int) or it or j >= SLOTS:
                    before = 2 * (j - SLOTS) + 1
                    sp.wait_ge(low_dve, dve_lows(it, before))
                    sp.sem_inc(sp_step, 1)
                    if not isinstance(it, int) or it or before >= POOL_EVERY - 1:
                        sp.wait_ge(low_pool, pool_lows(it, before))
                else:
                    sp.wait_ge(used, NSTREAM - SLOTS + j + 1)
                one = bass.ds(e, 1)
                if j < 8:
                    h, kh, gu = GU[j]
                    src = w_gu[one, :, 4 * kh:4 * kh + 4, 2 * gu + h, :].rearrange("a p k n -> (a p) k n")
                    sp.dma_start(slot4(j), src).then_inc(landed[j % SLOTS], 16)
                else:
                    src = w_dn[one, :, 2 * (j - 8):2 * (j - 8) + 2, :].rearrange("a p k n -> (a p) k n")
                    sp.dma_start(c3(slot(j), D), src).then_inc(landed[j % SLOTS], 16)

            def load_bias(it, e):
                if not isinstance(it, int) or it:
                    sp.wait_ge(bb_ready, it)
                sp.dma_start(bgrow[0:1, :], t["b_gu"][0, bass.ds(e, 1), :]).then_inc(brow_in, 16)

            def expert_loads(tp):
                load_bias(tp * NE, 0)
                for j in range(SLOTS):
                    load_expert_chunk(tp, tp * NE, 0, j)
                with sp.Fori(0, NE - 1) as e:
                    it = tp * NE + e
                    for j in range(SLOTS, EXP_CHUNKS):
                        load_expert_chunk(tp, it, e, j)
                    load_bias(it + 1, e + 1)
                    for j in range(SLOTS):
                        load_expert_chunk(tp, it + 1, e + 1, j)
                for j in range(SLOTS, EXP_CHUNKS):
                    load_expert_chunk(tp, tp * NE + (NE - 1), NE - 1, j)

            expert_loads(0)
            sp.wait_ge(rank_read, 2)
            most = sp.value_load(cnt_i[0:1, 0:1], min_val=0, max_val=NTOK)
            with sp.Fori(1, NT) as tp:
                with sp.If(most > tp * CAP):
                    expert_loads(tp)
                sp.nop()
            sp.nop()
            for i, (a, n) in enumerate(TILES):
                if i == 0:
                    sp.wait_ge(back_in, 1)
                dst = ring[0:n, 2 * i:2 * i + 2, :].rearrange("p s c -> p (s c)") if i < 2 else last_rows[0:n, :]
                sp.dma_start(dst, Y4[TOPK * a:TOPK * (a + n), :].rearrange("(p k) n -> p (k n)", k=TOPK)
                             ).then_inc(back[i], 16)
            y_dst = [o["y_prompt"][0, 0:P, :], o["y_prompt"][0, P:NPR, :], o["y_sample"].rearrange("b t n -> (b t) n")]
            for i, (a, n) in enumerate(TILES):
                sp.wait_ge(y_ready, i + 1)
                sp.dma_start(y_dst[i], acc[0:n, i, :]).then_inc(y_out, 16)
            sp.wait_ge(y_out, 16 * NT)

        @block.gpsimd
        def _(pool):
            done = [0]

            def chain(ins):
                done[0] += 1
                ins.then_inc(pool_done, 1)
                pool.wait_ge(pool_done, done[0])

            pool.dma_start(ptab[:, :], t["page_table"].rearrange("b n -> (b n)").rearrange("(a n) -> a n", a=1)).then_inc(in_pt, 16)
            pool.dma_start(qkg[:, 0, :], t["q_norm_g"].to_broadcast([P, HD])).then_inc(in_misc, 16)
            pool.dma_start(qkg[:, 1, :], t["k_norm_g"].to_broadcast([P, HD])).then_inc(in_misc, 16)
            pool.dma_start(brt, t["b_router"].to_broadcast([P, NE])).then_inc(in_misc, 16)
            pool.dma_start(wr[:, :, :], t["w_router"][0].rearrange("(k p) e -> p k e", p=P)).then_inc(in_misc, 16)
            pool.memset(QP, 0.0).then_inc(qp_zero, 1)

            outs = [(o["sb_v_prompt"], o["sb_v_sample"], vn[0], proj_free, 3),
                    (o["mb_v_prompt"], o["mb_v_sample"], vn[1], proj_free, 6),
                    (o["mb_k_prompt"], o["mb_k_sample"], nat[1], nat_ready, 2),
                    (o["sb_k_prompt"], o["sb_k_sample"], natks, tr_free, 3)]
            for dp, ds_, src, s, v in outs:
                pool.wait_ge(s, v)
                pool.dma_start(dp[0, 0].rearrange("(a p) h d -> p a (h d)", p=P), src[:, 0:2, :]).then_inc(out_rows, 16)
                pool.dma_start(ds_[0].rearrange("b t h d -> (b t) (h d)"), src[0:NSM, 2, :]).then_inc(out_rows, 16)

            def pad_queries(r):
                for p in range(PAIRS):
                    for s in range(2):
                        rows = slice(HD * s, HD * s + HD)
                        ins = pool.tensor_copy(
                            QP[rows, :, p, (2 * p + s) * NNEW:(2 * p + s + 1) * NNEW],
                            qT[r][rows, p, NPR:NTOK].rearrange("p (b t) -> p b t", t=NNEW))
                ins.then_inc(qp_ready, 1)

            pool.wait_ge(qp_zero, 1)
            pool.wait_ge(tr_free, 9)
            pad_queries(0)
            pool.wait_ge(s_fill, 2)
            pool.wait_ge(qp_ready, 1)
            pad_queries(1)
            pool.wait_ge(x1_ready, 1)
            pool.dma_start(bdn[0:NE, :], t["b_down"][0]).then_inc(in_bd, 16)

            def low_part(it, q):
                pool.wait_ge(high_ready, it * PARTS + (q + 1))
                pool.sem_inc(pool_step, 1)
                pool.tensor_tensor(WL[:, q % SPLITS, :], raw_part(q), WH[:, q % SPLITS, :].bitcast(F32),
                                   ALU.subtract).then_inc(low_pool, 1)

            def biases(it):
                pool.wait_ge(bb_used, it + 1)
                pool.wait_ge(brow_in, (it + 1) * 16)
                pool.sem_inc(pool_step, 1)
                pool.partition_broadcast(bb, bgrow[0:1, :], P).then_inc(bb_ready, 1)

            def expert_pool(tp):
                def body(it, more):
                    for q in (11, 15, 19):
                        low_part(it, q)
                    if more:
                        biases(it + 1)
                    low_part(it, 23)
                    if more:
                        low_part(it + 1, 3)
                    pool.wait_ge(y_scaled, it + 2)
                    pool.sem_inc(pool_step, 1)
                    pool.indirect_dma_start(
                        Y4, bass.IndirectOffsetOnAxis(ap=idx_cur[:, 0:1], axis=0), yb, None,
                        bounds_check=NTOK * TOPK - 1, oob_is_err=False).then_inc(scattered, 16)
                    if more:
                        low_part(it + 1, 7)
                    pool.wait_ge(scattered, (it + 1) * 16)
                    pool.sem_inc(rows_out, 1)

                biases(tp * NE)
                for q in (3, 7):
                    low_part(tp * NE, q)
                with pool.Fori(0, NE - 1) as e:
                    body(tp * NE + e, True)
                body(tp * NE + (NE - 1), False)

            pool.wait_ge(acc_ready, 1)
            pool.sem_inc(rows_out, 1)
            expert_pool(0)
            pool.wait_ge(rank_read, 2)
            most = pool.value_load(cnt_i[0:1, 0:1], min_val=0, max_val=NTOK)
            with pool.Fori(1, NT) as tp:
                with pool.If(most > tp * CAP):
                    expert_pool(tp)
                pool.nop()
            pool.nop()
            pool.sem_inc(back_in, 1)
            pool.wait_ge(out_rows, 16 * 8)

        @block.scalar
        def _(act):
            done = [0]

            def chain(ins):
                done[0] += 1
                ins.then_inc(act_done, 1)
                act.wait_ge(act_done, done[0])

            act.dma_start(cn[0:1, :], t["c_prompt"]).then_inc(in_c, 16)
            act.dma_start(cn[1:1 + NSEQ, :], t["c_sample"]).then_inc(in_c, 16)
            act.dma_start(cst[:, :], t["constants"]).then_inc(in_const, 16)
            act.dma_start(ban[0:NMOD * DT, :], t["b_ada"].rearrange("a (m p) -> (a m) p", p=P)).then_inc(in_c, 16)
            act.dma_start(gn[0:DT, :], t["g_norm1"].rearrange("a (m p) -> (a m) p", p=P)).then_inc(in_c, 16)
            act.dma_start(gn[DT:2 * DT, :], t["g_norm2"].rearrange("a (m p) -> (a m) p", p=P)).then_inc(in_c, 16)
            act.dma_start(xn[:, 0:2, :], t["x_prompt"][0].rearrange("(a p) n -> p a n", p=P)).then_inc(in_x, 16)
            act.dma_start(xn[0:NSM, 2, :], t["x_sample"].rearrange("b t n -> (b t) n")).then_inc(in_x, 16)
            act.wait_ge(in_c, 16 * 5)
            act.activation(ce[0:9, :], cn[0:9, :], ACT.Sigmoid).then_inc(c_sig, 1)
            act.wait_ge(set_copy, 8)
            act.activation(hT[:, :, :], xT[:, :, :], ACT.Square).then_inc(sq_ready, 1)


            def rstd(k):
                act.wait_ge(ms_ready, k + 1)
                act.activation(rst, rst, ACT.Sqrt).then_inc(rstd_ready, 1)

            rstd(0)
            for c in range(3):
                act.wait_ge(used, MOD_END[c])
                if c == 2:
                    act.wait_ge(mod_fill, 1)
                bank = 4 - 4 * (c % 2)
                act.activation(c3(mod_rows[0:9, c % 2, :], 512), PS[0:9, bank:bank + 4, :], ACT.Copy).then_inc(mod_copy, 1)

            def head_rstd(r):
                act.wait_ge(nat_ms, r + 1)
                v = ssh[:, r, :, :]
                act.activation(v, v, ACT.Sqrt).then_inc(nat_rs, 1)

            for c in range(6):
                act.wait_ge(used, PROJ_END[c])
                bank = proj_bank(c)
                if c < 2:
                    dst = (qT if c == 0 else kT)[0]
                    last = act.activation(dst, PS[:, bank:bank + 4, 0:NTOK], ACT.Copy, scale=SCALE if c == 0 else 1.0)
                else:
                    dst = {2: vn[0], 3: nat[0], 4: nat[1], 5: vn[1]}[c]
                    act.activation(dst[:, 0:2, :], PS[:, bank:bank + 2, :], ACT.Copy)
                    last = act.activation(dst[0:NSM, 2, :], PS[0:NSM, bank + 2, :], ACT.Copy)
                last.then_inc(proj_free, 1)
                if c >= 4:
                    head_rstd(c - 4)
            for n in range(9):
                kind, i = divmod(n, 3)
                a, m = TILES[i]
                act.wait_ge(tr_fill, n + 1)
                if kind == 0:
                    last = act.activation(natks[0:m, i, :], PS[0:m, n % 8, :], ACT.Copy)
                else:
                    src = c3(PS[:, n % 8, :], P)[:, :, 0:m]
                    last = act.activation((qT if kind == 1 else kT)[1][:, :, a:a + m], src, ACT.Copy,
                                          scale=SCALE if kind == 1 else 1.0)
                last.then_inc(tr_free, 1)

            def zview(j):
                return PS[:, 2 * (j % 2):2 * (j % 2) + 2, 0:3 * P]

            act.wait_ge(out_rows, 16 * 8)

            def softplus(src, tmp, out_sem):
                chain(act.activation(tmp, src, ACT.Abs))
                chain(act.activation(tmp, tmp, ACT.Exp, scale=-1.0))
                act.activation(tmp, tmp, ACT.Ln, bias=1.0).then_inc(out_sem, 1)

            def front(j):
                if j < 4:
                    act.wait_ge(pz_fill, j + 1)
                    if j >= 2:
                        act.wait_ge(pe_ready, j - 1)
                    softplus(zview(j), pt1[j % 2], pl_ready)

            front(0)
            for j in range(8):
                if j + 1 < 8:
                    front(j + 1)
                act.wait_ge(pd_ready, j + 1)
                if j < 4:
                    act.activation(pt2[j % 2], pt1[j % 2], ACT.Exp).then_inc(pe_ready, 1)
                else:
                    for h in range(2):
                        act.activation(pt2[j % 2][:, h, 0:P], pt1[j % 2][:, h, 0:P], ACT.Exp,
                                       bias=mx[:, h, 0:1], accum_out=ls[:, h, 0:1])
                        last = act.activation(pt2[j % 2][:, h, P:3 * P], pt1[j % 2][:, h, P:3 * P], ACT.Exp,
                                              bias=mx[:, h, 1:2], accum_out=ls[:, h, 1:2])
                    last.then_inc(pe_ready, 1)
                act.wait_ge(at_fill, j + 1)
                act.activation(pAT, PS[:, 4:6, 0:3 * P], ACT.Copy).then_inc(at_copy, 1)
                act.wait_ge(po_fill, j + 1)
                act.activation(oT[j // 4][:, j % 4, 0:NPR], PS[:, 6 + j % 2, 0:NPR], ACT.Copy).then_inc(po_copy, 1)

            def evacuate_keys(gi, a, b):
                for tp in range(32 * gi + HALF * a, 32 * gi + HALF * b, 2):
                    act.wait_ge(kt_fill, tp + 1)
                    act.activation(KT[:, (tp // HALF) % 2, :, (tp % HALF) * P:(tp % HALF + 1) * P],
                                   c3(PS[:, 0, :], P), ACT.Copy).then_inc(kt_act, 1)

            def copy_scores(gi):
                act.wait_ge(s_fill, gi + 1)
                if gi:
                    act.wait_ge(aw_ready, gi)
                act.activation(c3(Z[:, 0:PAST], 512), PS[:, 2:4, :], ACT.Copy)
                chain(act.activation(Z[:, PAST:ROWW], PS[:, 4, 0:NSM], ACT.Copy))
                act.sem_inc(z_copy, 1)

            def exponentials(gi):
                act.wait_ge(dd_ready, gi + 1)
                if gi < 2:
                    act.activation(T2, T1, ACT.Exp).then_inc(de_ready, 1)
                else:
                    act.activation(T2, T1, ACT.Exp, bias=dmx, accum_out=dls).then_inc(de_ready, 1)

            def copy_weights(gi):
                act.wait_ge(aw_fill, gi + 1)
                if gi:
                    act.wait_ge(pt_fill, gi)
                act.activation(c3(AT[:, 0:PAGES, :].rearrange("p a b -> p (a b)"), 512), PS[:, 5:7, :], ACT.Copy)
                act.activation(AT[0:NSM, PAGES, :], PS[0:NSM, 7, 0:P], ACT.Copy).then_inc(aw_copy, 1)

            def copy_product(gi):
                act.wait_ge(used, pages_at["v", gi] + 8)
                act.activation(pv_rows, PS[:, 4, :], ACT.Copy).then_inc(pv_copy, 1)

            def copy_heads(gi):
                r, g = divmod(gi, 2)
                act.wait_ge(pt_fill, gi + 1)
                for s in range(2):
                    rows = slice(HD * s, HD * s + HD)
                    for p in range(PAIRS):
                        src = c3(PS[rows, 7, p * P:(p + 1) * P], 32)[:, :, (2 * p + s) * NNEW:(2 * p + s + 1) * NNEW]
                        at = NPR + 4 * g * NNEW
                        last = act.activation(oT[r][rows, p, at:at + 4 * NNEW].rearrange("p (b t) -> p b t", t=NNEW), src, ACT.Copy)
                last.then_inc(oh_copy, 1)

            evacuate_keys(0, 0, 8)
            copy_scores(0)
            softplus(Z, T1, dl_ready)
            evacuate_keys(1, 0, 2)
            exponentials(0)
            evacuate_keys(1, 2, 8)
            copy_scores(1)
            for gi in range(4):
                copy_weights(gi)
                if gi + 1 < 4:
                    if gi + 1 < 2:
                        softplus(Z, T1, dl_ready)
                    exponentials(gi + 1)
                copy_product(gi)
                if gi + 2 < 4:
                    evacuate_keys(gi + 2, 0, 1)
                copy_heads(gi)
                if gi + 2 < 4:
                    evacuate_keys(gi + 2, 1, 8)
                    copy_scores(gi + 2)

            for s in range(4):
                act.wait_ge(used, GATE_END[s])
                if s:
                    act.wait_ge(b_free, s)
                act.activation(sg, PS[:, 0:4, 0:NTOK], ACT.Sigmoid).then_inc(gate_ready, 1)
            act.wait_ge(x1_ready, 1)
            act.activation(hT[:, :, :], xT[:, :, :], ACT.Square).then_inc(sq_ready, 1)
            rstd(1)
            for n in range(16):
                act.wait_ge(rt_fill, n + 1)
                if n < 12:
                    i, q = divmod(n % 6, 2)
                    m = TILES[i][1]
                    dst = (h2n if n < 6 else acc)[0:m, i, 512 * q:512 * q + 512]
                    bank = n % 6
                else:
                    i, q = divmod(n - 12, 2)
                    m = P if i == 0 else NSM
                    dst = ga2n[0:m, i, 512 * q:512 * q + 512]
                    bank = n - 12
                act.activation(dst, PS[0:m, bank, :], ACT.Copy).then_inc(rt_copy, 1)
            act.wait_ge(gl_ready, 1)
            for i, (a, m) in enumerate(TILES):
                last = act.activation(gt4[0:m, i, :], m8[0:m, i, 0:TOPK], ACT.Exp, bias=ngm[0:m, i:i + 1],
                                      accum_out=gls[0:m, i:i + 1])
            last.then_inc(ge_ready, 1)
            act.wait_ge(gT_fill, 1)
            act.activation(GT[:, :], PS[0:NE, 6, 0:NTOK], ACT.Copy).then_inc(gT_copy, 1)

            def high_part(it, q):
                if q % 2 == 0:
                    j = q // 2
                    act.wait_ge(landed[j % SLOTS], (it * (EXP_CHUNKS // SLOTS) + (j // SLOTS + 1)) * 16 + total[j % SLOTS])
                act.wait_ge(parts_used, it * PARTS + (q + 1))
                act.activation(WH[:, q % SPLITS, :], raw_part(q), ACT.Copy).then_inc(high_ready, 1)

            def high_rows(it):
                act.wait_ge(gathered, it + 1)
                act.activation(XH.rearrange("p (b c) k -> p b (c k)", b=2), PS[:, 6:8, :], ACT.Copy).then_inc(xh_ready, 1)

            def high_hidden(it, h):
                act.wait_ge(hg_fill, 2 * it + (h + 1))
                act.activation(HH[:, 4 * h:4 * h + 4, :], c3(PS[:, h, :], P), ACT.Copy).then_inc(hh_ready, 1)

            def sigmoid(it, h):
                act.wait_ge(g1_ready, 2 * it + (h + 1))
                act.activation(e1, g1, ACT.Sigmoid, scale=ALPHA).then_inc(e_ready, 1)

            def expert_act(tp):
                def body(it, more):
                    sigmoid(it, 0)
                    for q in range(15, 22):
                        high_part(it, q)
                    high_hidden(it, 0)
                    sigmoid(it, 1)
                    if more:
                        high_rows(it + 1)
                    high_part(it, 22)
                    high_part(it, 23)
                    high_hidden(it, 1)
                    if more:
                        for q in range(6):
                            high_part(it + 1, q)
                    act.wait_ge(parts_used, (it + 1) * PARTS + SPLITS)
                    act.wait_ge(cur_ready, it + 1)
                    act.wait_ge(rows_out, it + 1)
                    act.activation(yb.rearrange("p (b c) -> p b c", b=2), PS[:, 4:6, :], ACT.Copy,
                                   scale=gcur).then_inc(y_scaled, 1)
                    if more:
                        for q in range(6, 15):
                            high_part(it + 1, q)

                for q in range(6):
                    high_part(tp * NE, q)
                high_rows(tp * NE)
                for q in range(6, 15):
                    high_part(tp * NE, q)
                with act.Fori(0, NE - 1) as e:
                    body(tp * NE + e, True)
                body(tp * NE + (NE - 1), False)

            act.sem_inc(y_scaled, 1)
            expert_act(0)
            most = act.value_load(cnt_i[0:1, 0:1], min_val=0, max_val=NTOK)
            with act.Fori(1, NT) as tp:
                with act.If(most > tp * CAP):
                    expert_act(tp)
                act.nop()
            act.nop()

        @block.vector
        def _(dve):
            V = nc.vector
            done = [0]

            def chain(ins):
                done[0] += 1
                ins.then_inc(dve_done, 1)
                dve.wait_ge(dve_done, done[0])

            TT, TS, STT = V.tensor_tensor, V.tensor_scalar, V.scalar_tensor_tensor

            dve.wait_ge(c_sig, 1)
            TT(cn[0:9, :], cn[0:9, :], ce[0:9, :], ALU.mult).then_inc(c_silu, 1)
            dve.wait_ge(set_fill, 1)
            V.tensor_copy(sT, c3(PS[:, 0, 0:DT * 9], 9)).then_inc(set_copy, 1)
            dve.wait_ge(set_fill, 2)
            V.tensor_copy(badaT, PS[:, 1, 0:NMOD * DT])
            V.tensor_copy(gT, PS[:, 1, NMOD * DT:NMOD * DT + 2 * DT]).then_inc(set_copy, 1)
            for n in range(6):
                i, q = divmod(n, 2)
                a, m = TILES[i]
                dve.wait_ge(set_fill, n + 3)
                V.tensor_copy(xT[:, 4 * q:4 * q + 4, a:a + m], c3(PS[:, n + 2, :], P)[:, :, 0:m]).then_inc(set_copy, 1)

            def modulation(c, bank):
                dve.wait_ge(mod_fill, c + 1)
                part = slice(16 * c, 16 * c + 16)
                chain(TT(modT[:, part, :], c3(PS[:, bank, 0:16 * 9], 9),
                         badaT[:, part].unsqueeze(2).to_broadcast([P, 16, 9]), ALU.add))
                dve.sem_inc(mod_ready, 1)

            def scaled_gain(q):
                chain(STT(gs[:, q], modT[:, (3 * q + 1) * DT:(3 * q + 2) * DT, :], 1.0,
                          gT[:, q * DT:(q + 1) * DT].unsqueeze(2).to_broadcast([P, DT, 9]), ALU.add, ALU.mult))

            def norm(k):
                dve.wait_ge(ssq_done, k + 1)
                chain(TS(rst, PS[:, 0, 0:NTOK], 1.0 / D, EPS, ALU.mult, ALU.add))
                V.reciprocal(rst, rst).then_inc(ms_ready, 1)
                if k == 0:
                    modulation(0, 4)
                    scaled_gain(0)
                dve.wait_ge(rstd_ready, k + 1)
                chain(TT(hT[:, :, :], xT[:, :, :], rst.unsqueeze(1).to_broadcast([P, DT, NTOK]), ALU.mult))
                sh = modT[:, 3 * k * DT:(3 * k + 1) * DT, :]
                for m in range(DT):
                    last = TS(hT[:, m, 0:NPR], hT[:, m, 0:NPR], gs[:, k, m, 0:1], sh[:, m, 0:1], ALU.mult, ALU.add)
                hs = hT[:, :, NPR:NTOK].rearrange("p m (b t) -> p m b t", t=NNEW)
                shape = [P, DT, NSEQ, NNEW]
                chain(TT(hs, hs, gs[:, k, :, 1:9].unsqueeze(3).to_broadcast(shape), ALU.mult))
                TT(hs, hs, sh[:, :, 1:9].unsqueeze(3).to_broadcast(shape), ALU.add).then_inc(h_ready, 1)

            norm(0)
            modulation(1, 0)
            modulation(2, 1)
            scaled_gain(1)

            chain(V.memset(small[:, ssh_at:ssh_at + 2 * NT * HEADS], 1.0))
            t3 = c3(T2[:, 0:BW], HD)
            for r in range(2):
                dve.wait_ge(proj_free, 4 + r)
                if r == 0:
                    dve.wait_ge(in_misc, 64)
                x = nat[r]
                for i, (a, m) in enumerate(TILES):
                    xi = x[0:m, i, :]
                    chain(TT(T2[0:m, 0:BW], xi, xi, ALU.mult))
                    chain(V.tensor_reduce(ssh[0:m, r, i, :], t3[0:m], AX.X, ALU.add))
                last = TS(ssh[:, r, 0:2, :], ssh[:, r, 0:2, :], 1.0 / HD, EPS, ALU.mult, ALU.add)
                chain(last)
                chain(TS(ssh[0:NSM, r, 2, :], ssh[0:NSM, r, 2, :], 1.0 / HD, EPS, ALU.mult, ALU.add))
                chain(V.reciprocal(ssh[:, r, :, :], ssh[:, r, :, :]))
                dve.sem_inc(nat_ms, 1)
                dve.wait_ge(nat_rs, r + 1)
                for i, (a, m) in enumerate(TILES):
                    xi = c3(x[0:m, i, :], HD)
                    full = [m, HEADS, HD]
                    chain(TT(xi, xi, ssh[0:m, r, i, :].unsqueeze(2).to_broadcast(full), ALU.mult))
                    chain(TT(xi, xi, qkg[0:m, r, :].unsqueeze(1).to_broadcast(full), ALU.mult))
                    hh = [m, HEADS, HD // 2]
                    co, si = (v[0:m, i, :].unsqueeze(1).to_broadcast(hh) for v in (cosv, sinv))
                    xa, xb = xi[:, :, 0:HD // 2], xi[:, :, HD // 2:HD]
                    ta = c3(T2[0:m, 0:BW // 2], HD // 2)
                    tb = c3(T2[0:m, BW // 2:BW], HD // 2)
                    tc = c3(T1[0:m, 0:BW // 2], HD // 2)
                    TT(ta, xa, si, ALU.mult)
                    TT(tb, xb, si, ALU.mult)
                    TT(tc, xb, co, ALU.mult)
                    chain(TT(xa, xa, co, ALU.mult))
                    TT(xb, ta, tc, ALU.add)
                    chain(TT(xa, xa, tb, ALU.subtract))
                dve.sem_inc(nat_ready, 1)

            def zview(j):
                return PS[:, 2 * (j % 2):2 * (j % 2) + 2, 0:3 * P]

            def diag(ap):
                return ap.rearrange("p h (b k) -> p h b k", k=P)[:, :, 0:3:2, :]

            def over(m):
                return m.unsqueeze(1).unsqueeze(1).to_broadcast([P, 2, 2, P])

            dve.wait_ge(out_rows, 16 * 8)
            for j in range(8):
                a1, a2 = pt1[j % 2], pt2[j % 2]
                if j >= 2:
                    dve.wait_ge(at_fill, j - 1)
                if j < 4:
                    dve.wait_ge(pl_ready, j + 1)
                    chain(STT(a2, zview(j), 0.0, a1, ALU.max, ALU.add))
                    chain(TT(diag(a2), diag(a2), over(strict), ALU.mult))
                    for h in range(2):
                        for lo, hi in ((0, P), (P, 3 * P)):
                            rev = a2[:, h, lo:hi][:, ::-1]
                            last = V.tensor_tensor_scan(a1[:, h, lo:hi][:, ::-1], rev, rev, 0.0, ALU.add, ALU.bypass)
                            if h == 1 and lo:
                                chain(last)
                    chain(TT(a1, zview(j), a1, ALU.subtract))
                    dve.sem_inc(pz_free, 1)
                    dve.sem_inc(pd_ready, 1)
                    dve.wait_ge(pe_ready, j + 1)
                    TT(diag(a2), diag(a2), over(strict), ALU.mult).then_inc(pw_ready, 1)
                else:
                    dve.wait_ge(pz_fill, j + 1)
                    z = zview(j)
                    TT(diag(a1), diag(z), over(causal), ALU.add)
                    chain(V.tensor_copy(a1[:, :, P:2 * P], z[:, :, P:2 * P]))
                    dve.sem_inc(pz_free, 1)
                    V.tensor_reduce(mx[:, :, 0:1], a1[:, :, 0:P], AX.X, ALU.max, negate=True)
                    chain(V.tensor_reduce(mx[:, :, 1:2], a1[:, :, P:3 * P], AX.X, ALU.max, negate=True))
                    dve.sem_inc(pd_ready, 1)
                    dve.wait_ge(pe_ready, j + 1)
                    chain(V.reciprocal(ls, ls))
                    TT(a2[:, :, 0:P], a2[:, :, 0:P], ls[:, :, 0:1].to_broadcast([P, 2, P]), ALU.mult)
                    TT(a2[:, :, P:3 * P], a2[:, :, P:3 * P], ls[:, :, 1:2].to_broadcast([P, 2, 2 * P]),
                       ALU.mult).then_inc(pw_ready, 1)

            chain(V.memset(gt8, -3e38))
            def evacuate_keys(gi, a, b):
                for tp in range(32 * gi + HALF * a + 1, 32 * gi + HALF * b, 2):
                    dve.wait_ge(kt_fill, tp + 1)
                    V.tensor_copy(KT[:, (tp // HALF) % 2, :, (tp % HALF) * P:(tp % HALF + 1) * P],
                                  c3(PS[:, 1, :], P)).then_inc(kt_dve, 1)

            def exponents(gi):
                g = gi % 2
                if gi:
                    dve.wait_ge(aw_fill, gi)
                if gi < 2:
                    dve.wait_ge(dl_ready, gi + 1)
                    chain(STT(T2, Z, 0.0, T1, ALU.max, ALU.add))
                    chain(TT(T2[:, PAST:ROWW], T2[:, PAST:ROWW], newsb[:, g, :], ALU.mult))
                    chain(V.tensor_tensor_scan(T1[:, ::-1], T2[:, ::-1], T2[:, ::-1], 0.0, ALU.add, ALU.bypass))
                    TT(T1, Z, T1, ALU.subtract).then_inc(dd_ready, 1)
                else:
                    dve.wait_ge(z_copy, gi + 1)
                    zb = c3(Z[:, 0:PAST], MOBA)
                    chain(V.tensor_reduce(gt8[:, 0:NMB], zb, AX.X, ALU.add))
                    chain(V.max(m8d, gt8))
                    chain(V.max_index(i8[:, 0, :], m8d, gt8))
                    chain(V.tensor_copy(f8d, i8[:, 0, :]))
                    chain(TS(sel8, iota[:, 0:8], f8d[:, 0:1], -1.0, ALU.is_equal, ALU.add))
                    for q in range(1, MTOP):
                        chain(STT(sel8, iota[:, 0:8], f8d[:, q:q + 1], sel8, ALU.is_equal, ALU.add))
                    chain(TS(sel8, sel8, -NEG, None, ALU.mult))
                    TT(c3(T1[:, 0:PAST], MOBA), zb, sel8[:, 0:NMB].unsqueeze(2).to_broadcast([P, NMB, MOBA]), ALU.add)
                    chain(TT(T1[:, PAST:ROWW], Z[:, PAST:ROWW], newmb[:, g, :], ALU.add))
                    V.tensor_reduce(dmx, T1, AX.X, ALU.max, negate=True).then_inc(dd_ready, 1)

            def weights(gi):
                dve.wait_ge(de_ready, gi + 1)
                if gi < 2:
                    TT(T2[:, PAST:ROWW], T2[:, PAST:ROWW], newsb[:, gi % 2, :], ALU.mult).then_inc(aw_ready, 1)
                else:
                    chain(V.reciprocal(dls, dls))
                    TS(T2, T2, dls, None, ALU.mult).then_inc(aw_ready, 1)

            evacuate_keys(0, 0, 8)
            exponents(0)
            evacuate_keys(1, 0, 2)
            weights(0)
            evacuate_keys(1, 2, 8)
            for gi in range(1, 4):
                exponents(gi)
                weights(gi)
                if gi + 1 < 4:
                    evacuate_keys(gi + 1, 0, 8)

            for s in range(4):
                c, r = divmod(s, 2)
                dve.wait_ge(gate_ready, s + 1)
                dve.wait_ge(used, BRANCH_END[s])
                uc = uT[:, 4 * c:4 * c + 4, :]
                pb = PS[:, 4:8, 0:NTOK]
                if r == 0:
                    chain(TT(uc, pb, sg, ALU.mult))
                else:
                    chain(TT(sg, pb, sg, ALU.mult))
                    chain(TT(uc, uc, sg, ALU.add))
                dve.sem_inc(b_free, 1)
            for c in range(2):
                dve.wait_ge(used, OUT_END[c])
                for m in range(4 * c, 4 * c + 4):
                    STT(xT[:, m, 0:NPR], PS[:, m, 0:NPR], modT[:, 2 * DT + m, 0:1], xT[:, m, 0:NPR], ALU.mult, ALU.add)
                shape = [P, 4, NSEQ, NNEW]
                tmp = sg[:, :, 0:NSM].rearrange("p m (b t) -> p m b t", t=NNEW)
                xs = xT[:, 4 * c:4 * c + 4, NPR:NTOK].rearrange("p m (b t) -> p m b t", t=NNEW)
                ps = PS[:, 4 * c:4 * c + 4, NPR:NTOK].rearrange("p m (b t) -> p m b t", t=NNEW)
                chain(TT(tmp, ps, modT[:, 2 * DT + 4 * c:2 * DT + 4 * c + 4, 1:9].unsqueeze(3).to_broadcast(shape), ALU.mult))
                chain(TT(xs, xs, tmp, ALU.add))
            dve.sem_inc(x1_ready, 1)
            norm(1)
            V.tensor_copy(gx.rearrange("p m (b t) -> p m b t", t=NNEW),
                          modT[:, 5 * DT:6 * DT, 1:9].unsqueeze(3).to_broadcast([P, DT, NSEQ, NNEW])).then_inc(gx_ready, 1)

            dve.wait_ge(lg_fill, 1)
            for i, (a, m) in enumerate(TILES):
                chain(TT(LG[0:m, i, :], PS[0:m, 6, NE * i:NE * i + NE], brt[0:m, :], ALU.add))
                chain(V.max(m8[0:m, i, :], LG[0:m, i, :]))
                chain(V.max_index(i8[0:m, i, :], m8[0:m, i, :], LG[0:m, i, :]))
                chain(V.tensor_copy(f8[0:m, i, :], i8[0:m, i, :]))
                chain(TS(ngm[0:m, i:i + 1], m8[0:m, i, 0:1], -1.0, None, ALU.mult))
            dve.sem_inc(gl_ready, 1)
            chain(V.memset(msk, 0.0))
            chain(V.memset(gD, 0.0))
            chain(V.memset(pos, -1.0))
            chain(V.memset(val, 0.0))
            dve.wait_ge(ge_ready, 1)
            for i, (a, m) in enumerate(TILES):
                row, gate, kk = msk[0:m, i, :], gD[0:m, i, :], val[0:m, i, 0:NE, 1]
                chain(V.reciprocal(gls[0:m, i:i + 1], gls[0:m, i:i + 1]))
                chain(TS(gt4[0:m, i, :], gt4[0:m, i, :], gls[0:m, i:i + 1], None, ALU.mult))
                for q in range(TOPK):
                    one = oh[0:m, i, :]
                    chain(TS(one, iota[0:m, 0:NE], f8[0:m, i, q:q + 1], None, ALU.is_equal))
                    TT(row, row, one, ALU.add)
                    STT(gate, one, gt4[0:m, i, q:q + 1], gate, ALU.mult, ALU.add)
                    chain(STT(kk, one, float(q), kk, ALU.mult, ALU.add))
                chain(TS(kk, kk, row4[0:m, i:i + 1], None, ALU.add))
                chain(V.tensor_copy(val[0:m, i, 0:NE, 0], gate))
            dve.sem_inc(mask_ready, 1)
            dve.wait_ge(rank_fill, 1)
            for i, (a, m) in enumerate(TILES):
                chain(STT(pos[0:m, i, 0:NE], PS[0:m, 7, NE * i:NE * i + NE], 1.0, msk[0:m, i, :], ALU.add, ALU.mult))
                chain(TS(pos[0:m, i, 0:NE], pos[0:m, i, 0:NE], -1.0, None, ALU.add))
            chain(V.tensor_reduce(cnt, PS[:, 7, NT * NE:(NT + 1) * NE], AX.X, ALU.max))
            chain(V.tensor_copy(cnt_i[0:1, :], cnt[0:1, :]))
            dve.sem_inc(rank_read, 2)
            dve.wait_ge(bd_fill, 1)
            dve.wait_ge(rt_copy, 16)
            for i, (a, m) in enumerate(TILES):
                gv = ga2n[0:m, 0 if i < 2 else 1, :]
                tmp = hb[0:m, :]
                chain(TT(c3(tmp, 512), PS[0:m, 2 * i:2 * i + 2, :], c3(gv, 512), ALU.mult))
                chain(TT(acc[0:m, i, :], acc[0:m, i, :], tmp, ALU.add))
            dve.sem_inc(acc_ready, 1)

            def lchain(base, k, ins):
                ins.then_inc(dve_loop, 1)
                dve.wait_ge(dve_loop, base + (k + 1))

            def place(n, e):
                for i, (a, m) in enumerate(TILES):
                    last = TS(onehot[0:m, i, :], iota[0:m, :], pos[0:m, i, bass.ds(e, 1)], None, ALU.is_equal)
                last.then_inc(oh_ready, 1)

            def info(n, e):
                dve.wait_ge(info_fill, n + 1)
                V.tensor_copy(infos[:, bass.ds(e, 1), :].rearrange("p a c -> p (a c)"), PS[:, 3, 0:2]).then_inc(info_ready, 1)

            def low_parts(it, a, b):
                for q in range(a, b):
                    if not of_pool(q):
                        dve.wait_ge(high_ready, it * PARTS + (q + 1))
                        TT(WL[:, q % SPLITS, :], raw_part(q), WH[:, q % SPLITS, :].bitcast(F32),
                           ALU.subtract).then_inc(low_dve, 1)

            def low_rows(it):
                dve.wait_ge(xh_ready, it + 1)
                halves = [v.rearrange("p (b c) k -> p b (c k)", b=2) for v in (XL, XH.bitcast(F32))]
                TT(halves[0], PS[:, 6:8, :], halves[1], ALU.subtract).then_inc(xl_ready, 1)

            def low_hidden(it, h):
                dve.wait_ge(hh_ready, 2 * it + (h + 1))
                part = slice(4 * h, 4 * h + 4)
                TT(HL[:, part, :], c3(PS[:, h, :], P), HH[:, part, :].bitcast(F32), ALU.subtract).then_inc(hl_ready, 1)

            LK = 10

            def expert_dve(tp):
                base = tp * NE
                if not isinstance(tp, int):
                    chain_tp = V.tensor_scalar(pos, pos, -float(CAP), None, ALU.add)
                    lchain(tp * (NE * LK + 1) - 1, 0, chain_tp)
                lb0 = tp * (NE * LK + 1)

                def glu_first(it, lb, h):
                    dve.wait_ge(parts_used, it * PARTS + (SPLITS + 8 * h + 8))
                    if h == 0:
                        dve.wait_ge(bb_ready, it + 1)
                    else:
                        dve.wait_ge(hb_ready, 2 * it + 1)
                    TT(u1, PS[:, 2 * h + 1, :], bb[:, FF + 512 * h:FF + 512 * h + 512], ALU.add)
                    lchain(lb, (0, 4)[h], TT(g1, PS[:, 2 * h, :], bb[:, 512 * h:512 * h + 512], ALU.add))
                    lchain(lb, (1, 5)[h], TS(g1, g1, LIMIT, None, ALU.min))
                    dve.sem_inc(g1_ready, 1)

                def glu_last(it, lb, h):
                    lchain(lb, (2, 8)[h], TS(u1, u1, LIMIT, -LIMIT, ALU.min, ALU.max))
                    lchain(lb, (3, 9)[h], STT(u1, u1, 1.0, g1, ALU.add, ALU.mult))
                    dve.wait_ge(e_ready, 2 * it + (h + 1))
                    TT(hb[:, 512 * h:512 * h + 512], u1, e1, ALU.mult).then_inc(hb_ready, 1)

                def body(it, e, more):
                    lb = lb0 + e * LK
                    low_parts(it, 6, 14)
                    glu_first(it, lb, 0)
                    if more:
                        place(it + 1, e + 1)
                    low_parts(it, 14, 15)
                    glu_last(it, lb, 0)
                    low_parts(it, 15, 22)
                    glu_first(it, lb, 1)
                    dve.sem_inc(bb_used, 1)
                    low_hidden(it, 0)
                    dve.wait_ge(rows_out, it + 1)
                    cur = infos[:, bass.ds(e, 1), :].rearrange("p a c -> p (a c)")
                    lchain(lb, 6, V.tensor_copy(gcur, cur[:, 0:1]))
                    lchain(lb, 7, TS(idx_cur[:, 0:1], cur[:, 1:2], OFF, None, ALU.add))
                    dve.sem_inc(cur_ready, 1)
                    glu_last(it, lb, 1)
                    if more:
                        low_rows(it + 1)
                    low_parts(it, 22, 24)
                    low_hidden(it, 1)
                    if more:
                        info(it + 1, e + 1)
                        dve.wait_ge(info_ready, it + 2)
                        low_parts(it + 1, 0, 6)

                place(base, 0)
                low_parts(base, 0, 6)
                info(base, 0)
                dve.wait_ge(info_ready, base + 1)
                low_rows(base)
                with dve.Fori(0, NE - 1) as e:
                    body(tp * NE + e, e, True)
                body(tp * NE + (NE - 1), NE - 1, False)

            dve.sem_inc(bb_used, 1)
            expert_dve(0)
            most = dve.value_load(cnt_i[0:1, 0:1], min_val=0, max_val=NTOK)
            with dve.Fori(1, NT) as tp:
                with dve.If(most > tp * CAP):
                    expert_dve(tp)
                dve.nop()
            dve.nop()
            for i, (a, m) in enumerate(TILES):
                dve.wait_ge(back[i], 16)
                rows = c3(last_rows[0:m, :], D)
                if i < 2:
                    rows = ring[0:m, 2 * i:2 * i + 2, :].rearrange("p s (k n) -> p (s k) n", n=D)
                chain(TT(rows[:, 0:2, :], rows[:, 0:2, :], rows[:, 2:4, :], ALU.add))
                chain(TT(rows[:, 0, :], rows[:, 0, :], rows[:, 1, :], ALU.add))
                chain(TT(rows[:, 0, :], rows[:, 0, :], ga2n[0:m, 0 if i < 2 else 1, :], ALU.mult))
                chain(TT(acc[0:m, i, :], acc[0:m, i, :], rows[:, 0, :], ALU.add))
                dve.sem_inc(y_ready, 1)

        @block.tensor
        def _(pe):
            T = nc.tensor

            def mm(out, lhsT, rhs, start, stop):
                return T.matmul(out, lhsT, rhs, start=start, stop=stop, skip_group_check=True)

            pe.wait_ge(in_const, 16)
            pe.wait_ge(c_silu, 1)
            for k in range(DT):
                last = T.transpose(PS[:, 0, 9 * k:9 * k + 9], cn[0:9, k * P:(k + 1) * P], ident[0:9, 0:9])
            last.then_inc(set_fill, 1)
            T.transpose(PS[:, 1, 0:NMOD * DT], ban[0:NMOD * DT, :], ident[0:NMOD * DT, 0:NMOD * DT])
            T.transpose(PS[:, 1, NMOD * DT:NMOD * DT + 2 * DT], gn[0:2 * DT, :], ident[0:2 * DT, 0:2 * DT]).then_inc(set_fill, 1)
            pe.wait_ge(in_x, 32)
            for n in range(6):
                i, q = divmod(n, 2)
                m = TILES[i][1]
                for k in range(4):
                    last = T.transpose(PS[:, n + 2, k * P:k * P + m], xn[0:m, i, (4 * q + k) * P:(4 * q + k + 1) * P], ident[0:m, 0:m])
                last.then_inc(set_fill, 1)

            def sum_squares(k):
                pe.wait_ge(sq_ready, k + 1)
                for m in range(DT):
                    last = mm(PS[:, 0, 0:NTOK], ones, hT[:, m, :], m == 0, m == DT - 1)
                last.then_inc(ssq_done, 1)

            sum_squares(0)
            def modulation(c):
                for k in range(DT):
                    n = DT * c + k
                    await_chunk(pe, n)
                    for q in range(4):
                        last = mm(PS[0:9, 4 - 4 * (c % 2) + q, :], sT[:, k, :], slot4(n)[:, q, :], k == 0, k == DT - 1)
                    last.then_inc(used, 1)

            def turn_modulation(c, bank):
                pe.wait_ge(mod_copy, c + 1)
                for m in range(16):
                    last = T.transpose(PS[:, bank, 9 * m:9 * m + 9], mod_rows[0:9, c % 2, m * P:(m + 1) * P], ident[0:9, 0:9])
                last.then_inc(mod_fill, 1)

            pe.wait_ge(set_copy, 8)
            modulation(0)
            pe.wait_ge(ms_ready, 1)
            modulation(1)
            turn_modulation(0, 4)
            pe.wait_ge(mod_ready, 1)
            modulation(2)
            turn_modulation(1, 0)
            turn_modulation(2, 1)

            def turned(n0, rhs, bank, kts):
                for kh in range(kts // 4):
                    await_chunk(pe, n0 + kh)
                    for m in range(4):
                        for k in range(4):
                            last = mm(PS[:, bank + m, 0:NTOK], slot4(n0 + kh)[:, k, m * P:(m + 1) * P], rhs[:, 4 * kh + k, :],
                                      kh == 0 and k == 0, 4 * kh + k == kts - 1)
                    last.then_inc(used, 1)
                return n0 + kts // 4

            def natural(n0, bank):
                for kh in range(2):
                    await_chunk(pe, n0 + kh)
                    for i, (a, m) in enumerate(TILES):
                        for k in range(4):
                            last = mm(PS[0:m, bank + i, :], hT[:, 4 * kh + k, a:a + m], slot4(n0 + kh)[:, k, :],
                                      kh == 0 and k == 0, kh == 1 and k == 3)
                    last.then_inc(used, 1)
                return n0 + 2

            pe.wait_ge(h_ready, 1)
            n = 3 * DT
            for c in range(6):
                if c >= 2:
                    pe.wait_ge(proj_free, c - 1)
                if c == 1:
                    pe.wait_ge(mod_ready, 3)
                n = (turned if c < 2 else natural)(n, *((hT, proj_bank(c), DT) if c < 2 else (proj_bank(c),)))
            pe.wait_ge(proj_free, 6)
            for q in range(9):
                kind, i = divmod(q, 3)
                a, m = TILES[i]
                if kind:
                    pe.wait_ge(nat_ready, kind)
                if q == 8:
                    pe.wait_ge(tr_free, 1)
                for p in range(PAIRS):
                    if kind == 0:
                        last = T.transpose(PS[0:m, q % 8, p * P:(p + 1) * P], kT[0][:, p, a:a + m], ident)
                    else:
                        last = T.transpose(PS[:, q % 8, p * P:p * P + m], nat[kind - 1][0:m, i, p * P:(p + 1) * P], ident[0:m, 0:m])
                last.then_inc(tr_fill, 1)

            pe.wait_ge(tr_free, 9)

            def prompt_scores(j):
                r, p = divmod(j, 4)
                if j >= 2:
                    pe.wait_ge(pz_free, j - 1)
                for h in range(2):
                    rows = slice(HD * h, HD * h + HD)
                    bank = 2 * (j % 2) + h
                    mm(PS[:, bank, 0:P], qT[r][rows, p, 0:P], kT[r][rows, p, 0:P], True, True)
                    last = mm(PS[:, bank, P:3 * P], qT[r][rows, p, P:2 * P], kT[r][rows, p, 0:2 * P], True, True)
                last.then_inc(pz_fill, 1)

            prompt_scores(0)
            for j in range(8):
                r, p = divmod(j, 4)
                if j + 1 < 8:
                    prompt_scores(j + 1)
                pe.wait_ge(pw_ready, j + 1)
                for h in range(2):
                    for b in range(3):
                        last = T.transpose(PS[:, 4 + h, b * P:(b + 1) * P], pt2[j % 2][:, h, b * P:(b + 1) * P], ident)
                last.then_inc(at_fill, 1)
                pe.wait_ge(at_copy, j + 1)
                if j >= 2:
                    pe.wait_ge(po_copy, j - 1)
                for h in range(2):
                    v = [vn[r][:, i, (2 * p + h) * HD:(2 * p + h + 1) * HD] for i in range(2)]
                    out = PS[HD * h:HD * h + HD, 6 + j % 2, :]
                    mm(out[:, 0:2 * P], v[0], pAT[:, h, 0:2 * P], True, False)
                    last = mm(out[:, P:2 * P], v[1], pAT[:, h, 2 * P:3 * P], False, True)
                last.then_inc(po_fill, 1)

            pe.wait_ge(po_copy, 8)
            pe.wait_ge(pz_free, 8)

            def turn_keys(gi, hh):
                chunk = pages_at["k", gi] + hh
                await_chunk(pe, chunk)
                for pg in range(HALF):
                    tp = 32 * gi + HALF * hh + pg
                    if tp >= 2:
                        pe.wait_ge(kt_act if tp % 2 == 0 else kt_dve, tp // 2)
                    for p in range(PAIRS):
                        last = T.transpose(PS[:, tp % 2, p * P:(p + 1) * P], slot4(chunk)[:, pg, p * P:(p + 1) * P], ident)
                    last.then_inc(kt_fill, 1)

            def row_scores(gi, hh):
                g = gi % 2
                b, hf = divmod(hh, 2)
                for s in (kt_act, kt_dve):
                    pe.wait_ge(s, 2 * (8 * gi + hh + 1))
                for p in range(PAIRS):
                    last = mm(PS[32 * b:32 * b + 32, 2 + hf, :], QP[:, 4 * g + b, p, :], KT[:, hh % 2, p, :], p == 0, p == PAIRS - 1)
                last.then_inc(used, 1)

            def scores(gi):
                r, g = divmod(gi, 2)
                turn_keys(gi, 0)
                if gi >= 2:
                    turn_product(gi - 2)
                pe.wait_ge(qp_ready, r + 1)
                if gi:
                    pe.wait_ge(z_copy, gi)
                for hh in range(8):
                    if hh < 7:
                        turn_keys(gi, hh + 1)
                    row_scores(gi, hh)
                for b in range(4):
                    for p in range(PAIRS):
                        last = mm(PS[32 * b:32 * b + 32, 4, 0:NSM], QP[:, 4 * g + b, p, :], kT[r][:, p, NPR:NTOK], p == 0, p == PAIRS - 1)
                last.then_inc(s_fill, 1)

            def turn_weights(gi):
                pe.wait_ge(aw_ready, gi + 1)
                if gi:
                    pe.wait_ge(oh_copy, gi)
                for pg in range(PAGES):
                    T.transpose(PS[:, 5 + pg // 4, (pg % 4) * P:(pg % 4 + 1) * P], T2[:, pg * P:(pg + 1) * P], ident)
                T.transpose(PS[0:NSM, 7, 0:P], T2[:, PAST:ROWW], ident).then_inc(aw_fill, 1)

            def values(gi):
                pe.wait_ge(aw_copy, gi + 1)
                if gi < 3:
                    pe.wait_ge(z_copy, gi + 2)
                mm(PS[:, 4, :], AT[0:NSM, PAGES, :], vn[gi // 2][0:NSM, 2, :], True, False)
                for hh in range(8):
                    b, hf = divmod(hh, 2)
                    chunk = pages_at["v", gi] + hh
                    await_chunk(pe, chunk)
                    for pg in range(HALF):
                        last = mm(PS[32 * b:32 * b + 32, 4, :], AT[:, HALF * hf + pg, 32 * b:32 * b + 32], slot4(chunk)[:, pg, :],
                                  False, hf == 1 and pg == HALF - 1)
                    last.then_inc(used, 1)

            def turn_product(gi):
                pe.wait_ge(pv_copy, gi + 1)
                for p in range(PAIRS):
                    last = T.transpose(PS[:, 7, p * P:(p + 1) * P], pv_rows[:, p * P:(p + 1) * P], ident)
                last.then_inc(pt_fill, 1)

            scores(0)
            scores(1)
            for gi in range(4):
                turn_weights(gi)
                values(gi)
                if gi + 2 < 4:
                    scores(gi + 2)
                else:
                    turn_product(gi)
            n += 64

            for s in range(4):
                c, r = divmod(s, 2)
                if s:
                    pe.wait_ge(gate_ready, s)
                n = turned(n, hT, 0, DT)
                if s:
                    pe.wait_ge(b_free, s)
                else:
                    pe.wait_ge(oh_copy, 4)
                n = turned(n, oT[r], 4, PAIRS)
            pe.wait_ge(b_free, 4)
            for c in range(2):
                n = turned(n, uT, 4 * c, DT)
            assert n == NSTREAM
            sum_squares(1)
            pe.wait_ge(h_ready, 2)
            for q in range(6):
                i, hf = divmod(q, 2)
                a, m = TILES[i]
                for k in range(4):
                    last = T.transpose(PS[0:m, q, k * P:(k + 1) * P], hT[:, 4 * hf + k, a:a + m], ident)
                last.then_inc(rt_fill, 1)
            for i, (a, m) in enumerate(TILES):
                for k in range(DT):
                    last = mm(PS[0:m, 6, NE * i:NE * i + NE], hT[:, k, a:a + m], wr[:, k, :], k == 0, k == DT - 1)
            last.then_inc(lg_fill, 1)
            for q in range(6):
                i, hf = divmod(q, 2)
                a, m = TILES[i]
                pe.wait_ge(rt_copy, q + 1)
                for k in range(4):
                    last = T.transpose(PS[0:m, q, k * P:(k + 1) * P], xT[:, 4 * hf + k, a:a + m], ident)
                last.then_inc(rt_fill, 1)
            pe.wait_ge(gx_ready, 1)
            for q in range(4):
                i, hf = divmod(q, 2)
                m = P if i == 0 else NSM
                pe.wait_ge(rt_copy, 6 + q + 1)
                for k in range(4):
                    f = 4 * hf + k
                    src = modT[:, 5 * DT + f, 0:1].to_broadcast([P, P]) if i == 0 else gx[:, f, :]
                    last = T.transpose(PS[0:m, q, k * P:(k + 1) * P], src, ident)
                last.then_inc(rt_fill, 1)
            pe.wait_ge(mask_ready, 1)
            for i, (a, m) in enumerate(TILES):
                out = PS[0:m, 7, NE * i:NE * i + NE]
                for k in range(i + 1):
                    mk = TILES[k][1]
                    mm(out, (below if k == i else ones)[0:mk, 0:m], msk[0:mk, k, :], k == 0, k == i)
            for k, (a, m) in enumerate(TILES):
                last = mm(PS[:, 7, NT * NE:(NT + 1) * NE], ones[0:m, :], msk[0:m, k, :], k == 0, k == NT - 1)
            last.then_inc(rank_fill, 1)
            for i, (a, m) in enumerate(TILES):
                last = T.transpose(PS[0:NE, 6, a:a + m], gD[0:m, i, :], ident[0:m, 0:m])
            last.then_inc(gT_fill, 1)
            pe.wait_ge(gT_copy, 1)
            pe.wait_ge(rt_copy, 16)
            pe.wait_ge(in_bd, 16)
            for i, (a, m) in enumerate(TILES):
                for hf in range(2):
                    last = mm(PS[0:m, 2 * i + hf, :], GT[:, a:a + m], bdn[0:NE, 512 * hf:512 * hf + 512], True, True)
            last.then_inc(bd_fill, 1)
            pe.wait_ge(acc_ready, 1)

            def gather(it):
                pe.wait_ge(oh_ready, it + 1)
                for k in range(DT):
                    for i, (a, m) in enumerate(TILES):
                        last = mm(PS[:, 6 + k // 4, (k % 4) * P:(k % 4 + 1) * P], h2n[0:m, i, k * P:(k + 1) * P],
                                  onehot[0:m, i, :], i == 0, i == NT - 1)
                last.then_inc(gathered, 1)

            def gather_info(e):
                for i, (a, m) in enumerate(TILES):
                    last = mm(PS[:, 3, 0:2], onehot[0:m, i, :], val[0:m, i, bass.ds(e, 1), :].rearrange("p a c -> p (a c)"),
                              i == 0, i == NT - 1)
                last.then_inc(info_fill, 1)

            def three(out, xh, xl, wh, wl, start, stop):
                mm(out, xh, wh, start, False)
                mm(out, xh, wl, False, False)
                return mm(out, xl, wh, False, stop)

            def parts(it, q):
                if of_pool(q):
                    pe.wait_ge(low_pool, pool_lows(it, q))
                else:
                    pe.wait_ge(low_dve, dve_lows(it, q))
                return WH[:, q % SPLITS, :], WL[:, q % SPLITS, :]

            def turn_hidden(it, h):
                pe.wait_ge(hb_ready, 2 * it + (h + 1))
                for k in range(4):
                    at = (4 * h + k) * P
                    last = T.transpose(PS[:, h, k * P:(k + 1) * P], hb[:, at:at + P], ident)
                last.then_inc(hg_fill, 1)

            def down(it, j):
                for k in range(2 * j, 2 * j + 2):
                    wh, wl = parts(it, 16 + k)
                    for hf in range(2):
                        cols = slice(512 * hf, 512 * hf + 512)
                        last = three(PS[:, 4 + hf, :], HH[:, k, :], HL[:, k, :], wh[:, cols], wl[:, cols], k == 0, k == DT - 1)
                    last.then_inc(parts_used, 1)

            def expert_pe(tp):
                def body(it, e, more):
                    pe.wait_ge(xl_ready, it + 1)
                    for j, (h, kh, gu) in enumerate(GU):
                        if j == 4:
                            pe.wait_ge(info_ready, it + 1)
                        for k in range(4 * kh, 4 * kh + 4):
                            if k % 2 == 0:
                                wh, wl = (c3(w, 512) for w in parts(it, 2 * j + k % 4 // 2))
                            last = three(PS[:, 2 * h + gu, :], XH[:, k, :], XL[:, k, :], wh[:, k % 2, :], wl[:, k % 2, :],
                                         k == 0, k == DT - 1)
                            if k % 2:
                                last.then_inc(parts_used, 1)
                    turn_hidden(it, 0)
                    if more:
                        gather(it + 1)
                    pe.wait_ge(hl_ready, 2 * it + 1)
                    pe.wait_ge(y_scaled, it + 1)
                    down(it, 0)
                    turn_hidden(it, 1)
                    if more:
                        gather_info(e + 1)
                    down(it, 1)
                    pe.wait_ge(hl_ready, 2 * it + 2)
                    down(it, 2)
                    down(it, 3)

                gather(tp * NE)
                gather_info(0)
                with pe.Fori(0, NE - 1) as e:
                    body(tp * NE + e, e, True)
                body(tp * NE + (NE - 1), NE - 1, False)

            pe.sem_inc(parts_used, SPLITS)
            expert_pe(0)
            most = pe.value_load(cnt_i[0:1, 0:1], min_val=0, max_val=NTOK)
            with pe.Fori(1, NT) as tp:
                with pe.If(most > tp * CAP):
                    expert_pe(tp)
                pe.nop()
            pe.nop()


_INS = ["x_prompt", "x_sample", "c_prompt", "c_sample", "cache_sb_k", "cache_sb_v", "cache_mb_k", "cache_mb_v",
        "page_table", "w_ada", "b_ada", "g_norm1", "g_norm2", "w_in", "q_norm_g", "k_norm_g", "w_br_sb", "w_br_mb",
        "w_out", "w_router", "b_router", "w_gu", "b_gu", "w_down", "b_down"]
_OUTS = [("y_prompt", (1, NPR, D)), ("y_sample", (NSEQ, NNEW, D))]
_OUTS += [(f"{r}_{x}_prompt", (1, 1, NPR, HEADS, HD)) for r in ("sb", "mb") for x in "kv"]
_OUTS += [(f"{r}_{x}_sample", (1, NSEQ, NNEW, HEADS, HD)) for r in ("sb", "mb") for x in "kv"]


def kernel(**inputs):
    import concourse.bacc as _bacc
    from concourse.bass_utils import run_bass_kernel_spmd as _run

    nc = _bacc.Bacc("TRN2", target_bir_lowering=False, num_devices=1)
    arrays, ins, outs = {}, {}, {}
    for name in _INS:
        a = np.ascontiguousarray(inputs[name])
        arrays[f"in_{name}"] = a
        ins[name] = nc.dram_tensor(f"in_{name}", a.shape, mybir.dt.from_np(a.dtype), kind="ExternalInput").ap()
    arrays["constants"] = constants()
    ins["constants"] = nc.dram_tensor("constants", (P, NCONST), F32, kind="ExternalInput").ap()
    for name, shape in _OUTS:
        outs[name] = nc.dram_tensor(f"out_{name}", shape, F32, kind="ExternalOutput").ap()
    build(nc, ins, outs)
    r = _run(nc, [arrays], core_ids=[0])
    return tuple(r.results[0][f"out_{name}"] for name, _ in _OUTS)
```

```python
from contextlib import ExitStack

import concourse.bass as bass
import numpy as np
from concourse import mybir

F32 = mybir.dt.float32
F32R = mybir.dt.float32r
I32 = mybir.dt.int32
U32 = mybir.dt.uint32
ALU = mybir.AluOpType
ACT = mybir.ActivationFunctionType
AX = mybir.AxisListType

P = 128
D = 1024
DT = D // P
HD = 64
HEADS = 8
BW = HEADS * HD
PAIRS = BW // P
NPR = 256
NSEQ, NNEW = 8, 4
NSM = NSEQ * NNEW
NTOK = NPR + NSM
TILES = [(0, P), (P, P), (NPR, NSM)]
NT = len(TILES)
PAST = 1024
PAGES = PAST // P
HALF = PAGES // 2
MOBA = 256
NMB = PAST // MOBA
MTOP = 3
NE, TOPK = 32, 4
FF = 1024
CAP = P
LIMIT, ALPHA = 7.0, 1.702
EPS = 1e-6
SCALE = HD ** -0.5
NMOD = 6
SLOTS = 4
SLOTW = 2048
SPLITW = 1024
SPLITS = 6
POOL_EVERY = 4
OFF = float(1 << 20)
NEG = -1e30

CONST = {}
_at = 0
for _name, _n in (("ident", P), ("ones", P), ("below", P), ("iota", P), ("strict", P), ("causal", P),
                  ("cos", NT * HD // 2), ("sin", NT * HD // 2), ("newsb", 2 * NSM), ("newmb", 2 * NSM),
                  ("row4", NT)):
    CONST[_name] = (_at, _at + _n)
    _at += _n
NCONST = _at


def constants():
    c = np.zeros((P, NCONST), np.float32)

    def put(name, x):
        a, b = CONST[name]
        c[:, a:b] = x

    i = np.arange(P)
    put("ident", np.eye(P))
    put("ones", 1.0)
    put("below", i[:, None] < i[None, :])
    put("iota", i[None, :])
    put("strict", i[None, :] < i[:, None])
    put("causal", np.where(i[None, :] <= i[:, None], 0.0, NEG))
    inv = (np.float32(10000.0) ** (-np.arange(0, HD, 2, dtype=np.float32) / np.float32(HD))).astype(np.float32)
    pos = np.zeros((NT, P), np.float32)
    pos[0], pos[1] = i, P + i
    pos[2, :NSM] = PAST + np.arange(NSM) % NNEW
    ang = (pos[:, :, None] * inv).astype(np.float32)
    put("cos", np.cos(ang).transpose(1, 0, 2).reshape(P, -1))
    put("sin", np.sin(ang).transpose(1, 0, 2).reshape(P, -1))
    b, t = i // (HEADS * NNEW), i % NNEW
    kb, kt = np.arange(NSM) // NNEW, np.arange(NSM) % NNEW
    same = [(b[:, None] + 4 * g) == kb[None, :] for g in range(2)]
    put("newsb", np.concatenate([s & (kt[None, :] < t[:, None]) for s in same], 1))
    put("newmb", np.concatenate([np.where(s & (kt[None, :] <= t[:, None]), 0.0, NEG) for s in same], 1))
    put("row4", TOPK * (i[:, None] + np.array([a for a, _ in TILES])[None, :]) - OFF)
    return c


def build(nc, t, o):
    ctx = ExitStack()
    with ctx:
        def sb(name, shape, dt=F32):
            return ctx.enter_context(nc.sbuf_tensor(name, shape, dt))

        def sem(name):
            return ctx.enter_context(nc.semaphore(name))

        PS = ctx.enter_context(nc.psum_tensor("PS", [P, 8, 512], F32))
        ring = sb("ring", [P, SLOTS, SLOTW])
        WH, WL = sb("WH", [P, SPLITS, SPLITW], F32R), sb("WL", [P, SPLITS, SPLITW], F32R)
        XH, XL = sb("XH", [P, DT, P], F32R), sb("XL", [P, DT, P], F32R)
        HH, HL = sb("HH", [P, DT, P], F32R), sb("HL", [P, DT, P], F32R)
        xT = sb("xT", [P, DT, NTOK])
        hT = sb("hT", [P, DT, NTOK])
        modT = sb("modT", [P, NMOD * DT, 1 + NSEQ])
        gs = sb("gs", [P, 2, DT, 1 + NSEQ])
        cst = sb("cst", [P, NCONST])
        small = sb("small", [P, 1600])
        ptab = sb("ptab", [1, NSEQ * PAGES], I32)
        cnt_i = sb("cnt_i", [1, 1], I32)
        idx_cur = sb("idx_cur", [P, 1], U32)
        i8 = sb("i8", [P, NT, 8], U32)
        arena = sb("arena", [P, 19600])

        cursor = [0]

        def carve(width, start=None):
            if start is not None:
                cursor[0] = start
            a = cursor[0]
            cursor[0] += width
            assert cursor[0] <= 19600, cursor[0]
            return arena[:, a:a + width]

        def c3(ap, b):
            return ap.rearrange("p (a b) -> p a b", b=b)

        qT = [c3(carve(PAIRS * NTOK, 0 if r == 0 else None), NTOK) for r in range(2)]
        kT = [c3(carve(PAIRS * NTOK), NTOK) for _ in range(2)]
        vn_at = cursor[0]
        vn = [c3(carve(NT * BW), BW) for _ in range(2)]
        oT = [c3(carve(PAIRS * NTOK), NTOK) for _ in range(2)]
        QP = carve(NSEQ * PAIRS * 32).rearrange("p (b a c) -> p b a c", a=PAIRS, c=32)
        KT_at = cursor[0]
        KT = carve(2 * PAIRS * 512).rearrange("p (s a c) -> p s a c", a=PAIRS, c=512)
        ROWW = PAST + NSM
        Z, T1, T2 = carve(ROWW), carve(ROWW), carve(ROWW)
        AT = c3(carve((PAGES + 1) * P), P)
        pv_rows = AT[:, 0:PAIRS, :].rearrange("p a b -> p (a b)")
        W_end = cursor[0]
        mod_rows = c3(carve(2 * SLOTW, vn_at), SLOTW)
        cursor[0] = W_end
        xn = c3(carve(NT * D, KT_at), D)
        nat = [c3(carve(NT * BW, KT_at), BW), c3(carve(NT * BW), BW)]
        natks = c3(carve(NT * BW), BW)
        PW = 2 * 3 * P
        carve(0, KT_at)
        pt1 = [carve(PW).rearrange("p (h c) -> p h c", h=2), carve(PW).rearrange("p (h c) -> p h c", h=2)]
        pt2 = [carve(PW).rearrange("p (h c) -> p h c", h=2), carve(PW).rearrange("p (h c) -> p h c", h=2)]
        pAT = carve(PW).rearrange("p (h c) -> p h c", h=2)
        assert cursor[0] <= KT_at + 2 * PAIRS * 512
        uT = c3(carve(DT * NTOK, KT_at), NTOK)
        sg = c3(carve(4 * NTOK), NTOK)
        h2n = c3(carve(NT * D, 0), D)
        acc = c3(carve(NT * D), D)
        ga2n = c3(carve(2 * D), D)
        last_at = cursor[0]
        bb = carve(2 * FF)
        g1, u1, e1 = carve(512), carve(512), carve(512)
        hb = carve(FF)
        last_rows = carve(TOPK * D, last_at)
        yb = carve(D)
        bdn = carve(D)
        onehot = c3(carve(NT * P), P)
        choice = bb[:, 0:NT * TOPK * NE].rearrange("p (a q e) -> p a q e", a=NT, q=TOPK)
        weighed = bb[:, NT * TOPK * NE:2 * NT * TOPK * NE].rearrange("p (a q e) -> p a q e", a=NT, q=TOPK)
        bgrow = carve(2 * FF)
        gx = c3(carve(DT * NSM), NSM)
        MOE_END = cursor[0]

        scur = [0]

        def tiny(n, w=None):
            a = scur[0]
            scur[0] += n
            assert scur[0] <= 1600
            ap = small[:, a:a + n]
            return ap if w is None else c3(ap, w)

        badaT = tiny(NMOD * DT)
        gT = tiny(2 * DT)
        sT = tiny(DT * 9, 9)
        rst = tiny(NTOK)
        qkg = tiny(2 * HD, HD)
        ssh_at = scur[0]
        ssh = tiny(NT * HEADS * 2).rearrange("p (r a b) -> p r a b", r=2, b=HEADS)
        mx = [tiny(4, 2), tiny(4, 2)]
        ls = [tiny(4, 2), tiny(4, 2)]
        gt8, m8d, f8d, sel8 = tiny(8), tiny(8), tiny(8), tiny(8)
        dmx, dls = tiny(1), tiny(1)
        LG = tiny(NT * NE, NE)
        m8 = tiny(NT * 8, 8)
        f8 = tiny(NT * 8, 8)
        gt4 = tiny(NT * TOPK, TOPK)
        gls = tiny(NT)
        ngm = tiny(NT)
        msk = tiny(NT * NE, NE)
        gD = tiny(NT * NE, NE)
        pos = tiny(NT * (NE + 1), NE + 1)
        val = tiny(NT * (NE + 1) * 2).rearrange("p (a e c) -> p a e c", a=NT, c=2)
        cnt = tiny(1)
        infos = tiny((NE + 1) * 2, 2)
        gcur = tiny(1)
        brt = tiny(NE)
        wr = sb("wr", [P, DT, NE])
        GT = sb("GT", [NE, NTOK])
        cn = carve(D, 15700)
        ce = carve(D)
        ban = carve(P)
        gn = carve(P)

        def K(name, rows=P):
            a, b = CONST[name]
            return cst[0:rows, a:b]

        ident, ones, below, iota = K("ident"), K("ones"), K("below"), K("iota")
        strict, causal = K("strict"), K("causal")
        cosv, sinv = c3(K("cos"), HD // 2), c3(K("sin"), HD // 2)
        newsb, newmb = c3(K("newsb"), NSM), c3(K("newmb"), NSM)
        row4 = K("row4")

        Y4 = nc.dram_tensor("choice_rows", (NTOK * TOPK, D), F32, kind="Internal").ap()

        in_const, in_c, in_x, in_misc, in_pt = sem("in_const"), sem("in_c"), sem("in_x"), sem("in_misc"), sem("in_pt")
        landed = [sem(f"landed{s}") for s in range(SLOTS)]
        paged = [sem(f"paged{s}") for s in range(SLOTS)]
        used = sem("used")
        c_sig, c_silu = sem("c_sig"), sem("c_silu")
        set_fill, set_copy = sem("set_fill"), sem("set_copy")
        sq_ready, ssq_done, ms_ready, rstd_ready = sem("sq_ready"), sem("ssq_done"), sem("ms_ready"), sem("rstd_ready")
        h_ready = sem("h_ready")
        proj_free = sem("proj_free")
        nat_ready = sem("nat_ready")
        nat_ms, nat_rs = sem("nat_ms"), sem("nat_rs")
        tr_fill, tr_free = sem("tr_fill"), sem("tr_free")
        qp_zero, qp_ready = sem("qp_zero"), sem("qp_ready")
        out_rows, out_keys = sem("out_rows"), sem("out_keys")
        pz_fill, pz_free, pl_ready, pd_ready, pe_ready, pw_ready = (
            sem("pz_fill"), sem("pz_free"), sem("pl_ready"), sem("pd_ready"), sem("pe_ready"), sem("pw_ready"))
        at_fill, at_copy, po_fill, po_copy = sem("at_fill"), sem("at_copy"), sem("po_fill"), sem("po_copy")
        kt_fill, kt_act, kt_dve = sem("kt_fill"), sem("kt_act"), sem("kt_dve")
        s_fill, z_copy, dl_ready, dd_ready, de_ready, aw_ready = (
            sem("s_fill"), sem("z_copy"), sem("dl_ready"), sem("dd_ready"), sem("de_ready"), sem("aw_ready"))
        aw_fill, aw_copy, pv_copy = sem("aw_fill"), sem("aw_copy"), sem("pv_copy")
        pt_fill, oh_copy = sem("pt_fill"), sem("oh_copy")
        mod_copy, mod_fill, mod_ready = sem("mod_copy"), sem("mod_fill"), sem("mod_ready")
        gate_ready, b_free = sem("gate_ready"), sem("b_free")
        x1_ready = sem("x1_ready")
        gx_ready = sem("gx_ready")
        rt_fill, rt_copy = sem("rt_fill"), sem("rt_copy")
        lg_fill, mask_ready, rank_fill, rank_read, gl_ready, ge_ready = (
            sem("lg_fill"), sem("mask_ready"), sem("rank_fill"), sem("rank_read"), sem("gl_ready"), sem("ge_ready"))
        bd_fill, val_ready = sem("bd_fill"), sem("val_ready")
        oh_ready, gathered, info_fill, info_ready = sem("oh_ready"), sem("gathered"), sem("info_fill"), sem("info_ready")
        high_ready, low_dve, low_pool, parts_used = sem("high_ready"), sem("low_dve"), sem("low_pool"), sem("parts_used")
        xh_ready, xl_ready, hh_ready, hl_ready = sem("xh_ready"), sem("xl_ready"), sem("hh_ready"), sem("hl_ready")
        g1_ready, e_ready, hb_ready = sem("g1_ready"), sem("e_ready"), sem("hb_ready")
        hg_fill, y_scaled = sem("hg_fill"), sem("y_scaled")
        cur_ready, scattered, rows_out = sem("cur_ready"), sem("scattered"), sem("rows_out")
        brow_in, bb_ready, bb_used = sem("brow_in"), sem("bb_ready"), sem("bb_used")
        back_in, y_ready, y_out, in_bd = sem("back_in"), sem("y_ready"), sem("y_out"), sem("in_bd")
        back = [sem(f"back{i}") for i in range(NT)]
        dve_done, act_done, pool_done = sem("dve_done"), sem("act_done"), sem("pool_done")
        dve_loop, pool_step, sp_step = sem("dve_loop"), sem("pool_step"), sem("sp_step")

        cache_k = [t["cache_sb_k"], t["cache_mb_k"]]
        cache_v = [t["cache_sb_v"], t["cache_mb_v"]]
        w_ada = t["w_ada"][0].rearrange("(k p) n -> p k n", p=P)
        w_in = t["w_in"][0].rearrange("(k p) n -> p k n", p=P)
        w_out = t["w_out"][0].rearrange("(k p) n -> p k n", p=P)
        w_br = [t["w_br_sb"][0].rearrange("(k p) n -> p k n", p=P), t["w_br_mb"][0].rearrange("(k p) n -> p k n", p=P)]
        stream = []
        for c in range(3):
            for k in range(DT):
                stream.append(("w", w_ada[:, k, c * SLOTW:(c + 1) * SLOTW]))

        def add_cols(w, col):
            for kh in range(w.shape[1] // 4):
                stream.append(("w4", w[:, 4 * kh:4 * kh + 4, col:col + 512]))

        Q_SB, K_SB, V_SB, Q_MB, K_MB, V_MB = range(6)
        PROJ = [Q_MB, K_MB, Q_SB, K_SB, V_SB, V_MB]
        for c in PROJ:
            add_cols(w_in, BW * c)
        pages_at = {}
        for kind, gi in (("k", 0), ("k", 1), ("v", 0), ("k", 2), ("v", 1), ("k", 3), ("v", 2), ("v", 3)):
            r, g = divmod(gi, 2)
            pages_at[kind, gi] = len(stream)
            for b in range(4 * g, 4 * g + 4):
                for hf in range(2):
                    stream.append(("pages", (cache_k if kind == "k" else cache_v)[r], b * PAGES + hf * HALF))
        for c in range(2):
            for r in range(2):
                add_cols(w_in, 6 * BW + r * D + 512 * c)
                add_cols(w_br[r], 512 * c)
        for c in range(2):
            add_cols(w_out, 512 * c)
        NSTREAM = len(stream)
        lands, total, paged_total = [], [0] * SLOTS, [0] * SLOTS
        for n, item in enumerate(stream):
            total[n % SLOTS] += 16 * (HALF // 2 if item[0] == "pages" else 1)
            paged_total[n % SLOTS] += 16 * (HALF // 2 if item[0] == "pages" else 0)
            lands.append((total[n % SLOTS], paged_total[n % SLOTS] if item[0] == "pages" else 0))

        def slot(n):
            return ring[:, n % SLOTS, :]

        def slot4(n):
            return c3(ring[:, n % SLOTS, :], 512)

        def await_chunk(eng, n):
            eng.wait_ge(landed[n % SLOTS], lands[n][0])
            if lands[n][1]:
                eng.wait_ge(paged[n % SLOTS], lands[n][1])

        MOD_END = [DT * (c + 1) for c in range(3)]
        PROJ_END = [MOD_END[-1] + 2 * (c + 1) for c in range(6)]
        att = PROJ_END[-1] + 64
        GATE_END = [att + 3 * s + 2 for s in range(4)]
        BRANCH_END = [att + 3 * s + 3 for s in range(4)]
        OUT_END = [att + 12 + 2 * (c + 1) for c in range(2)]
        assert OUT_END[-1] == NSTREAM
        EXP_CHUNKS = 12
        PARTS = EXP_CHUNKS * SLOTW // SPLITW
        assert NSTREAM % SLOTS == 0 and EXP_CHUNKS % SLOTS == 0 and PARTS % SPLITS == 0 and PARTS % POOL_EVERY == 0

        def of_pool(q):
            return q % POOL_EVERY == POOL_EVERY - 1

        def pool_lows(it, q):
            return it * (PARTS // POOL_EVERY) + ((q + 1) // POOL_EVERY)

        def dve_lows(it, q):
            return it * (PARTS - PARTS // POOL_EVERY) + (q + 1 - (q + 1) // POOL_EVERY)

        def raw_part(q):
            at = q % 2 * SPLITW
            return slot(q // 2)[:, at:at + SPLITW]
        w_gu = t["w_gu"][0].rearrange("e (k p) (j n) -> e p k j n", p=P, j=4)
        w_dn = t["w_down"][0].rearrange("e (k p) n -> e p k n", p=P)

        GU = [(h, kh, j) for h in range(2) for kh in range(2) for j in range(2)]

        banks = [0, 1, 2, 3, 6, 7]
        TURNS = [(0, "gates", 0, 0, NE)]
        TURNS += [(banks[(n + 1) % 6], "x1", n // 2, n % 2, TILES[n // 2][1]) for n in range(6)]
        TURNS += [(banks[(n + 7) % 6], "gate", n // 2, n % 2, (P, NSM)[n // 2]) for n in range(4)]
        BIAS_BANKS = [4, 6, 0]

        def proj_bank(c):
            return 4 - 4 * (c % 2)

        block = ctx.enter_context(nc.Block())

        @block.sync
        def _(sp):
            for n, item in enumerate(stream):
                if item[0] == "pages":
                    _, cache, at = item
                    if stream[n - 1][0] != "pages":
                        sp.wait_ge(in_pt, 16)
                    pages = [sp.value_load(ptab[0:1, at + j:at + j + 1], min_val=0, max_val=cache.shape[1] - 1)
                             for j in range(HALF // 2)]
                if n >= SLOTS:
                    sp.wait_ge(used, n - SLOTS + 1)
                if item[0] == "w":
                    sp.dma_start(slot(n), item[1]).then_inc(landed[n % SLOTS], 16)
                elif item[0] == "w4":
                    sp.dma_start(slot4(n), item[1]).then_inc(landed[n % SLOTS], 16)
                else:
                    for j, page in enumerate(pages):
                        src = cache[0, bass.ds(page, 1)].rearrange("a p h d -> (a p) (h d)")
                        sp.dma_start(slot4(n)[:, j, :], src).then_inc(landed[n % SLOTS], 16)

            def load_expert_chunk(tp, it, e, j):
                if not isinstance(it, int) or it or j >= SLOTS:
                    before = 2 * (j - SLOTS) + 1
                    sp.wait_ge(low_dve, dve_lows(it, before))
                    sp.sem_inc(sp_step, 1)
                    if not isinstance(it, int) or it or before >= POOL_EVERY - 1:
                        sp.wait_ge(low_pool, pool_lows(it, before))
                else:
                    sp.wait_ge(used, NSTREAM - SLOTS + j + 1)
                one = bass.ds(e, 1)
                if j < 8:
                    h, kh, gu = GU[j]
                    src = w_gu[one, :, 4 * kh:4 * kh + 4, 2 * gu + h, :].rearrange("a p k n -> (a p) k n")
                    sp.dma_start(slot4(j), src).then_inc(landed[j % SLOTS], 16)
                else:
                    src = w_dn[one, :, 2 * (j - 8):2 * (j - 8) + 2, :].rearrange("a p k n -> (a p) k n")
                    sp.dma_start(c3(slot(j), D), src).then_inc(landed[j % SLOTS], 16)

            def load_bias(it, e):
                if not isinstance(it, int) or it:
                    sp.wait_ge(bb_ready, it)
                sp.dma_start(bgrow[0:1, :], t["b_gu"][0, bass.ds(e, 1), :]).then_inc(brow_in, 16)

            def expert_loads(tp):
                load_bias(tp * NE, 0)
                for j in range(SLOTS):
                    load_expert_chunk(tp, tp * NE, 0, j)
                with sp.Fori(0, NE - 1) as e:
                    it = tp * NE + e
                    for j in range(SLOTS, EXP_CHUNKS):
                        load_expert_chunk(tp, it, e, j)
                    load_bias(it + 1, e + 1)
                    for j in range(SLOTS):
                        load_expert_chunk(tp, it + 1, e + 1, j)
                for j in range(SLOTS, EXP_CHUNKS):
                    load_expert_chunk(tp, tp * NE + (NE - 1), NE - 1, j)

            expert_loads(0)
            sp.wait_ge(rank_read, 2)
            most = sp.value_load(cnt_i[0:1, 0:1], min_val=0, max_val=NTOK)
            with sp.Fori(1, NT) as tp:
                with sp.If(most > tp * CAP):
                    expert_loads(tp)
                sp.nop()
            sp.nop()
            for i, (a, n) in enumerate(TILES):
                if i == 0:
                    sp.wait_ge(back_in, 1)
                dst = ring[0:n, 2 * i:2 * i + 2, :].rearrange("p s c -> p (s c)") if i < 2 else last_rows[0:n, :]
                sp.dma_start(dst, Y4[TOPK * a:TOPK * (a + n), :].rearrange("(p k) n -> p (k n)", k=TOPK)
                             ).then_inc(back[i], 16)
            y_dst = [o["y_prompt"][0, 0:P, :], o["y_prompt"][0, P:NPR, :], o["y_sample"].rearrange("b t n -> (b t) n")]
            for i, (a, n) in enumerate(TILES):
                sp.wait_ge(y_ready, i + 1)
                sp.dma_start(y_dst[i], acc[0:n, i, :]).then_inc(y_out, 16)
            sp.wait_ge(y_out, 16 * NT)

        @block.gpsimd
        def _(pool):
            done = [0]

            def chain(ins):
                done[0] += 1
                ins.then_inc(pool_done, 1)
                pool.wait_ge(pool_done, done[0])

            pool.dma_start(ptab[:, :], t["page_table"].rearrange("b n -> (b n)").rearrange("(a n) -> a n", a=1)).then_inc(in_pt, 16)
            pool.dma_start(qkg[:, 0, :], t["q_norm_g"].to_broadcast([P, HD])).then_inc(in_misc, 16)
            pool.dma_start(qkg[:, 1, :], t["k_norm_g"].to_broadcast([P, HD])).then_inc(in_misc, 16)
            pool.dma_start(brt, t["b_router"].to_broadcast([P, NE])).then_inc(in_misc, 16)
            pool.dma_start(wr[:, :, :], t["w_router"][0].rearrange("(k p) e -> p k e", p=P)).then_inc(in_misc, 16)
            pool.memset(QP, 0.0).then_inc(qp_zero, 1)

            def load_pages(a, b):
                for n in range(a, b):
                    _, cache, at = stream[n]
                    pages = [pool.value_load(ptab[0:1, at + j:at + j + 1], min_val=0, max_val=cache.shape[1] - 1)
                             for j in range(HALF // 2, HALF)]
                    pool.wait_ge(used, n - SLOTS + 1)
                    for j, page in enumerate(pages):
                        src = cache[0, bass.ds(page, 1)].rearrange("a p h d -> (a p) (h d)")
                        pool.dma_start(slot4(n)[:, HALF // 2 + j, :], src).then_inc(paged[n % SLOTS], 16)

            outs = [(o["sb_v_prompt"], o["sb_v_sample"], vn[0], proj_free, PROJ.index(V_SB) + 1),
                    (o["mb_v_prompt"], o["mb_v_sample"], vn[1], proj_free, PROJ.index(V_MB) + 1),
                    (o["mb_k_prompt"], o["mb_k_sample"], nat[1], nat_ready, 2),
                    (o["sb_k_prompt"], o["sb_k_sample"], natks, tr_free, 3)]
            for dp, ds_, src, s, v in outs:
                pool.wait_ge(s, v)
                done = out_keys if src is nat[1] else out_rows
                pool.dma_start(dp[0, 0].rearrange("(a p) h d -> p a (h d)", p=P), src[:, 0:2, :]).then_inc(done, 16)
                pool.dma_start(ds_[0].rearrange("b t h d -> (b t) (h d)"), src[0:NSM, 2, :]).then_inc(done, 16)

            def pad_queries(r):
                for p in range(PAIRS):
                    for s in range(2):
                        rows = slice(HD * s, HD * s + HD)
                        ins = pool.tensor_copy(
                            QP[rows, :, p, (2 * p + s) * NNEW:(2 * p + s + 1) * NNEW],
                            qT[r][rows, p, NPR:NTOK].rearrange("p (b t) -> p b t", t=NNEW))
                ins.then_inc(qp_ready, 1)

            pool.wait_ge(in_pt, 16)
            pool.wait_ge(qp_zero, 1)
            pool.wait_ge(tr_free, 9)
            pad_queries(0)
            load_pages(pages_at["k", 0], pages_at["k", 2])
            pool.wait_ge(s_fill, 2)
            pool.wait_ge(qp_ready, 1)
            pad_queries(1)
            load_pages(pages_at["k", 2], pages_at["v", 3] + 8)
            pool.wait_ge(x1_ready, 2)
            pool.dma_start(bdn[0:NE, :], t["b_down"][0]).then_inc(in_bd, 16)

            def low_part(it, q):
                pool.wait_ge(high_ready, it * PARTS + (q + 1))
                pool.sem_inc(pool_step, 1)
                pool.tensor_tensor(WL[:, q % SPLITS, :], raw_part(q), WH[:, q % SPLITS, :].bitcast(F32),
                                   ALU.subtract).then_inc(low_pool, 1)

            def biases(it):
                pool.wait_ge(bb_used, it + 1)
                pool.wait_ge(brow_in, (it + 1) * 16)
                pool.sem_inc(pool_step, 1)
                pool.partition_broadcast(bb, bgrow[0:1, :], P).then_inc(bb_ready, 1)

            def expert_pool(tp):
                def body(it, more):
                    for q in (11, 15, 19):
                        low_part(it, q)
                    if more:
                        biases(it + 1)
                    low_part(it, 23)
                    if more:
                        low_part(it + 1, 3)
                    pool.wait_ge(y_scaled, it + 2)
                    pool.sem_inc(pool_step, 1)
                    pool.indirect_dma_start(
                        Y4, bass.IndirectOffsetOnAxis(ap=idx_cur[:, 0:1], axis=0), yb, None,
                        bounds_check=NTOK * TOPK - 1, oob_is_err=False).then_inc(scattered, 16)
                    if more:
                        low_part(it + 1, 7)
                    pool.wait_ge(scattered, (it + 1) * 16)
                    pool.sem_inc(rows_out, 1)

                biases(tp * NE)
                for q in (3, 7):
                    low_part(tp * NE, q)
                with pool.Fori(0, NE - 1) as e:
                    body(tp * NE + e, True)
                body(tp * NE + (NE - 1), False)

            pool.sem_inc(rows_out, 1)
            expert_pool(0)
            pool.wait_ge(rank_read, 2)
            most = pool.value_load(cnt_i[0:1, 0:1], min_val=0, max_val=NTOK)
            with pool.Fori(1, NT) as tp:
                with pool.If(most > tp * CAP):
                    expert_pool(tp)
                pool.nop()
            pool.nop()
            pool.sem_inc(back_in, 1)
            pool.wait_ge(out_rows, 16 * 6)
            pool.wait_ge(out_keys, 16 * 2)

        @block.scalar
        def _(act):
            done = [0]

            def chain(ins):
                done[0] += 1
                ins.then_inc(act_done, 1)
                act.wait_ge(act_done, done[0])

            act.dma_start(cn[0:1, :], t["c_prompt"]).then_inc(in_c, 16)
            act.dma_start(cn[1:1 + NSEQ, :], t["c_sample"]).then_inc(in_c, 16)
            act.dma_start(cst[:, :], t["constants"]).then_inc(in_const, 16)
            act.dma_start(ban[0:NMOD * DT, :], t["b_ada"].rearrange("a (m p) -> (a m) p", p=P)).then_inc(in_c, 16)
            act.dma_start(gn[0:DT, :], t["g_norm1"].rearrange("a (m p) -> (a m) p", p=P)).then_inc(in_c, 16)
            act.dma_start(gn[DT:2 * DT, :], t["g_norm2"].rearrange("a (m p) -> (a m) p", p=P)).then_inc(in_c, 16)
            act.dma_start(xn[:, 0:2, :], t["x_prompt"][0].rearrange("(a p) n -> p a n", p=P)).then_inc(in_x, 16)
            act.dma_start(xn[0:NSM, 2, :], t["x_sample"].rearrange("b t n -> (b t) n")).then_inc(in_x, 16)
            act.wait_ge(in_c, 16 * 5)
            act.activation(ce[0:9, :], cn[0:9, :], ACT.Sigmoid).then_inc(c_sig, 1)
            act.wait_ge(set_copy, 8)
            act.activation(hT[:, :, :], xT[:, :, :], ACT.Square).then_inc(sq_ready, 1)


            def rstd(k):
                act.wait_ge(ms_ready, k + 1)
                act.activation(rst, rst, ACT.Sqrt).then_inc(rstd_ready, 1)

            rstd(0)
            for c in range(3):
                act.wait_ge(used, MOD_END[c])
                if c == 2:
                    act.wait_ge(mod_fill, 1)
                bank = 4 - 4 * (c % 2)
                act.activation(c3(mod_rows[0:9, c % 2, :], 512), PS[0:9, bank:bank + 4, :], ACT.Copy).then_inc(mod_copy, 1)

            def head_rstd(r):
                act.wait_ge(nat_ms, r + 1)
                v = ssh[:, r, :, :]
                act.activation(v, v, ACT.Sqrt).then_inc(nat_rs, 1)

            for at, c in enumerate(PROJ):
                act.wait_ge(used, PROJ_END[at])
                bank = proj_bank(at)
                if c in (Q_SB, K_SB):
                    dst = (qT if c == Q_SB else kT)[0]
                    last = act.activation(dst, PS[:, bank:bank + 4, 0:NTOK], ACT.Copy, scale=SCALE if c == Q_SB else 1.0)
                else:
                    dst = {V_SB: vn[0], Q_MB: nat[0], K_MB: nat[1], V_MB: vn[1]}[c]
                    act.activation(dst[:, 0:2, :], PS[:, bank:bank + 2, :], ACT.Copy)
                    last = act.activation(dst[0:NSM, 2, :], PS[0:NSM, bank + 2, :], ACT.Copy)
                last.then_inc(proj_free, 1)
                if at in (2, 3):
                    head_rstd(at - 2)
            for n in range(9):
                kind, i = divmod(n, 3)
                a, m = TILES[i]
                act.wait_ge(tr_fill, n + 1)
                if kind == 0:
                    last = act.activation(natks[0:m, i, :], PS[0:m, n % 8, :], ACT.Copy)
                else:
                    src = c3(PS[:, n % 8, :], P)[:, :, 0:m]
                    last = act.activation((qT if kind == 1 else kT)[1][:, :, a:a + m], src, ACT.Copy,
                                          scale=SCALE if kind == 1 else 1.0)
                last.then_inc(tr_free, 1)

            def zview(j):
                return PS[:, 2 * (j % 2):2 * (j % 2) + 2, 0:3 * P]

            def softplus(src, tmp, out_sem):
                chain(act.activation(tmp, src, ACT.Abs))
                chain(act.activation(tmp, tmp, ACT.Exp, scale=-1.0))
                act.activation(tmp, tmp, ACT.Ln, bias=1.0).then_inc(out_sem, 1)

            act.preload_act_table_set("natural_log_exp_and_others")
            act.wait_ge(out_keys, 16 * 2)

            def front(j):
                act.wait_ge(pz_fill, j + 1)
                softplus(zview(j), pt1[j % 2], pl_ready)

            def exponentials_of(j):
                act.wait_ge(pd_ready, j + 1)
                if j < 4:
                    act.activation(pt2[j % 2], pt1[j % 2], ACT.Exp).then_inc(pe_ready, 1)
                else:
                    for h in range(2):
                        act.activation(pt2[j % 2][:, h, 0:P], pt1[j % 2][:, h, 0:P], ACT.Exp,
                                       bias=mx[j % 2][:, h, 0:1], accum_out=ls[j % 2][:, h, 0:1])
                        last = act.activation(pt2[j % 2][:, h, P:3 * P], pt1[j % 2][:, h, P:3 * P], ACT.Exp,
                                              bias=mx[j % 2][:, h, 1:2], accum_out=ls[j % 2][:, h, 1:2])
                    last.then_inc(pe_ready, 1)

            def copies_of(j):
                act.wait_ge(at_fill, j + 1)
                act.activation(pAT, PS[:, 5:7, 0:3 * P], ACT.Copy).then_inc(at_copy, 1)
                act.wait_ge(po_fill, j + 1)
                act.activation(oT[j // 4][:, j % 4, 0:NPR], PS[:, 7, 0:NPR], ACT.Copy).then_inc(po_copy, 1)

            def evacuate_keys(gi, a, b):
                for tp in range(32 * gi + HALF * a, 32 * gi + HALF * b, 2):
                    act.wait_ge(kt_fill, tp + 1)
                    act.activation(KT[:, (tp // HALF) % 2, :, (tp % HALF) * P:(tp % HALF + 1) * P],
                                   c3(PS[:, 0, :], P), ACT.Copy).then_inc(kt_act, 1)

            def copy_scores(gi):
                act.wait_ge(s_fill, gi + 1)
                if gi:
                    act.wait_ge(aw_ready, gi)
                act.activation(c3(Z[:, 0:PAST], 512), PS[:, 2:4, :], ACT.Copy)
                chain(act.activation(Z[:, PAST:ROWW], PS[:, 4, 0:NSM], ACT.Copy))
                act.sem_inc(z_copy, 1)

            def exponentials(gi):
                act.wait_ge(dd_ready, gi + 1)
                if gi < 2:
                    act.activation(T2, T1, ACT.Exp).then_inc(de_ready, 1)
                else:
                    act.activation(T2, T1, ACT.Exp, bias=dmx, accum_out=dls).then_inc(de_ready, 1)

            def copy_weights(gi):
                act.wait_ge(aw_fill, gi + 1)
                if gi:
                    act.wait_ge(pt_fill, gi)
                act.activation(c3(AT[:, 0:PAGES, :].rearrange("p a b -> p (a b)"), 512), PS[:, 5:7, :], ACT.Copy)
                act.activation(AT[0:NSM, PAGES, :], PS[0:NSM, 7, 0:P], ACT.Copy).then_inc(aw_copy, 1)

            def copy_product(gi):
                act.wait_ge(used, pages_at["v", gi] + 8)
                act.activation(pv_rows, PS[:, 4, :], ACT.Copy).then_inc(pv_copy, 1)

            def copy_heads(gi):
                r, g = divmod(gi, 2)
                act.wait_ge(pt_fill, gi + 1)
                for s in range(2):
                    rows = slice(HD * s, HD * s + HD)
                    for p in range(PAIRS):
                        src = c3(PS[rows, 7, p * P:(p + 1) * P], 32)[:, :, (2 * p + s) * NNEW:(2 * p + s + 1) * NNEW]
                        at = NPR + 4 * g * NNEW
                        last = act.activation(oT[r][rows, p, at:at + 4 * NNEW].rearrange("p (b t) -> p b t", t=NNEW), src, ACT.Copy)
                last.then_inc(oh_copy, 1)

            evacuate_keys(0, 0, 8)
            act.wait_ge(out_rows, 16 * 6)
            copy_scores(0)
            softplus(Z, T1, dl_ready)
            evacuate_keys(1, 0, 2)
            exponentials(0)
            evacuate_keys(1, 2, 8)
            copy_scores(1)
            for gi in range(4):
                copy_weights(gi)
                pair = (2 * gi, 2 * gi + 1)
                if gi < 2:
                    for j in pair:
                        front(j)
                for j in pair:
                    exponentials_of(j)
                for j in pair:
                    copies_of(j)
                if gi + 1 < 4:
                    if gi + 1 < 2:
                        softplus(Z, T1, dl_ready)
                    exponentials(gi + 1)
                copy_product(gi)
                if gi + 2 < 4:
                    evacuate_keys(gi + 2, 0, 1)
                copy_heads(gi)
                if gi + 2 < 4:
                    evacuate_keys(gi + 2, 1, 8)
                    copy_scores(gi + 2)

            def high_part(it, q):
                if q % 2 == 0:
                    j = q // 2
                    act.wait_ge(landed[j % SLOTS], (it * (EXP_CHUNKS // SLOTS) + (j // SLOTS + 1)) * 16 + total[j % SLOTS])
                act.wait_ge(parts_used, it * PARTS + (q + 1))
                act.activation(WH[:, q % SPLITS, :], raw_part(q), ACT.Copy).then_inc(high_ready, 1)

            for s in range(4):
                act.wait_ge(used, GATE_END[s])
                if s:
                    act.wait_ge(b_free, s)
                act.activation(sg, PS[:, 0:4, 0:NTOK], ACT.Sigmoid).then_inc(gate_ready, 1)
            for c in range(2):
                half = slice(4 * c, 4 * c + 4)
                act.wait_ge(x1_ready, c + 1)
                act.activation(hT[:, half, :], xT[:, half, :], ACT.Square).then_inc(sq_ready, 1)
            for q in range(SPLITS):
                high_part(0, q)
            rstd(1)
            def softmax_exp():
                act.wait_ge(gl_ready, 1)
                for i in range(NT):
                    last = act.activation(gt4[:, i, :], m8[:, i, 0:TOPK], ACT.Exp, bias=ngm[:, i:i + 1], accum_out=gls[:, i:i + 1])
                last.then_inc(ge_ready, 1)

            for n in range(6):
                i, q = divmod(n, 2)
                m = TILES[i][1]
                act.wait_ge(rt_fill, n + 1)
                act.activation(h2n[0:m, i, 512 * q:512 * q + 512], PS[0:m, n, :], ACT.Copy).then_inc(rt_copy, 1)
            softmax_exp()

            def high_rows(it):
                act.wait_ge(gathered, it + 1)
                act.activation(XH.rearrange("p (b c) k -> p b (c k)", b=2), PS[:, 6:8, :], ACT.Copy).then_inc(xh_ready, 1)

            def high_hidden(it, h):
                act.wait_ge(hg_fill, 2 * it + (h + 1))
                act.activation(HH[:, 4 * h:4 * h + 4, :], c3(PS[:, h, :], P), ACT.Copy).then_inc(hh_ready, 1)

            def sigmoid(it, h):
                act.wait_ge(g1_ready, 2 * it + (h + 1))
                act.activation(e1, g1, ACT.Sigmoid, scale=ALPHA).then_inc(e_ready, 1)

            def expert_act(tp):
                def body(it, more):
                    sigmoid(it, 0)
                    for q in range(15, 21):
                        high_part(it, q)
                    high_hidden(it, 0)
                    sigmoid(it, 1)
                    high_part(it, 21)
                    if more:
                        high_rows(it + 1)
                    high_part(it, 22)
                    high_part(it, 23)
                    high_hidden(it, 1)
                    if more:
                        for q in range(6):
                            high_part(it + 1, q)
                    act.wait_ge(parts_used, (it + 1) * PARTS + SPLITS)
                    act.wait_ge(cur_ready, it + 1)
                    act.wait_ge(rows_out, it + 1)
                    act.activation(yb.rearrange("p (b c) -> p b c", b=2), PS[:, 4:6, :], ACT.Copy,
                                   scale=gcur).then_inc(y_scaled, 1)
                    if more:
                        for q in range(6, 15):
                            high_part(it + 1, q)

                if not isinstance(tp, int):
                    for q in range(SPLITS):
                        high_part(tp * NE, q)
                high_rows(tp * NE)
                for q in range(6, 15):
                    high_part(tp * NE, q)
                with act.Fori(0, NE - 1) as e:
                    body(tp * NE + e, True)
                body(tp * NE + (NE - 1), False)

            act.sem_inc(y_scaled, 1)
            act.preload_act_table_set("sigmoid_and_others")
            expert_act(0)
            most = act.value_load(cnt_i[0:1, 0:1], min_val=0, max_val=NTOK)
            with act.Fori(1, NT) as tp:
                with act.If(most > tp * CAP):
                    expert_act(tp)
                act.nop()
            act.nop()
            act.wait_ge(rt_fill, 7)
            act.activation(GT[:, :], PS[0:NE, TURNS[0][0], 0:NTOK], ACT.Copy).then_inc(rt_copy, 1)
            for n, (bank, kind, i, q, m) in enumerate(TURNS[1:]):
                act.wait_ge(rt_fill, 8 + n)
                dst = (acc if kind == "x1" else ga2n)[0:m, i, 512 * q:512 * q + 512]
                act.activation(dst, PS[0:m, bank, :], ACT.Copy).then_inc(rt_copy, 1)

        @block.vector
        def _(dve):
            V = nc.vector
            done = [0]

            def chain(ins):
                done[0] += 1
                ins.then_inc(dve_done, 1)
                dve.wait_ge(dve_done, done[0])

            TT, TS, STT = V.tensor_tensor, V.tensor_scalar, V.scalar_tensor_tensor

            dve.wait_ge(c_sig, 1)
            TT(cn[0:9, :], cn[0:9, :], ce[0:9, :], ALU.mult).then_inc(c_silu, 1)
            dve.wait_ge(set_fill, 1)
            V.tensor_copy(sT, c3(PS[:, 0, 0:DT * 9], 9)).then_inc(set_copy, 1)
            dve.wait_ge(set_fill, 2)
            V.tensor_copy(badaT, PS[:, 1, 0:NMOD * DT])
            V.tensor_copy(gT, PS[:, 1, NMOD * DT:NMOD * DT + 2 * DT]).then_inc(set_copy, 1)
            for n in range(6):
                i, q = divmod(n, 2)
                a, m = TILES[i]
                dve.wait_ge(set_fill, n + 3)
                V.tensor_copy(xT[:, 4 * q:4 * q + 4, a:a + m], c3(PS[:, n + 2, :], P)[:, :, 0:m]).then_inc(set_copy, 1)

            def modulation(c, bank):
                dve.wait_ge(mod_fill, c + 1)
                part = slice(16 * c, 16 * c + 16)
                chain(TT(modT[:, part, :], c3(PS[:, bank, 0:16 * 9], 9),
                         badaT[:, part].unsqueeze(2).to_broadcast([P, 16, 9]), ALU.add))
                dve.sem_inc(mod_ready, 1)

            def scaled_gain(q):
                chain(STT(gs[:, q], modT[:, (3 * q + 1) * DT:(3 * q + 2) * DT, :], 1.0,
                          gT[:, q * DT:(q + 1) * DT].unsqueeze(2).to_broadcast([P, DT, 9]), ALU.add, ALU.mult))

            def norm(k):
                dve.wait_ge(ssq_done, k + 1)
                chain(TS(rst, PS[:, 0, 0:NTOK], 1.0 / D, EPS, ALU.mult, ALU.add))
                V.reciprocal(rst, rst).then_inc(ms_ready, 1)
                if k == 0:
                    modulation(0, 4)
                    scaled_gain(0)
                dve.wait_ge(rstd_ready, k + 1)
                chain(TT(hT[:, :, :], xT[:, :, :], rst.unsqueeze(1).to_broadcast([P, DT, NTOK]), ALU.mult))
                sh = modT[:, 3 * k * DT:(3 * k + 1) * DT, :]
                for m in range(DT):
                    last = TS(hT[:, m, 0:NPR], hT[:, m, 0:NPR], gs[:, k, m, 0:1], sh[:, m, 0:1], ALU.mult, ALU.add)
                hs = hT[:, :, NPR:NTOK].rearrange("p m (b t) -> p m b t", t=NNEW)
                shape = [P, DT, NSEQ, NNEW]
                chain(TT(hs, hs, gs[:, k, :, 1:9].unsqueeze(3).to_broadcast(shape), ALU.mult))
                TT(hs, hs, sh[:, :, 1:9].unsqueeze(3).to_broadcast(shape), ALU.add).then_inc(h_ready, 1)

            norm(0)
            modulation(1, 0)
            modulation(2, 1)
            scaled_gain(1)

            chain(V.memset(small[:, ssh_at:ssh_at + 2 * NT * HEADS], 1.0))
            t3 = c3(T2[:, 0:BW], HD)
            for r in range(2):
                dve.wait_ge(proj_free, 1 + r)
                if r == 0:
                    dve.wait_ge(in_misc, 64)
                x = nat[r]
                for i, (a, m) in enumerate(TILES):
                    xi = x[0:m, i, :]
                    chain(TT(T2[0:m, 0:BW], xi, xi, ALU.mult))
                    chain(V.tensor_reduce(ssh[0:m, r, i, :], t3[0:m], AX.X, ALU.add))
                last = TS(ssh[:, r, 0:2, :], ssh[:, r, 0:2, :], 1.0 / HD, EPS, ALU.mult, ALU.add)
                chain(last)
                chain(TS(ssh[0:NSM, r, 2, :], ssh[0:NSM, r, 2, :], 1.0 / HD, EPS, ALU.mult, ALU.add))
                chain(V.reciprocal(ssh[:, r, :, :], ssh[:, r, :, :]))
                dve.sem_inc(nat_ms, 1)
                dve.wait_ge(nat_rs, r + 1)
                for i, (a, m) in enumerate(TILES):
                    xi = c3(x[0:m, i, :], HD)
                    full = [m, HEADS, HD]
                    chain(TT(xi, xi, ssh[0:m, r, i, :].unsqueeze(2).to_broadcast(full), ALU.mult))
                    chain(TT(xi, xi, qkg[0:m, r, :].unsqueeze(1).to_broadcast(full), ALU.mult))
                    hh = [m, HEADS, HD // 2]
                    co, si = (v[0:m, i, :].unsqueeze(1).to_broadcast(hh) for v in (cosv, sinv))
                    xa, xb = xi[:, :, 0:HD // 2], xi[:, :, HD // 2:HD]
                    ta = c3(T2[0:m, 0:BW // 2], HD // 2)
                    tb = c3(T2[0:m, BW // 2:BW], HD // 2)
                    tc = c3(T2[0:m, BW:BW + BW // 2], HD // 2)
                    TT(ta, xa, si, ALU.mult)
                    TT(tb, xb, si, ALU.mult)
                    TT(tc, xb, co, ALU.mult)
                    chain(TT(xa, xa, co, ALU.mult))
                    TT(xb, ta, tc, ALU.add)
                    chain(TT(xa, xa, tb, ALU.subtract))
                dve.sem_inc(nat_ready, 1)

            def zview(j):
                return PS[:, 2 * (j % 2):2 * (j % 2) + 2, 0:3 * P]

            def diag(ap):
                return ap.rearrange("p h (b k) -> p h b k", k=P)[:, :, 0:3:2, :]

            def over(m):
                return m.unsqueeze(1).unsqueeze(1).to_broadcast([P, 2, 2, P])

            dve.wait_ge(out_keys, 16 * 2)

            def exponents_of(j):
                a1, a2 = pt1[j % 2], pt2[j % 2]
                z = zview(j)
                if j >= 2:
                    dve.wait_ge(at_fill, j - 1)
                if j < 4:
                    dve.wait_ge(pl_ready, j + 1)
                    chain(STT(a2, z, 0.0, a1, ALU.max, ALU.add))
                    chain(TT(diag(a2), diag(a2), over(strict), ALU.mult))
                    for h in range(2):
                        for lo, hi in ((0, P), (P, 3 * P)):
                            rev = a2[:, h, lo:hi][:, ::-1]
                            last = V.tensor_tensor_scan(a1[:, h, lo:hi][:, ::-1], rev, rev, 0.0, ALU.add, ALU.bypass)
                            if h == 1 and lo:
                                chain(last)
                    chain(TT(a1, z, a1, ALU.subtract))
                    dve.sem_inc(pz_free, 1)
                else:
                    dve.wait_ge(pz_fill, j + 1)
                    TT(diag(a1), diag(z), over(causal), ALU.add)
                    chain(V.tensor_copy(a1[:, :, P:2 * P], z[:, :, P:2 * P]))
                    dve.sem_inc(pz_free, 1)
                    V.tensor_reduce(mx[j % 2][:, :, 0:1], a1[:, :, 0:P], AX.X, ALU.max, negate=True)
                    chain(V.tensor_reduce(mx[j % 2][:, :, 1:2], a1[:, :, P:3 * P], AX.X, ALU.max, negate=True))
                dve.sem_inc(pd_ready, 1)

            def weights_of(j):
                a2, sums = pt2[j % 2], ls[j % 2]
                dve.wait_ge(pe_ready, j + 1)
                if j < 4:
                    TT(diag(a2), diag(a2), over(strict), ALU.mult).then_inc(pw_ready, 1)
                else:
                    chain(V.reciprocal(sums, sums))
                    TT(a2[:, :, 0:P], a2[:, :, 0:P], sums[:, :, 0:1].to_broadcast([P, 2, P]), ALU.mult)
                    TT(a2[:, :, P:3 * P], a2[:, :, P:3 * P], sums[:, :, 1:2].to_broadcast([P, 2, 2 * P]),
                       ALU.mult).then_inc(pw_ready, 1)

            chain(V.memset(gt8, -3e38))
            def evacuate_keys(gi, a, b):
                for tp in range(32 * gi + HALF * a + 1, 32 * gi + HALF * b, 2):
                    dve.wait_ge(kt_fill, tp + 1)
                    V.tensor_copy(KT[:, (tp // HALF) % 2, :, (tp % HALF) * P:(tp % HALF + 1) * P],
                                  c3(PS[:, 1, :], P)).then_inc(kt_dve, 1)

            def exponents(gi):
                g = gi % 2
                if gi:
                    dve.wait_ge(aw_fill, gi)
                if gi < 2:
                    dve.wait_ge(dl_ready, gi + 1)
                    chain(STT(T2, Z, 0.0, T1, ALU.max, ALU.add))
                    chain(TT(T2[:, PAST:ROWW], T2[:, PAST:ROWW], newsb[:, g, :], ALU.mult))
                    chain(V.tensor_tensor_scan(T1[:, ::-1], T2[:, ::-1], T2[:, ::-1], 0.0, ALU.add, ALU.bypass))
                    TT(T1, Z, T1, ALU.subtract).then_inc(dd_ready, 1)
                else:
                    dve.wait_ge(z_copy, gi + 1)
                    zb = c3(Z[:, 0:PAST], MOBA)
                    chain(V.tensor_reduce(gt8[:, 0:NMB], zb, AX.X, ALU.add))
                    chain(V.max(m8d, gt8))
                    chain(V.max_index(i8[:, 0, :], m8d, gt8))
                    chain(V.tensor_copy(f8d, i8[:, 0, :]))
                    chain(TS(sel8, iota[:, 0:8], f8d[:, 0:1], -1.0, ALU.is_equal, ALU.add))
                    for q in range(1, MTOP):
                        chain(STT(sel8, iota[:, 0:8], f8d[:, q:q + 1], sel8, ALU.is_equal, ALU.add))
                    chain(TS(sel8, sel8, -NEG, None, ALU.mult))
                    TT(c3(T1[:, 0:PAST], MOBA), zb, sel8[:, 0:NMB].unsqueeze(2).to_broadcast([P, NMB, MOBA]), ALU.add)
                    chain(TT(T1[:, PAST:ROWW], Z[:, PAST:ROWW], newmb[:, g, :], ALU.add))
                    V.tensor_reduce(dmx, T1, AX.X, ALU.max, negate=True).then_inc(dd_ready, 1)

            def weights(gi):
                dve.wait_ge(de_ready, gi + 1)
                if gi < 2:
                    TT(T2[:, PAST:ROWW], T2[:, PAST:ROWW], newsb[:, gi % 2, :], ALU.mult).then_inc(aw_ready, 1)
                else:
                    chain(V.reciprocal(dls, dls))
                    TS(T2, T2, dls, None, ALU.mult).then_inc(aw_ready, 1)

            evacuate_keys(0, 0, 8)
            exponents(0)
            evacuate_keys(1, 0, 2)
            weights(0)
            evacuate_keys(1, 2, 8)
            for gi in range(4):
                pair = (2 * gi, 2 * gi + 1)
                for j in pair:
                    exponents_of(j)
                for j in pair:
                    weights_of(j)
                if gi + 1 < 4:
                    exponents(gi + 1)
                    weights(gi + 1)
                if gi + 2 < 4:
                    evacuate_keys(gi + 2, 0, 8)

            def low_parts(it, a, b):
                for q in range(a, b):
                    if not of_pool(q):
                        dve.wait_ge(high_ready, it * PARTS + (q + 1))
                        TT(WL[:, q % SPLITS, :], raw_part(q), WH[:, q % SPLITS, :].bitcast(F32),
                           ALU.subtract).then_inc(low_dve, 1)

            for s in range(4):
                c, r = divmod(s, 2)
                dve.wait_ge(gate_ready, s + 1)
                dve.wait_ge(used, BRANCH_END[s])
                uc = uT[:, 4 * c:4 * c + 4, :]
                pb = PS[:, 4:8, 0:NTOK]
                if r == 0:
                    chain(TT(uc, pb, sg, ALU.mult))
                else:
                    chain(TT(sg, pb, sg, ALU.mult))
                    chain(TT(uc, uc, sg, ALU.add))
                dve.sem_inc(b_free, 1)
            for c in range(2):
                dve.wait_ge(used, OUT_END[c])
                for m in range(4 * c, 4 * c + 4):
                    STT(xT[:, m, 0:NPR], PS[:, m, 0:NPR], modT[:, 2 * DT + m, 0:1], xT[:, m, 0:NPR], ALU.mult, ALU.add)
                shape = [P, 4, NSEQ, NNEW]
                tmp = sg[:, :, 0:NSM].rearrange("p m (b t) -> p m b t", t=NNEW)
                xs = xT[:, 4 * c:4 * c + 4, NPR:NTOK].rearrange("p m (b t) -> p m b t", t=NNEW)
                ps = PS[:, 4 * c:4 * c + 4, NPR:NTOK].rearrange("p m (b t) -> p m b t", t=NNEW)
                chain(TT(tmp, ps, modT[:, 2 * DT + 4 * c:2 * DT + 4 * c + 4, 1:9].unsqueeze(3).to_broadcast(shape), ALU.mult))
                chain(TT(xs, xs, tmp, ALU.add))
                dve.sem_inc(x1_ready, 1)
            norm(1)
            V.tensor_copy(gx.rearrange("p m (b t) -> p m b t", t=NNEW),
                          modT[:, 5 * DT:6 * DT, 1:9].unsqueeze(3).to_broadcast([P, DT, NSEQ, NNEW])).then_inc(gx_ready, 1)

            low_parts(0, 0, SPLITS)

            chain(V.memset(LG, 0.0))
            chain(V.memset(pos, -1.0))
            chain(V.memset(val, 0.0))
            dve.wait_ge(lg_fill, 1)
            TT(LG[:, 0:2, :], c3(PS[:, 6, 0:2 * NE], NE), brt.unsqueeze(1).to_broadcast([P, 2, NE]), ALU.add)
            chain(TT(LG[0:NSM, 2, :], PS[0:NSM, 6, 2 * NE:3 * NE], brt[0:NSM, :], ALU.add))
            for i in range(NT):
                last = V.max(m8[:, i, :], LG[:, i, :])
            chain(last)
            for i in range(NT):
                last = V.max_index(i8[:, i, :], m8[:, i, :], LG[:, i, :])
            chain(last)
            chain(TS(ngm, m8[:, :, 0], -1.0, None, ALU.mult))
            dve.sem_inc(gl_ready, 1)
            chain(V.tensor_copy(f8, i8[:, :, :]))
            full = [P, NT, TOPK, NE]
            chain(TT(choice, f8[:, :, 0:TOPK].unsqueeze(3).to_broadcast(full),
                     iota[:, 0:NE].unsqueeze(1).unsqueeze(1).to_broadcast(full), ALU.is_equal))
            chain(V.tensor_reduce(msk, choice.rearrange("p a q e -> p a e q"), AX.X, ALU.add))
            dve.sem_inc(mask_ready, 1)
            chain(TT(weighed, choice, iota[:, 0:TOPK].unsqueeze(1).unsqueeze(3).to_broadcast(full), ALU.mult))
            chain(V.tensor_reduce(val[:, :, 0:NE, 1], weighed.rearrange("p a q e -> p a e q"), AX.X, ALU.add))
            chain(TT(val[:, :, 0:NE, 1], val[:, :, 0:NE, 1], row4.unsqueeze(2).to_broadcast([P, NT, NE]), ALU.add))
            dve.wait_ge(rank_fill, 1)
            STT(pos[:, 0:2, 0:NE], c3(PS[:, 7, 0:2 * NE], NE), 1.0, msk[:, 0:2, :], ALU.add, ALU.mult)
            chain(STT(pos[0:NSM, 2, 0:NE], PS[0:NSM, 7, 2 * NE:3 * NE], 1.0, msk[0:NSM, 2, :], ALU.add, ALU.mult))
            TS(pos[:, :, 0:NE], pos[:, :, 0:NE], -1.0, None, ALU.add)
            chain(V.tensor_reduce(cnt, PS[:, 7, NT * NE:(NT + 1) * NE], AX.X, ALU.max))
            chain(V.tensor_copy(cnt_i[0:1, :], cnt[0:1, :]))
            dve.sem_inc(rank_read, 2)

            def gates():
                dve.wait_ge(ge_ready, 1)
                chain(V.reciprocal(gls, gls))
                chain(TT(gt4, gt4, gls.unsqueeze(2).to_broadcast([P, NT, TOPK]), ALU.mult))
                chain(TT(weighed, choice, gt4.unsqueeze(3).to_broadcast(full), ALU.mult))
                chain(V.tensor_reduce(gD, weighed.rearrange("p a q e -> p a e q"), AX.X, ALU.add))
                chain(V.tensor_copy(val[:, :, 0:NE, 0], gD))
                dve.sem_inc(val_ready, 1)
                dve.sem_inc(bb_used, 1)

            def lchain(base, k, ins):
                ins.then_inc(dve_loop, 1)
                dve.wait_ge(dve_loop, base + (k + 1))

            def place(n, e):
                for i, (a, m) in enumerate(TILES):
                    last = TS(onehot[0:m, i, :], iota[0:m, :], pos[0:m, i, bass.ds(e, 1)], None, ALU.is_equal)
                last.then_inc(oh_ready, 1)

            def info(n, e):
                dve.wait_ge(info_fill, n + 1)
                V.tensor_copy(infos[:, bass.ds(e, 1), :].rearrange("p a c -> p (a c)"), PS[:, 3, 0:2]).then_inc(info_ready, 1)

            def low_rows(it):
                dve.wait_ge(xh_ready, it + 1)
                halves = [v.rearrange("p (b c) k -> p b (c k)", b=2) for v in (XL, XH.bitcast(F32))]
                TT(halves[0], PS[:, 6:8, :], halves[1], ALU.subtract).then_inc(xl_ready, 1)

            def low_hidden(it, h):
                dve.wait_ge(hh_ready, 2 * it + (h + 1))
                part = slice(4 * h, 4 * h + 4)
                TT(HL[:, part, :], c3(PS[:, h, :], P), HH[:, part, :].bitcast(F32), ALU.subtract).then_inc(hl_ready, 1)

            LK = 10

            def expert_dve(tp):
                base = tp * NE
                if not isinstance(tp, int):
                    chain_tp = V.tensor_scalar(pos, pos, -float(CAP), None, ALU.add)
                    lchain(tp * (NE * LK + 1) - 1, 0, chain_tp)
                lb0 = tp * (NE * LK + 1)

                def glu_first(it, lb, h):
                    dve.wait_ge(parts_used, it * PARTS + (SPLITS + 8 * h + 8))
                    if h == 0:
                        dve.wait_ge(bb_ready, it + 1)
                    else:
                        dve.wait_ge(hb_ready, 2 * it + 1)
                    TT(u1, PS[:, 2 * h + 1, :], bb[:, FF + 512 * h:FF + 512 * h + 512], ALU.add)
                    lchain(lb, (0, 4)[h], TT(g1, PS[:, 2 * h, :], bb[:, 512 * h:512 * h + 512], ALU.add))
                    lchain(lb, (1, 5)[h], TS(g1, g1, LIMIT, None, ALU.min))
                    dve.sem_inc(g1_ready, 1)

                def glu_last(it, lb, h):
                    lchain(lb, (2, 8)[h], TS(u1, u1, LIMIT, -LIMIT, ALU.min, ALU.max))
                    lchain(lb, (3, 9)[h], STT(u1, u1, 1.0, g1, ALU.add, ALU.mult))
                    dve.wait_ge(e_ready, 2 * it + (h + 1))
                    TT(hb[:, 512 * h:512 * h + 512], u1, e1, ALU.mult).then_inc(hb_ready, 1)

                def body(it, e, more):
                    lb = lb0 + e * LK
                    low_parts(it, 6, 14)
                    glu_first(it, lb, 0)
                    if more:
                        place(it + 1, e + 1)
                    low_parts(it, 14, 15)
                    glu_last(it, lb, 0)
                    low_parts(it, 15, 20)
                    glu_first(it, lb, 1)
                    dve.sem_inc(bb_used, 1)
                    low_hidden(it, 0)
                    low_parts(it, 20, 21)
                    dve.wait_ge(rows_out, it + 1)
                    cur = infos[:, bass.ds(e, 1), :].rearrange("p a c -> p (a c)")
                    lchain(lb, 6, V.tensor_copy(gcur, cur[:, 0:1]))
                    lchain(lb, 7, TS(idx_cur[:, 0:1], cur[:, 1:2], OFF, None, ALU.add))
                    dve.sem_inc(cur_ready, 1)
                    glu_last(it, lb, 1)
                    low_parts(it, 21, 22)
                    if more:
                        low_rows(it + 1)
                    low_parts(it, 22, 24)
                    low_hidden(it, 1)
                    if more:
                        info(it + 1, e + 1)
                        dve.wait_ge(info_ready, it + 2)
                        low_parts(it + 1, 0, 6)

                place(base, 0)
                if isinstance(tp, int):
                    gates()
                else:
                    low_parts(base, 0, SPLITS)
                info(base, 0)
                dve.wait_ge(info_ready, base + 1)
                low_rows(base)
                with dve.Fori(0, NE - 1) as e:
                    body(tp * NE + e, e, True)
                body(tp * NE + (NE - 1), NE - 1, False)

            expert_dve(0)
            most = dve.value_load(cnt_i[0:1, 0:1], min_val=0, max_val=NTOK)
            with dve.Fori(1, NT) as tp:
                with dve.If(most > tp * CAP):
                    expert_dve(tp)
                dve.nop()
            dve.nop()
            for i, (a, m) in enumerate(TILES):
                if i == 0:
                    dve.wait_ge(rt_copy, 6 + len(TURNS))
                dve.wait_ge(back[i], 16)
                rows = c3(last_rows[0:m, :], D)
                if i < 2:
                    rows = ring[0:m, 2 * i:2 * i + 2, :].rearrange("p s (k n) -> p (s k) n", n=D)
                chain(TT(rows[:, 0:2, :], rows[:, 0:2, :], rows[:, 2:4, :], ALU.add))
                chain(TT(rows[:, 0, :], rows[:, 0, :], rows[:, 1, :], ALU.add))
                dve.wait_ge(bd_fill, i + 1)
                chain(TT(c3(rows[:, 0, :], 512), c3(rows[:, 0, :], 512), PS[0:m, BIAS_BANKS[i]:BIAS_BANKS[i] + 2, :], ALU.add))
                chain(TT(rows[:, 0, :], rows[:, 0, :], ga2n[0:m, 0 if i < 2 else 1, :], ALU.mult))
                chain(TT(acc[0:m, i, :], acc[0:m, i, :], rows[:, 0, :], ALU.add))
                dve.sem_inc(y_ready, 1)

        @block.tensor
        def _(pe):
            T = nc.tensor

            def mm(out, lhsT, rhs, start, stop):
                return T.matmul(out, lhsT, rhs, start=start, stop=stop, skip_group_check=True)

            pe.sem_inc(parts_used, SPLITS)
            pe.wait_ge(in_const, 16)
            pe.wait_ge(c_silu, 1)
            for k in range(DT):
                last = T.transpose(PS[:, 0, 9 * k:9 * k + 9], cn[0:9, k * P:(k + 1) * P], ident[0:9, 0:9])
            last.then_inc(set_fill, 1)
            T.transpose(PS[:, 1, 0:NMOD * DT], ban[0:NMOD * DT, :], ident[0:NMOD * DT, 0:NMOD * DT])
            T.transpose(PS[:, 1, NMOD * DT:NMOD * DT + 2 * DT], gn[0:2 * DT, :], ident[0:2 * DT, 0:2 * DT]).then_inc(set_fill, 1)
            pe.wait_ge(in_x, 32)
            for n in range(6):
                i, q = divmod(n, 2)
                m = TILES[i][1]
                for k in range(4):
                    last = T.transpose(PS[:, n + 2, k * P:k * P + m], xn[0:m, i, (4 * q + k) * P:(4 * q + k + 1) * P], ident[0:m, 0:m])
                last.then_inc(set_fill, 1)

            def sum_squares(k):
                pe.wait_ge(sq_ready, 2 * k + 1)
                for m in range(DT):
                    if k and m == 4:
                        pe.wait_ge(sq_ready, 3)
                    last = mm(PS[:, 0, 0:NTOK], ones, hT[:, m, :], m == 0, m == DT - 1)
                last.then_inc(ssq_done, 1)

            sum_squares(0)
            def modulation(c):
                for k in range(DT):
                    n = DT * c + k
                    await_chunk(pe, n)
                    for q in range(4):
                        last = mm(PS[0:9, 4 - 4 * (c % 2) + q, :], sT[:, k, :], slot4(n)[:, q, :], k == 0, k == DT - 1)
                    last.then_inc(used, 1)

            def turn_modulation(c, bank):
                pe.wait_ge(mod_copy, c + 1)
                for m in range(16):
                    last = T.transpose(PS[:, bank, 9 * m:9 * m + 9], mod_rows[0:9, c % 2, m * P:(m + 1) * P], ident[0:9, 0:9])
                last.then_inc(mod_fill, 1)

            pe.wait_ge(set_copy, 8)
            modulation(0)
            pe.wait_ge(ms_ready, 1)
            modulation(1)
            turn_modulation(0, 4)
            pe.wait_ge(mod_ready, 1)
            modulation(2)
            turn_modulation(1, 0)
            turn_modulation(2, 1)

            def turned(n0, rhs, bank, kts):
                for kh in range(kts // 4):
                    await_chunk(pe, n0 + kh)
                    for m in range(4):
                        for k in range(4):
                            last = mm(PS[:, bank + m, 0:NTOK], slot4(n0 + kh)[:, k, m * P:(m + 1) * P], rhs[:, 4 * kh + k, :],
                                      kh == 0 and k == 0, 4 * kh + k == kts - 1)
                    last.then_inc(used, 1)
                return n0 + kts // 4

            def natural(n0, bank):
                for kh in range(2):
                    await_chunk(pe, n0 + kh)
                    for i, (a, m) in enumerate(TILES):
                        for k in range(4):
                            last = mm(PS[0:m, bank + i, :], hT[:, 4 * kh + k, a:a + m], slot4(n0 + kh)[:, k, :],
                                      kh == 0 and k == 0, kh == 1 and k == 3)
                    last.then_inc(used, 1)
                return n0 + 2

            pe.wait_ge(h_ready, 1)
            n = 3 * DT
            for at, c in enumerate(PROJ):
                if at >= 2:
                    pe.wait_ge(proj_free, at - 1)
                if at == 1:
                    pe.wait_ge(mod_ready, 3)
                n = turned(n, hT, proj_bank(at), DT) if c in (Q_SB, K_SB) else natural(n, proj_bank(at))
            pe.wait_ge(proj_free, 6)
            for q in range(9):
                kind, i = divmod(q, 3)
                a, m = TILES[i]
                if kind:
                    pe.wait_ge(nat_ready, kind)
                if q == 8:
                    pe.wait_ge(tr_free, 1)
                for p in range(PAIRS):
                    if kind == 0:
                        last = T.transpose(PS[0:m, q % 8, p * P:(p + 1) * P], kT[0][:, p, a:a + m], ident)
                    else:
                        last = T.transpose(PS[:, q % 8, p * P:p * P + m], nat[kind - 1][0:m, i, p * P:(p + 1) * P], ident[0:m, 0:m])
                last.then_inc(tr_fill, 1)

            pe.wait_ge(tr_free, 9)

            def prompt_scores(j):
                r, p = divmod(j, 4)
                if j >= 2:
                    pe.wait_ge(pz_free, j - 1)
                for h in range(2):
                    rows = slice(HD * h, HD * h + HD)
                    bank = 2 * (j % 2) + h
                    mm(PS[:, bank, 0:P], qT[r][rows, p, 0:P], kT[r][rows, p, 0:P], True, True)
                    last = mm(PS[:, bank, P:3 * P], qT[r][rows, p, P:2 * P], kT[r][rows, p, 0:2 * P], True, True)
                last.then_inc(pz_fill, 1)

            def turn_prompt(j):
                pe.wait_ge(pw_ready, j + 1)
                for h in range(2):
                    for b in range(3):
                        last = T.transpose(PS[:, 5 + h, b * P:(b + 1) * P], pt2[j % 2][:, h, b * P:(b + 1) * P], ident)
                last.then_inc(at_fill, 1)

            def prompt_values(j):
                r, p = divmod(j, 4)
                pe.wait_ge(at_copy, j + 1)
                if j:
                    pe.wait_ge(po_copy, j)
                for h in range(2):
                    v = [vn[r][:, i, (2 * p + h) * HD:(2 * p + h + 1) * HD] for i in range(2)]
                    out = PS[HD * h:HD * h + HD, 7, :]
                    mm(out[:, 0:2 * P], v[0], pAT[:, h, 0:2 * P], True, False)
                    last = mm(out[:, P:2 * P], v[1], pAT[:, h, 2 * P:3 * P], False, True)
                last.then_inc(po_fill, 1)

            def turn_keys(gi, hh):
                chunk = pages_at["k", gi] + hh
                await_chunk(pe, chunk)
                for pg in range(HALF):
                    tp = 32 * gi + HALF * hh + pg
                    if tp >= 2:
                        pe.wait_ge(kt_act if tp % 2 == 0 else kt_dve, tp // 2)
                    for p in range(PAIRS):
                        last = T.transpose(PS[:, tp % 2, p * P:(p + 1) * P], slot4(chunk)[:, pg, p * P:(p + 1) * P], ident)
                    last.then_inc(kt_fill, 1)

            def row_scores(gi, hh):
                g = gi % 2
                b, hf = divmod(hh, 2)
                for s in (kt_act, kt_dve):
                    pe.wait_ge(s, 2 * (8 * gi + hh + 1))
                for p in range(PAIRS):
                    last = mm(PS[32 * b:32 * b + 32, 2 + hf, :], QP[:, 4 * g + b, p, :], KT[:, hh % 2, p, :], p == 0, p == PAIRS - 1)
                last.then_inc(used, 1)

            def scores(gi):
                r, g = divmod(gi, 2)
                turn_keys(gi, 0)
                if gi >= 2:
                    turn_product(gi - 2)
                pe.wait_ge(qp_ready, r + 1)
                if gi:
                    pe.wait_ge(z_copy, gi)
                for hh in range(8):
                    if hh < 7:
                        turn_keys(gi, hh + 1)
                    row_scores(gi, hh)
                for b in range(4):
                    for p in range(PAIRS):
                        last = mm(PS[32 * b:32 * b + 32, 4, 0:NSM], QP[:, 4 * g + b, p, :], kT[r][:, p, NPR:NTOK], p == 0, p == PAIRS - 1)
                last.then_inc(s_fill, 1)

            def turn_weights(gi):
                pe.wait_ge(aw_ready, gi + 1)
                if gi:
                    pe.wait_ge(oh_copy, gi)
                for pg in range(PAGES):
                    T.transpose(PS[:, 5 + pg // 4, (pg % 4) * P:(pg % 4 + 1) * P], T2[:, pg * P:(pg + 1) * P], ident)
                T.transpose(PS[0:NSM, 7, 0:P], T2[:, PAST:ROWW], ident).then_inc(aw_fill, 1)

            def values(gi):
                pe.wait_ge(aw_copy, gi + 1)
                pe.wait_ge(z_copy, min(gi + 2, 4))
                mm(PS[:, 4, :], AT[0:NSM, PAGES, :], vn[gi // 2][0:NSM, 2, :], True, False)
                beside = {1: (turn_prompt, 2 * gi), 2: (prompt_values, 2 * gi),
                          4: (turn_prompt, 2 * gi + 1), 5: (prompt_values, 2 * gi + 1)}
                prompt_scores(2 * gi)
                prompt_scores(2 * gi + 1)
                for hh in range(8):
                    b, hf = divmod(hh, 2)
                    chunk = pages_at["v", gi] + hh
                    await_chunk(pe, chunk)
                    for pg in range(HALF):
                        last = mm(PS[32 * b:32 * b + 32, 4, :], AT[:, HALF * hf + pg, 32 * b:32 * b + 32], slot4(chunk)[:, pg, :],
                                  False, hf == 1 and pg == HALF - 1)
                    last.then_inc(used, 1)
                    if hh in beside:
                        beside[hh][0](beside[hh][1])

            def turn_product(gi):
                pe.wait_ge(pv_copy, gi + 1)
                for p in range(PAIRS):
                    last = T.transpose(PS[:, 7, p * P:(p + 1) * P], pv_rows[:, p * P:(p + 1) * P], ident)
                last.then_inc(pt_fill, 1)

            scores(0)
            scores(1)
            for gi in range(4):
                turn_weights(gi)
                values(gi)
                if gi + 2 < 4:
                    scores(gi + 2)
                else:
                    turn_product(gi)
            n += 64

            for s in range(4):
                c, r = divmod(s, 2)
                if s:
                    pe.wait_ge(gate_ready, s)
                n = turned(n, hT, 0, DT)
                if s:
                    pe.wait_ge(b_free, s)
                else:
                    pe.wait_ge(oh_copy, 4)
                n = turned(n, oT[r], 4, PAIRS)
            pe.wait_ge(b_free, 4)
            for c in range(2):
                n = turned(n, uT, 4 * c, DT)
            assert n == NSTREAM
            sum_squares(1)
            pe.wait_ge(h_ready, 2)
            for i, (a, m) in enumerate(TILES):
                for k in range(DT):
                    last = mm(PS[0:m, 6, NE * i:NE * i + NE], hT[:, k, a:a + m], wr[:, k, :], k == 0, k == DT - 1)
            last.then_inc(lg_fill, 1)
            for q in range(6):
                i, hf = divmod(q, 2)
                a, m = TILES[i]
                for k in range(4):
                    last = T.transpose(PS[0:m, q, k * P:(k + 1) * P], hT[:, 4 * hf + k, a:a + m], ident)
                last.then_inc(rt_fill, 1)
            pe.wait_ge(mask_ready, 1)
            for i, (a, m) in enumerate(TILES):
                out = PS[0:m, 7, NE * i:NE * i + NE]
                for k in range(i + 1):
                    mk = TILES[k][1]
                    mm(out, (below if k == i else ones)[0:mk, 0:m], msk[0:mk, k, :], k == 0, k == i)
            for k, (a, m) in enumerate(TILES):
                last = mm(PS[:, 7, NT * NE:(NT + 1) * NE], ones[0:m, :], msk[0:m, k, :], k == 0, k == NT - 1)
            last.then_inc(rank_fill, 1)
            pe.wait_ge(rt_copy, 6)

            def gather(it):
                pe.wait_ge(oh_ready, it + 1)
                for k in range(DT):
                    for i, (a, m) in enumerate(TILES):
                        last = mm(PS[:, 6 + k // 4, (k % 4) * P:(k % 4 + 1) * P], h2n[0:m, i, k * P:(k + 1) * P],
                                  onehot[0:m, i, :], i == 0, i == NT - 1)
                last.then_inc(gathered, 1)

            def gather_info(e):
                for i, (a, m) in enumerate(TILES):
                    last = mm(PS[:, 3, 0:2], onehot[0:m, i, :], val[0:m, i, bass.ds(e, 1), :].rearrange("p a c -> p (a c)"),
                              i == 0, i == NT - 1)
                last.then_inc(info_fill, 1)

            def three(out, xh, xl, wh, wl, start, stop):
                mm(out, xh, wh, start, False)
                mm(out, xh, wl, False, False)
                return mm(out, xl, wh, False, stop)

            def parts(it, q):
                if of_pool(q):
                    pe.wait_ge(low_pool, pool_lows(it, q))
                else:
                    pe.wait_ge(low_dve, dve_lows(it, q))
                return WH[:, q % SPLITS, :], WL[:, q % SPLITS, :]

            def turn_hidden(it, h):
                pe.wait_ge(hb_ready, 2 * it + (h + 1))
                for k in range(4):
                    at = (4 * h + k) * P
                    last = T.transpose(PS[:, h, k * P:(k + 1) * P], hb[:, at:at + P], ident)
                last.then_inc(hg_fill, 1)

            def down(it, j):
                for k in range(2 * j, 2 * j + 2):
                    wh, wl = parts(it, 16 + k)
                    for hf in range(2):
                        cols = slice(512 * hf, 512 * hf + 512)
                        last = three(PS[:, 4 + hf, :], HH[:, k, :], HL[:, k, :], wh[:, cols], wl[:, cols], k == 0, k == DT - 1)
                    last.then_inc(parts_used, 1)

            def expert_pe(tp):
                def body(it, e, more):
                    pe.wait_ge(xl_ready, it + 1)
                    for j, (h, kh, gu) in enumerate(GU):
                        if j == 4:
                            pe.wait_ge(info_ready, it + 1)
                        for k in range(4 * kh, 4 * kh + 4):
                            if k % 2 == 0:
                                wh, wl = (c3(w, 512) for w in parts(it, 2 * j + k % 4 // 2))
                            last = three(PS[:, 2 * h + gu, :], XH[:, k, :], XL[:, k, :], wh[:, k % 2, :], wl[:, k % 2, :],
                                         k == 0, k == DT - 1)
                            if k % 2:
                                last.then_inc(parts_used, 1)
                    turn_hidden(it, 0)
                    if more:
                        gather(it + 1)
                    pe.wait_ge(hl_ready, 2 * it + 1)
                    pe.wait_ge(y_scaled, it + 1)
                    down(it, 0)
                    turn_hidden(it, 1)
                    if more:
                        gather_info(e + 1)
                    down(it, 1)
                    pe.wait_ge(hl_ready, 2 * it + 2)
                    down(it, 2)
                    down(it, 3)

                gather(tp * NE)
                if isinstance(tp, int):
                    pe.wait_ge(val_ready, 1)
                gather_info(0)
                with pe.Fori(0, NE - 1) as e:
                    body(tp * NE + e, e, True)
                body(tp * NE + (NE - 1), NE - 1, False)

            expert_pe(0)
            most = pe.value_load(cnt_i[0:1, 0:1], min_val=0, max_val=NTOK)
            with pe.Fori(1, NT) as tp:
                with pe.If(most > tp * CAP):
                    expert_pe(tp)
                pe.nop()
            pe.nop()
            pe.wait_ge(gx_ready, 1)
            pe.wait_ge(in_bd, 16)

            def weighted_biases(i):
                a, m = TILES[i]
                for hf in range(2):
                    last = mm(PS[0:m, BIAS_BANKS[i] + hf, :], GT[:, a:a + m], bdn[0:NE, 512 * hf:512 * hf + 512], True, True)
                last.then_inc(bd_fill, 1)

            for n, (bank, kind, i, hf, m) in enumerate(TURNS):
                if n >= len(banks):
                    pe.wait_ge(rt_copy, 6 + n - len(banks) + 1)
                if kind == "gates":
                    for i, (a, m) in enumerate(TILES):
                        last = T.transpose(PS[0:NE, bank, a:a + m], gD[0:m, i, :], ident[0:m, 0:m])
                else:
                    for k in range(4):
                        f = 4 * hf + k
                        if kind == "x1":
                            src = xT[:, f, TILES[i][0]:TILES[i][0] + m]
                        else:
                            src = modT[:, 5 * DT + f, 0:1].to_broadcast([P, P]) if i == 0 else gx[:, f, :]
                        last = T.transpose(PS[0:m, bank, k * P:(k + 1) * P], src, ident)
                last.then_inc(rt_fill, 1)
                if n == 6:
                    pe.wait_ge(rt_copy, 6 + 1)
                    weighted_biases(0)
            pe.wait_ge(rt_copy, 6 + len(TURNS))
            weighted_biases(1)
            weighted_biases(2)


_INS = ["x_prompt", "x_sample", "c_prompt", "c_sample", "cache_sb_k", "cache_sb_v", "cache_mb_k", "cache_mb_v",
        "page_table", "w_ada", "b_ada", "g_norm1", "g_norm2", "w_in", "q_norm_g", "k_norm_g", "w_br_sb", "w_br_mb",
        "w_out", "w_router", "b_router", "w_gu", "b_gu", "w_down", "b_down"]
_OUTS = [("y_prompt", (1, NPR, D)), ("y_sample", (NSEQ, NNEW, D))]
_OUTS += [(f"{r}_{x}_prompt", (1, 1, NPR, HEADS, HD)) for r in ("sb", "mb") for x in "kv"]
_OUTS += [(f"{r}_{x}_sample", (1, NSEQ, NNEW, HEADS, HD)) for r in ("sb", "mb") for x in "kv"]


def kernel(**inputs):
    import concourse.bacc as _bacc
    from concourse.bass_utils import run_bass_kernel_spmd as _run

    nc = _bacc.Bacc("TRN2", target_bir_lowering=False, num_devices=1)
    arrays, ins, outs = {}, {}, {}
    for name in _INS:
        a = np.ascontiguousarray(inputs[name])
        arrays[f"in_{name}"] = a
        ins[name] = nc.dram_tensor(f"in_{name}", a.shape, mybir.dt.from_np(a.dtype), kind="ExternalInput").ap()
    arrays["constants"] = constants()
    ins["constants"] = nc.dram_tensor("constants", (P, NCONST), F32, kind="ExternalInput").ap()
    for name, shape in _OUTS:
        outs[name] = nc.dram_tensor(f"out_{name}", shape, F32, kind="ExternalOutput").ap()
    build(nc, ins, outs)
    r = _run(nc, [arrays], core_ids=[0])
    return tuple(r.results[0][f"out_{name}"] for name, _ in _OUTS)
```

```python
from contextlib import ExitStack

import concourse.bass as bass
import numpy as np
from concourse import mybir

F32 = mybir.dt.float32
F32R = mybir.dt.float32r
I32 = mybir.dt.int32
U32 = mybir.dt.uint32
ALU = mybir.AluOpType
ACT = mybir.ActivationFunctionType
AX = mybir.AxisListType

P = 128
D = 1024
DT = D // P
HD = 64
HEADS = 8
BW = HEADS * HD
PAIRS = BW // P
NPR = 256
NSEQ, NNEW = 8, 4
NSM = NSEQ * NNEW
NTOK = NPR + NSM
TILES = [(0, P), (P, P), (NPR, NSM)]
NT = len(TILES)
PAST = 1024
PAGES = PAST // P
HALF = PAGES // 2
MOBA = 256
NMB = PAST // MOBA
MTOP = 3
NE, TOPK = 32, 4
FF = 1024
CAP = P
LIMIT, ALPHA = 7.0, 1.702
EPS = 1e-6
SCALE = HD ** -0.5
NMOD = 6
SLOTS = 4
SLOTW = 2048
SPLITW = 1024
SPLITS = 6
POOL_EVERY = 4
OFF = float(1 << 20)
NEG = -1e30

CONST = {}
_at = 0
for _name, _n in (("ident", P), ("ones", P), ("below", P), ("iota", P), ("strict", P), ("causal", P),
                  ("cos", NT * HD // 2), ("sin", NT * HD // 2), ("newsb", 2 * NSM), ("newmb", 2 * NSM),
                  ("row4", NT)):
    CONST[_name] = (_at, _at + _n)
    _at += _n
NCONST = _at


def constants():
    c = np.zeros((P, NCONST), np.float32)

    def put(name, x):
        a, b = CONST[name]
        c[:, a:b] = x

    i = np.arange(P)
    put("ident", np.eye(P))
    put("ones", 1.0)
    put("below", i[:, None] < i[None, :])
    put("iota", i[None, :])
    put("strict", i[None, :] < i[:, None])
    put("causal", np.where(i[None, :] <= i[:, None], 0.0, NEG))
    inv = (np.float32(10000.0) ** (-np.arange(0, HD, 2, dtype=np.float32) / np.float32(HD))).astype(np.float32)
    pos = np.zeros((NT, P), np.float32)
    pos[0], pos[1] = i, P + i
    pos[2, :NSM] = PAST + np.arange(NSM) % NNEW
    ang = (pos[:, :, None] * inv).astype(np.float32)
    put("cos", np.cos(ang).transpose(1, 0, 2).reshape(P, -1))
    put("sin", np.sin(ang).transpose(1, 0, 2).reshape(P, -1))
    b, t = i // (HEADS * NNEW), i % NNEW
    kb, kt = np.arange(NSM) // NNEW, np.arange(NSM) % NNEW
    same = [(b[:, None] + 4 * g) == kb[None, :] for g in range(2)]
    put("newsb", np.concatenate([s & (kt[None, :] < t[:, None]) for s in same], 1))
    put("newmb", np.concatenate([np.where(s & (kt[None, :] <= t[:, None]), 0.0, NEG) for s in same], 1))
    put("row4", TOPK * (i[:, None] + np.array([a for a, _ in TILES])[None, :]) - OFF)
    return c


def build(nc, t, o):
    ctx = ExitStack()
    with ctx:
        def sb(name, shape, dt=F32):
            return ctx.enter_context(nc.sbuf_tensor(name, shape, dt))

        def sem(name):
            return ctx.enter_context(nc.semaphore(name))

        PS = ctx.enter_context(nc.psum_tensor("PS", [P, 8, 512], F32))
        ring = sb("ring", [P, SLOTS, SLOTW])
        WH, WL = sb("WH", [P, SPLITS, SPLITW], F32R), sb("WL", [P, SPLITS, SPLITW], F32R)
        XP = sb("XP", [P, 4, DT, P], F32R)
        XH, XL = XP[:, 0], XP[:, 1]
        HH, HL = XP[:, 2], XP[:, 3]
        xT = sb("xT", [P, DT, NTOK])
        hT = sb("hT", [P, DT, NTOK])
        modT = sb("modT", [P, NMOD * DT, 1 + NSEQ])
        gs = sb("gs", [P, 2, DT, 1 + NSEQ])
        cst = sb("cst", [P, NCONST])
        small = sb("small", [P, 1600])
        ptab = sb("ptab", [1, NSEQ * PAGES], I32)
        cnt_i = sb("cnt_i", [1, 1], I32)
        idx_cur = sb("idx_cur", [P, 1], U32)
        i8 = sb("i8", [P, NT, 8], U32)
        arena = sb("arena", [P, 19600])

        cursor = [0]

        def carve(width, start=None):
            if start is not None:
                cursor[0] = start
            a = cursor[0]
            cursor[0] += width
            assert cursor[0] <= 19600, cursor[0]
            return arena[:, a:a + width]

        def c3(ap, b):
            return ap.rearrange("p (a b) -> p a b", b=b)

        def two_parts(flat, kts):
            n = kts * NTOK
            return c3(flat[:, 0:n], NTOK), c3(flat[:, n:2 * n], NTOK)

        hP = two_parts(WH.rearrange("p a b -> p (a b)"), DT)
        oP = two_parts(XP.rearrange("p a b c -> p (a b c)"), PAIRS)
        MIX_SPLITS = 3

        def mix_part(h):
            at = h % MIX_SPLITS * 2
            return c3(WL[:, at, :], 512), c3(WL[:, at + 1, :], 512)

        qT = [c3(carve(PAIRS * NTOK, 0 if r == 0 else None), NTOK) for r in range(2)]
        kT = [c3(carve(PAIRS * NTOK), NTOK) for _ in range(2)]
        vn_at = cursor[0]
        vn = [c3(carve(NT * BW), BW) for _ in range(2)]
        oT = [c3(carve(PAIRS * NTOK), NTOK) for _ in range(2)]
        QP = carve(NSEQ * PAIRS * 32).rearrange("p (b a c) -> p b a c", a=PAIRS, c=32)
        KT_at = cursor[0]
        KT = carve(2 * PAIRS * 512).rearrange("p (s a c) -> p s a c", a=PAIRS, c=512)
        ROWW = PAST + NSM
        Z, T1, T2 = carve(ROWW), carve(ROWW), carve(ROWW)
        AT = c3(carve((PAGES + 1) * P), P)
        pv_rows = AT[:, 0:PAIRS, :].rearrange("p a b -> p (a b)")
        W_end = cursor[0]
        mod_rows = c3(carve(2 * SLOTW, vn_at), SLOTW)
        cursor[0] = W_end
        xn = c3(carve(NT * D, KT_at), D)
        nat = [c3(carve(NT * BW, KT_at), BW), c3(carve(NT * BW), BW)]
        natks = c3(carve(NT * BW, KT_at + 2 * PAIRS * 512), BW)
        PW = 2 * 3 * P
        carve(0, KT_at)
        pt1 = [carve(PW).rearrange("p (h c) -> p h c", h=2), carve(PW).rearrange("p (h c) -> p h c", h=2)]
        pt2 = [carve(PW).rearrange("p (h c) -> p h c", h=2), carve(PW).rearrange("p (h c) -> p h c", h=2)]
        pAT = carve(PW).rearrange("p (h c) -> p h c", h=2)
        assert cursor[0] <= KT_at + 2 * PAIRS * 512
        uT = c3(carve(DT * NTOK, KT_at), NTOK)
        sg = c3(carve(4 * NTOK), NTOK)
        h2n = c3(carve(NT * D, 0), D)
        acc = c3(carve(NT * D), D)
        ga2n = c3(carve(2 * D), D)
        last_at = cursor[0]
        bb = carve(2 * FF)
        g1, u1, e1 = carve(512), carve(512), carve(512)
        hb = carve(FF)
        last_rows = carve(TOPK * D, last_at)
        yb = carve(D)
        bdn = carve(D)
        onehot = c3(carve(NT * P), P)
        choice = bb[:, 0:NT * TOPK * NE].rearrange("p (a q e) -> p a q e", a=NT, q=TOPK)
        weighed = bb[:, NT * TOPK * NE:2 * NT * TOPK * NE].rearrange("p (a q e) -> p a q e", a=NT, q=TOPK)
        bgrow = carve(2 * FF)
        gx = c3(carve(DT * NSM), NSM)
        MOE_END = cursor[0]

        scur = [0]

        def tiny(n, w=None):
            a = scur[0]
            scur[0] += n
            assert scur[0] <= 1600
            ap = small[:, a:a + n]
            return ap if w is None else c3(ap, w)

        badaT = tiny(NMOD * DT)
        gT = tiny(2 * DT)
        sT = tiny(DT * 9, 9)
        rst = tiny(NTOK)
        qkg = tiny(2 * HD, HD)
        ssh_at = scur[0]
        ssh = tiny(NT * HEADS * 2).rearrange("p (r a b) -> p r a b", r=2, b=HEADS)
        mx = [tiny(4, 2), tiny(4, 2)]
        ls = [tiny(4, 2), tiny(4, 2)]
        gt8, m8d, f8d, sel8 = tiny(8), tiny(8), tiny(8), tiny(8)
        dmx, dls = tiny(1), tiny(1)
        LG = tiny(NT * NE, NE)
        m8 = tiny(NT * 8, 8)
        f8 = tiny(NT * 8, 8)
        gt4 = tiny(NT * TOPK, TOPK)
        gls = tiny(NT)
        ngm = tiny(NT)
        msk = tiny(NT * NE, NE)
        gD = tiny(NT * NE, NE)
        pos = tiny(NT * (NE + 1), NE + 1)
        val = tiny(NT * (NE + 1) * 2).rearrange("p (a e c) -> p a e c", a=NT, c=2)
        cnt = tiny(1)
        infos = tiny((NE + 1) * 2, 2)
        gcur = tiny(1)
        brt = tiny(NE)
        wr = sb("wr", [P, DT, NE])
        GT = sb("GT", [NE, NTOK])
        cn = carve(D, 15700)
        ce = carve(D)
        ban = carve(P)
        gn = carve(P)

        def K(name, rows=P):
            a, b = CONST[name]
            return cst[0:rows, a:b]

        ident, ones, below, iota = K("ident"), K("ones"), K("below"), K("iota")
        strict, causal = K("strict"), K("causal")
        cosv, sinv = c3(K("cos"), HD // 2), c3(K("sin"), HD // 2)
        newsb, newmb = c3(K("newsb"), NSM), c3(K("newmb"), NSM)
        row4 = K("row4")

        Y4 = nc.dram_tensor("choice_rows", (NTOK * TOPK, D), F32, kind="Internal").ap()

        in_const, in_c, in_x, in_misc, in_pt = sem("in_const"), sem("in_c"), sem("in_x"), sem("in_misc"), sem("in_pt")
        landed = [sem(f"landed{s}") for s in range(SLOTS)]
        paged = [sem(f"paged{s}") for s in range(SLOTS)]
        used = sem("used")
        mix_high, mix_low, halves_used = sem("mix_high"), sem("mix_low"), sem("halves_used")
        hp_high, hp_low, op_high, op_low = sem("hp_high"), sem("hp_low"), sem("op_high"), sem("op_low")
        up_high, up_low, u_ready = sem("up_high"), sem("up_low"), sem("u_ready")
        c_sig, c_silu = sem("c_sig"), sem("c_silu")
        set_fill, set_copy = sem("set_fill"), sem("set_copy")
        sq_ready, ssq_done, ms_ready, rstd_ready = sem("sq_ready"), sem("ssq_done"), sem("ms_ready"), sem("rstd_ready")
        h_ready = sem("h_ready")
        proj_free = sem("proj_free")
        nat_ready = sem("nat_ready")
        nat_ms, nat_rs = sem("nat_ms"), sem("nat_rs")
        tr_fill, tr_free = sem("tr_fill"), sem("tr_free")
        qp_zero, qp_ready = sem("qp_zero"), sem("qp_ready")
        out_rows, out_keys = sem("out_rows"), sem("out_keys")
        pz_fill, pz_free, pl_ready, pd_ready, pe_ready, pw_ready = (
            sem("pz_fill"), sem("pz_free"), sem("pl_ready"), sem("pd_ready"), sem("pe_ready"), sem("pw_ready"))
        at_fill, at_copy, po_fill, po_copy = sem("at_fill"), sem("at_copy"), sem("po_fill"), sem("po_copy")
        kt_fill, kt_act, kt_dve = sem("kt_fill"), sem("kt_act"), sem("kt_dve")
        s_fill, z_copy, dl_ready, dd_ready, de_ready, aw_ready = (
            sem("s_fill"), sem("z_copy"), sem("dl_ready"), sem("dd_ready"), sem("de_ready"), sem("aw_ready"))
        aw_fill, aw_copy, pv_copy = sem("aw_fill"), sem("aw_copy"), sem("pv_copy")
        pt_fill, oh_copy = sem("pt_fill"), sem("oh_copy")
        mod_copy, mod_fill, mod_ready = sem("mod_copy"), sem("mod_fill"), sem("mod_ready")
        gate_ready, b_free = sem("gate_ready"), sem("b_free")
        x1_ready = sem("x1_ready")
        gx_ready = sem("gx_ready")
        rt_fill, rt_copy = sem("rt_fill"), sem("rt_copy")
        lg_fill, mask_ready, rank_fill, rank_read, gl_ready, ge_ready = (
            sem("lg_fill"), sem("mask_ready"), sem("rank_fill"), sem("rank_read"), sem("gl_ready"), sem("ge_ready"))
        bd_fill, val_ready, acc_ready, y_small = sem("bd_fill"), sem("val_ready"), sem("acc_ready"), sem("y_small")
        oh_ready, gathered, info_fill, info_ready = sem("oh_ready"), sem("gathered"), sem("info_fill"), sem("info_ready")
        high_ready, low_dve, low_pool, parts_used = sem("high_ready"), sem("low_dve"), sem("low_pool"), sem("parts_used")
        xh_ready, xl_ready, hh_ready, hl_ready = sem("xh_ready"), sem("xl_ready"), sem("hh_ready"), sem("hl_ready")
        g1_ready, e_ready, hb_ready = sem("g1_ready"), sem("e_ready"), sem("hb_ready")
        hg_fill, y_scaled = sem("hg_fill"), sem("y_scaled")
        cur_ready, scattered, rows_out = sem("cur_ready"), sem("scattered"), sem("rows_out")
        brow_in, bb_ready, bb_used = sem("brow_in"), sem("bb_ready"), sem("bb_used")
        back_in, y_ready, y_out, in_bd = sem("back_in"), sem("y_ready"), sem("y_out"), sem("in_bd")
        back = [sem(f"back{i}") for i in range(NT)]
        dve_done, act_done, pool_done = sem("dve_done"), sem("act_done"), sem("pool_done")
        dve_loop, pool_step, sp_step = sem("dve_loop"), sem("pool_step"), sem("sp_step")

        cache_k = [t["cache_sb_k"], t["cache_mb_k"]]
        cache_v = [t["cache_sb_v"], t["cache_mb_v"]]
        w_ada = t["w_ada"][0].rearrange("(k p) n -> p k n", p=P)
        w_in = t["w_in"][0].rearrange("(k p) n -> p k n", p=P)
        w_out = t["w_out"][0].rearrange("(k p) n -> p k n", p=P)
        w_br = [t["w_br_sb"][0].rearrange("(k p) n -> p k n", p=P), t["w_br_mb"][0].rearrange("(k p) n -> p k n", p=P)]
        stream = []
        for c in range(3):
            for k in range(DT):
                stream.append(("w", w_ada[:, k, c * SLOTW:(c + 1) * SLOTW]))

        def add_cols(w, col):
            for kh in range(w.shape[1] // 4):
                stream.append(("w4", w[:, 4 * kh:4 * kh + 4, col:col + 512]))

        Q_SB, K_SB, V_SB, Q_MB, K_MB, V_MB = range(6)
        PROJ = [Q_MB, K_MB, Q_SB, K_SB, V_SB, V_MB]
        for c in PROJ:
            add_cols(w_in, BW * c)
        page_chunk, GATE_END, BRANCH_END = {}, [], []

        def add_pages(kind, gi, hh):
            r, g = divmod(gi, 2)
            page_chunk[kind, gi, hh] = len(stream)
            cache = (cache_k if kind == "k" else cache_v)[r]
            stream.append(("pages", cache, (4 * g + hh // 2) * PAGES + hh % 2 * HALF))

        def add_gate(s, kh):
            r, c = divmod(s, 2)
            col = 6 * BW + r * D + 512 * c
            stream.append(("w4", w_in[:, 4 * kh:4 * kh + 4, col:col + 512]))
            if kh:
                GATE_END.append(len(stream))

        def add_branch(s):
            r, c = divmod(s, 2)
            add_cols(w_br[r], 512 * c)
            BRANCH_END.append(len(stream))

        for kind, gi in (("k", 0), ("k", 1), ("v", 0), ("k", 2), ("v", 1), ("k", 3), ("v", 2), ("v", 3)):
            for hh in range(8):
                add_pages(kind, gi, hh)
                if (kind, gi) == ("v", 3) and hh % 2:
                    add_gate(hh // 4, hh // 2 % 2)
        add_branch(0)
        add_branch(1)
        for s in (2, 3):
            add_gate(s, 0)
            add_gate(s, 1)
            add_branch(s)
        for c in range(2):
            add_cols(w_out, 512 * c)
        NSTREAM = len(stream)
        lands, total, paged_total = [], [0] * SLOTS, [0] * SLOTS
        for n, item in enumerate(stream):
            total[n % SLOTS] += 16 * (HALF // 2 if item[0] == "pages" else 1)
            paged_total[n % SLOTS] += 16 * (HALF // 2 if item[0] == "pages" else 0)
            lands.append((total[n % SLOTS], paged_total[n % SLOTS] if item[0] == "pages" else 0))

        MIX = [n for n, item in enumerate(stream) if item[0] == "w4"]

        def await_half_used(eng, h):
            if h % 2:
                eng.wait_ge(used, MIX[h // 2] + 1)
            else:
                eng.wait_ge(halves_used, h // 2 + 1)

        def raw_half(h):
            return slot4(MIX[h // 2])[:, 2 * (h % 2):2 * (h % 2) + 2, :]

        def slot(n):
            return ring[:, n % SLOTS, :]

        def slot4(n):
            return c3(ring[:, n % SLOTS, :], 512)

        def await_chunk(eng, n):
            eng.wait_ge(landed[n % SLOTS], lands[n][0])
            if lands[n][1]:
                eng.wait_ge(paged[n % SLOTS], lands[n][1])

        MOD_END = [DT * (c + 1) for c in range(3)]
        PROJ_END = [MOD_END[-1] + 2 * (c + 1) for c in range(6)]
        OUT_END = [BRANCH_END[-1] + 2 * (c + 1) for c in range(2)]
        assert OUT_END[-1] == NSTREAM
        EXP_CHUNKS = 12
        PARTS = EXP_CHUNKS * SLOTW // SPLITW
        assert NSTREAM % SLOTS == 0 and EXP_CHUNKS % SLOTS == 0 and PARTS % SPLITS == 0 and PARTS % POOL_EVERY == 0

        def of_pool(q):
            return q % POOL_EVERY == POOL_EVERY - 1

        def pool_lows(it, q):
            return it * (PARTS // POOL_EVERY) + ((q + 1) // POOL_EVERY)

        def dve_lows(it, q):
            return it * (PARTS - PARTS // POOL_EVERY) + (q + 1 - (q + 1) // POOL_EVERY)

        def raw_part(q):
            at = q % 2 * SPLITW
            return slot(q // 2)[:, at:at + SPLITW]
        w_gu = t["w_gu"][0].rearrange("e (k p) (j n) -> e p k j n", p=P, j=4)
        w_dn = t["w_down"][0].rearrange("e (k p) n -> e p k n", p=P)

        GU = [(h, kh, j) for h in range(2) for kh in range(2) for j in range(2)]

        banks = [0, 1, 2, 3, 6, 7]
        TURNS = [(0, "gates", 0, 0, NE)]
        TURNS += [(banks[(n + 1) % 6], "x1", n // 2, n % 2, TILES[n // 2][1]) for n in range(6)]
        TURNS += [(banks[(n + 7) % 6], "gate", n // 2, n % 2, (P, NSM)[n // 2]) for n in range(4)]
        BIAS_BANKS = [4, 6, 0]

        def key_bank(tp):
            return (0, 1, 5, 6)[tp % 4]

        def proj_bank(c):
            return 4 - 4 * (c % 2)

        block = ctx.enter_context(nc.Block())

        @block.sync
        def _(sp):
            sp.wait_ge(in_const, 16)
            sp.wait_ge(in_c, 16 * 5)
            for n, item in enumerate(stream):
                if item[0] == "pages":
                    _, cache, at = item
                    if stream[n - 1][0] != "pages":
                        sp.wait_ge(in_pt, 16)
                    pages = [sp.value_load(ptab[0:1, at + j:at + j + 1], min_val=0, max_val=cache.shape[1] - 1)
                             for j in range(HALF // 2)]
                if n >= SLOTS:
                    sp.wait_ge(used, n - SLOTS + 1)
                if item[0] == "w":
                    sp.dma_start(slot(n), item[1]).then_inc(landed[n % SLOTS], 16)
                elif item[0] == "w4":
                    sp.dma_start(slot4(n), item[1]).then_inc(landed[n % SLOTS], 16)
                else:
                    for j, page in enumerate(pages):
                        src = cache[0, bass.ds(page, 1)].rearrange("a p h d -> (a p) (h d)")
                        sp.dma_start(slot4(n)[:, j, :], src).then_inc(landed[n % SLOTS], 16)

            def load_expert_chunk(tp, it, e, j):
                if not isinstance(it, int) or it or j >= SLOTS:
                    before = 2 * (j - SLOTS) + 1
                    sp.wait_ge(low_dve, dve_lows(it, before))
                    sp.sem_inc(sp_step, 1)
                    if not isinstance(it, int) or it or before >= POOL_EVERY - 1:
                        sp.wait_ge(low_pool, pool_lows(it, before))
                else:
                    sp.wait_ge(used, NSTREAM - SLOTS + j + 1)
                one = bass.ds(e, 1)
                if j < 8:
                    h, kh, gu = GU[j]
                    src = w_gu[one, :, 4 * kh:4 * kh + 4, 2 * gu + h, :].rearrange("a p k n -> (a p) k n")
                    sp.dma_start(slot4(j), src).then_inc(landed[j % SLOTS], 16)
                else:
                    src = w_dn[one, :, 2 * (j - 8):2 * (j - 8) + 2, :].rearrange("a p k n -> (a p) k n")
                    sp.dma_start(c3(slot(j), D), src).then_inc(landed[j % SLOTS], 16)

            def load_bias(it, e):
                if not isinstance(it, int) or it:
                    sp.wait_ge(bb_ready, it)
                sp.dma_start(bgrow[0:1, :], t["b_gu"][0, bass.ds(e, 1), :]).then_inc(brow_in, 16)

            def expert_loads(tp):
                load_bias(tp * NE, 0)
                for j in range(SLOTS):
                    load_expert_chunk(tp, tp * NE, 0, j)
                with sp.Fori(0, NE - 1) as e:
                    it = tp * NE + e
                    for j in range(SLOTS, EXP_CHUNKS):
                        load_expert_chunk(tp, it, e, j)
                    load_bias(it + 1, e + 1)
                    for j in range(SLOTS):
                        load_expert_chunk(tp, it + 1, e + 1, j)
                for j in range(SLOTS, EXP_CHUNKS):
                    load_expert_chunk(tp, tp * NE + (NE - 1), NE - 1, j)

            expert_loads(0)
            sp.wait_ge(rank_read, 2)
            most = sp.value_load(cnt_i[0:1, 0:1], min_val=0, max_val=NTOK)
            with sp.Fori(1, NT) as tp:
                with sp.If(most > tp * CAP):
                    expert_loads(tp)
                sp.nop()
            sp.nop()
            sp.wait_ge(back_in, 1)
            for i in (2, 0, 1):
                a, n = TILES[i]
                dst = ring[0:n, 2 * i:2 * i + 2, :].rearrange("p s c -> p (s c)") if i < 2 else last_rows[0:n, :]
                sp.dma_start(dst, Y4[TOPK * a:TOPK * (a + n), :].rearrange("(p k) n -> p (k n)", k=TOPK)
                             ).then_inc(back[i], 16)
            sp.wait_ge(y_ready, 1)
            sp.dma_start(o["y_prompt"][0, 0:P, :], acc[:, 0, :]).then_inc(y_out, 16)
            sp.wait_ge(y_small, 1)
            sp.dma_start(o["y_sample"].rearrange("b t n -> (b t) n"), acc[0:NSM, 2, :]).then_inc(y_out, 16)
            sp.wait_ge(y_ready, 2)
            sp.dma_start(o["y_prompt"][0, P:NPR, :], acc[:, 1, :]).then_inc(y_out, 16)
            sp.wait_ge(y_out, 16 * NT)

        @block.gpsimd
        def _(pool):
            done = [0]

            def chain(ins):
                done[0] += 1
                ins.then_inc(pool_done, 1)
                pool.wait_ge(pool_done, done[0])

            pool.dma_start(ptab[:, :], t["page_table"].rearrange("b n -> (b n)").rearrange("(a n) -> a n", a=1)).then_inc(in_pt, 16)
            pool.dma_start(qkg[:, 0, :], t["q_norm_g"].to_broadcast([P, HD])).then_inc(in_misc, 16)
            pool.dma_start(qkg[:, 1, :], t["k_norm_g"].to_broadcast([P, HD])).then_inc(in_misc, 16)
            pool.dma_start(brt, t["b_router"].to_broadcast([P, NE])).then_inc(in_misc, 16)
            pool.dma_start(wr[:, :, :], t["w_router"][0].rearrange("(k p) e -> p k e", p=P)).then_inc(in_misc, 16)
            pool.memset(QP, 0.0).then_inc(qp_zero, 1)

            def load_pages(a, b):
                for n in range(a, b):
                    if stream[n][0] != "pages":
                        continue
                    _, cache, at = stream[n]
                    pages = [pool.value_load(ptab[0:1, at + j:at + j + 1], min_val=0, max_val=cache.shape[1] - 1)
                             for j in range(HALF // 2, HALF)]
                    pool.wait_ge(used, n - SLOTS + 1)
                    for j, page in enumerate(pages):
                        src = cache[0, bass.ds(page, 1)].rearrange("a p h d -> (a p) (h d)")
                        pool.dma_start(slot4(n)[:, HALF // 2 + j, :], src).then_inc(paged[n % SLOTS], 16)

            def mix_lows(a, b):
                for h in range(a, b):
                    pool.wait_ge(mix_high, h + 1)
                    high, low = mix_part(h)
                    pool.tensor_tensor(low, raw_half(h), high.bitcast(F32), ALU.subtract).then_inc(mix_low, 1)

            def rows_out_of(dp, ds_, src, done):
                pool.dma_start(dp[0, 0].rearrange("(a p) h d -> p a (h d)", p=P), src[:, 0:2, :]).then_inc(done, 16)
                pool.dma_start(ds_[0].rearrange("b t h d -> (b t) (h d)"), src[0:NSM, 2, :]).then_inc(done, 16)

            def pad_queries(r):
                for p in range(PAIRS):
                    for s in range(2):
                        rows = slice(HD * s, HD * s + HD)
                        ins = pool.tensor_copy(
                            QP[rows, :, p, (2 * p + s) * NNEW:(2 * p + s + 1) * NNEW],
                            qT[r][rows, p, NPR:NTOK].rearrange("p (b t) -> p b t", t=NNEW))
                ins.then_inc(qp_ready, 1)

            mix_lows(0, 20)
            pool.wait_ge(nat_ready, 2)
            rows_out_of(o["mb_k_prompt"], o["mb_k_sample"], nat[1], out_keys)
            mix_lows(20, 24)
            pool.wait_ge(proj_free, PROJ.index(V_SB) + 1)
            rows_out_of(o["sb_v_prompt"], o["sb_v_sample"], vn[0], out_rows)
            pool.wait_ge(in_pt, 16)
            first = page_chunk["k", 0, 0]
            load_pages(first, first + SLOTS - 1)
            pool.wait_ge(qp_zero, 1)
            pool.wait_ge(tr_free, 9)
            pad_queries(0)
            load_pages(first + SLOTS - 1, first + 8)
            rows_out_of(o["mb_v_prompt"], o["mb_v_sample"], vn[1], out_rows)
            rows_out_of(o["sb_k_prompt"], o["sb_k_sample"], natks, out_rows)
            load_pages(first + 8, page_chunk["k", 2, 0])
            pool.wait_ge(s_fill, 2)
            pool.wait_ge(qp_ready, 1)
            pad_queries(1)
            load_pages(page_chunk["k", 2, 0], page_chunk["v", 3, 7] + 1)
            pool.wait_ge(mix_low, 32)
            mix_lows(32, 2 * len(MIX))
            pool.wait_ge(x1_ready, 2)
            pool.dma_start(bdn[0:NE, :], t["b_down"][0]).then_inc(in_bd, 16)

            def low_part(it, q):
                pool.wait_ge(high_ready, it * PARTS + (q + 1))
                pool.sem_inc(pool_step, 1)
                pool.tensor_tensor(WL[:, q % SPLITS, :], raw_part(q), WH[:, q % SPLITS, :].bitcast(F32),
                                   ALU.subtract).then_inc(low_pool, 1)

            def biases(it):
                pool.wait_ge(bb_used, it + 1)
                pool.wait_ge(brow_in, (it + 1) * 16)
                pool.sem_inc(pool_step, 1)
                pool.partition_broadcast(bb, bgrow[0:1, :], P).then_inc(bb_ready, 1)

            def expert_pool(tp):
                def body(it, more):
                    for q in (11, 15, 19):
                        low_part(it, q)
                    if more:
                        biases(it + 1)
                    low_part(it, 23)
                    if more:
                        low_part(it + 1, 3)
                    pool.wait_ge(y_scaled, it + 2)
                    pool.sem_inc(pool_step, 1)
                    pool.indirect_dma_start(
                        Y4, bass.IndirectOffsetOnAxis(ap=idx_cur[:, 0:1], axis=0), yb, None,
                        bounds_check=NTOK * TOPK - 1, oob_is_err=False).then_inc(scattered, 16)
                    if more:
                        low_part(it + 1, 7)
                    pool.wait_ge(scattered, (it + 1) * 16)
                    pool.sem_inc(rows_out, 1)

                low_part(tp * NE, 3)
                biases(tp * NE)
                low_part(tp * NE, 7)
                with pool.Fori(0, NE - 1) as e:
                    body(tp * NE + e, True)
                body(tp * NE + (NE - 1), False)

            pool.sem_inc(rows_out, 1)
            expert_pool(0)
            pool.wait_ge(rank_read, 2)
            most = pool.value_load(cnt_i[0:1, 0:1], min_val=0, max_val=NTOK)
            with pool.Fori(1, NT) as tp:
                with pool.If(most > tp * CAP):
                    expert_pool(tp)
                pool.nop()
            pool.nop()
            pool.sem_inc(back_in, 1)
            pool.wait_ge(acc_ready, 1)
            pool.wait_ge(back[2], 16)
            rows, m = c3(last_rows[0:NSM, :], D), NSM
            chain(pool.tensor_tensor(rows[:, 0:2, :], rows[:, 0:2, :], rows[:, 2:4, :], ALU.add))
            chain(pool.tensor_tensor(rows[:, 0, :], rows[:, 0, :], rows[:, 1, :], ALU.add))
            chain(pool.tensor_tensor(rows[:, 0, :], rows[:, 0, :], ga2n[0:m, 1, :], ALU.mult))
            pool.tensor_tensor(acc[0:m, 2, :], acc[0:m, 2, :], rows[:, 0, :], ALU.add).then_inc(y_small, 1)
            pool.wait_ge(out_rows, 16 * 6)
            pool.wait_ge(out_keys, 16 * 2)

        @block.scalar
        def _(act):
            done = [0]

            def chain(ins):
                done[0] += 1
                ins.then_inc(act_done, 1)
                act.wait_ge(act_done, done[0])

            act.dma_start(cst[:, :], t["constants"]).then_inc(in_const, 16)
            act.dma_start(cn[0:1, :], t["c_prompt"]).then_inc(in_c, 16)
            act.dma_start(cn[1:1 + NSEQ, :], t["c_sample"]).then_inc(in_c, 16)
            act.dma_start(ban[0:NMOD * DT, :], t["b_ada"].rearrange("a (m p) -> (a m) p", p=P)).then_inc(in_c, 16)
            act.dma_start(gn[0:DT, :], t["g_norm1"].rearrange("a (m p) -> (a m) p", p=P)).then_inc(in_c, 16)
            act.dma_start(gn[DT:2 * DT, :], t["g_norm2"].rearrange("a (m p) -> (a m) p", p=P)).then_inc(in_c, 16)
            act.dma_start(xn[:, 0:2, :], t["x_prompt"][0].rearrange("(a p) n -> p a n", p=P)).then_inc(in_x, 16)
            act.dma_start(xn[0:NSM, 2, :], t["x_sample"].rearrange("b t n -> (b t) n")).then_inc(in_x, 16)
            act.wait_ge(in_c, 16 * 5)
            act.activation(ce[0:9, :], cn[0:9, :], ACT.Sigmoid).then_inc(c_sig, 1)
            act.wait_ge(set_copy, 8)
            act.activation(hT[:, :, :], xT[:, :, :], ACT.Square).then_inc(sq_ready, 1)


            def rstd(k):
                act.wait_ge(ms_ready, k + 1)
                act.activation(rst, rst, ACT.Sqrt).then_inc(rstd_ready, 1)

            rstd(0)
            def mix_highs(a, b):
                for h in range(a, b):
                    if h % 2 == 0:
                        await_chunk(act, MIX[h // 2])
                    if h >= MIX_SPLITS:
                        await_half_used(act, h - MIX_SPLITS)
                    act.activation(mix_part(h)[0], raw_half(h), ACT.Copy).then_inc(mix_high, 1)

            for c in range(3):
                if c == 2:
                    act.wait_ge(h_ready, 1)
                    act.activation(hP[0], hT[:, :, :], ACT.Copy).then_inc(hp_high, 1)
                    mix_highs(0, 2)
                act.wait_ge(used, MOD_END[c])
                if c == 2:
                    act.wait_ge(mod_fill, 1)
                bank = 4 - 4 * (c % 2)
                act.activation(c3(mod_rows[0:9, c % 2, :], 512), PS[0:9, bank:bank + 4, :], ACT.Copy).then_inc(mod_copy, 1)

            def head_rstd(r):
                act.wait_ge(nat_ms, r + 1)
                v = ssh[:, r, :, :]
                act.activation(v, v, ACT.Sqrt).then_inc(nat_rs, 1)

            mix_highs(2, 6)
            for at, c in enumerate(PROJ):
                act.wait_ge(used, PROJ_END[at])
                bank = proj_bank(at)
                if c in (Q_SB, K_SB):
                    dst = (qT if c == Q_SB else kT)[0]
                    last = act.activation(dst, PS[:, bank:bank + 4, 0:NTOK], ACT.Copy, scale=SCALE if c == Q_SB else 1.0)
                else:
                    dst = {V_SB: vn[0], Q_MB: nat[0], K_MB: nat[1], V_MB: vn[1]}[c]
                    act.activation(dst[:, 0:2, :], PS[:, bank:bank + 2, :], ACT.Copy)
                    last = act.activation(dst[0:NSM, 2, :], PS[0:NSM, bank + 2, :], ACT.Copy)
                last.then_inc(proj_free, 1)
                if at == 1:
                    head_rstd(0)
                mix_highs(4 * at + 6, min(4 * at + 8, 24))
                if at == 2:
                    head_rstd(1)
                mix_highs(4 * at + 8, min(4 * at + 10, 24))
            for n in range(9):
                kind, i = divmod(n, 3)
                a, m = TILES[i]
                act.wait_ge(tr_fill, n + 1)
                if kind == 0:
                    last = act.activation(natks[0:m, i, :], PS[0:m, n % 8, :], ACT.Copy)
                else:
                    src = c3(PS[:, n % 8, :], P)[:, :, 0:m]
                    last = act.activation((qT if kind == 1 else kT)[1][:, :, a:a + m], src, ACT.Copy,
                                          scale=SCALE if kind == 1 else 1.0)
                last.then_inc(tr_free, 1)

            def zview(j):
                return PS[:, 2 * (j % 2):2 * (j % 2) + 2, 0:3 * P]

            def softplus(src, tmp, out_sem):
                chain(act.activation(tmp, src, ACT.Abs))
                chain(act.activation(tmp, tmp, ACT.Exp, scale=-1.0))
                act.activation(tmp, tmp, ACT.Ln, bias=1.0).then_inc(out_sem, 1)

            act.preload_act_table_set("natural_log_exp_and_others")
            act.wait_ge(out_keys, 16 * 2)

            def front(j):
                act.wait_ge(pz_fill, j + 1)
                softplus(zview(j), pt1[j % 2], pl_ready)

            def exponentials_of(j):
                act.wait_ge(pd_ready, j + 1)
                if j < 4:
                    act.activation(pt2[j % 2], pt1[j % 2], ACT.Exp).then_inc(pe_ready, 1)
                else:
                    for h in range(2):
                        act.activation(pt2[j % 2][:, h, 0:P], pt1[j % 2][:, h, 0:P], ACT.Exp,
                                       bias=mx[j % 2][:, h, 0:1], accum_out=ls[j % 2][:, h, 0:1])
                        last = act.activation(pt2[j % 2][:, h, P:3 * P], pt1[j % 2][:, h, P:3 * P], ACT.Exp,
                                              bias=mx[j % 2][:, h, 1:2], accum_out=ls[j % 2][:, h, 1:2])
                    last.then_inc(pe_ready, 1)

            def copies_of(j):
                act.wait_ge(at_fill, j + 1)
                act.activation(pAT, PS[:, 5:7, 0:3 * P], ACT.Copy).then_inc(at_copy, 1)
                act.wait_ge(po_fill, j + 1)
                act.activation(oT[j // 4][:, j % 4, 0:NPR], PS[:, 7, 0:NPR], ACT.Copy).then_inc(po_copy, 1)

            def evacuate_keys(gi, a, b):
                for tp in range(32 * gi + HALF * a, 32 * gi + HALF * b, 2):
                    act.wait_ge(kt_fill, tp + 1)
                    act.activation(KT[:, (tp // HALF) % 2, :, (tp % HALF) * P:(tp % HALF + 1) * P],
                                   c3(PS[:, key_bank(tp), :], P), ACT.Copy).then_inc(kt_act, 1)

            def copy_scores(gi):
                act.wait_ge(s_fill, gi + 1)
                if gi:
                    act.wait_ge(aw_ready, gi)
                act.activation(c3(Z[:, 0:PAST], 512), PS[:, 2:4, :], ACT.Copy)
                chain(act.activation(Z[:, PAST:ROWW], PS[:, 4, 0:NSM], ACT.Copy))
                act.sem_inc(z_copy, 1)

            def exponentials(gi):
                act.wait_ge(dd_ready, gi + 1)
                if gi < 2:
                    act.activation(T2, T1, ACT.Exp).then_inc(de_ready, 1)
                else:
                    act.activation(T2, T1, ACT.Exp, bias=dmx, accum_out=dls).then_inc(de_ready, 1)

            def copy_weights(gi):
                act.wait_ge(aw_fill, gi + 1)
                if gi:
                    act.wait_ge(pt_fill, gi)
                act.activation(c3(AT[:, 0:PAGES, :].rearrange("p a b -> p (a b)"), 512), PS[:, 5:7, :], ACT.Copy)
                act.activation(AT[0:NSM, PAGES, :], PS[0:NSM, 7, 0:P], ACT.Copy).then_inc(aw_copy, 1)

            def copy_product(gi):
                act.wait_ge(used, page_chunk["v", gi, 7] + 1)
                act.activation(pv_rows, PS[:, 4, :], ACT.Copy).then_inc(pv_copy, 1)

            def copy_heads(gi):
                r, g = divmod(gi, 2)
                act.wait_ge(pt_fill, gi + 1)
                for s in range(2):
                    rows = slice(HD * s, HD * s + HD)
                    for p in range(PAIRS):
                        src = c3(PS[rows, 7, p * P:(p + 1) * P], 32)[:, :, (2 * p + s) * NNEW:(2 * p + s + 1) * NNEW]
                        at = NPR + 4 * g * NNEW
                        last = act.activation(oT[r][rows, p, at:at + 4 * NNEW].rearrange("p (b t) -> p b t", t=NNEW), src, ACT.Copy)
                last.then_inc(oh_copy, 1)

            evacuate_keys(0, 0, 8)
            act.wait_ge(out_rows, 16 * 6)
            copy_scores(0)
            softplus(Z, T1, dl_ready)
            evacuate_keys(1, 0, 2)
            exponentials(0)
            evacuate_keys(1, 2, 8)
            copy_scores(1)
            def branch_high(r):
                act.activation(oP[0], oT[r], ACT.Copy).then_inc(op_high, 1)

            def merged_high(c):
                act.wait_ge(u_ready, c + 1)
                half = slice(4 * c, 4 * c + 4)
                act.activation(hP[0][:, half, :], uT[:, half, :], ACT.Copy).then_inc(up_high, 1)

            def gate_sigmoid(s):
                act.wait_ge(used, GATE_END[s])
                if s:
                    act.wait_ge(b_free, s)
                act.activation(sg, PS[:, 0:4, 0:NTOK], ACT.Sigmoid).then_inc(gate_ready, 1)

            for gi in range(2):
                copy_weights(gi)
                pair = (2 * gi, 2 * gi + 1)
                if gi < 2:
                    for j in pair:
                        front(j)
                for j in pair:
                    exponentials_of(j)
                for j in pair:
                    copies_of(j)
                if gi == 0:
                    softplus(Z, T1, dl_ready)
                exponentials(gi + 1)
                copy_product(gi)
                evacuate_keys(gi + 2, 0, 1)
                copy_heads(gi)
                evacuate_keys(gi + 2, 1, 8)
                copy_scores(gi + 2)
            copy_weights(2)
            exponentials(3)
            for j in range(4, 8):
                exponentials_of(j)
                copies_of(j)
            copy_product(2)
            copy_heads(2)
            copy_weights(3)
            act.wait_ge(po_copy, 4)
            act.wait_ge(oh_copy, 2)
            branch_high(0)
            mix_highs(24, 30)
            gate_sigmoid(0)
            mix_highs(30, 32)
            copy_product(3)
            mix_highs(32, 34)
            copy_heads(3)
            mix_highs(34, 36)
            gate_sigmoid(1)
            mix_highs(36, 39)
            act.wait_ge(used, BRANCH_END[1])
            act.wait_ge(po_copy, 8)
            act.wait_ge(oh_copy, 4)
            branch_high(1)
            mix_highs(39, 42)
            gate_sigmoid(2)
            mix_highs(42, 48)
            gate_sigmoid(3)
            merged_high(0)
            mix_highs(48, 51)
            merged_high(1)
            mix_highs(51, 56)

            def high_part(it, q):
                if q % 2 == 0:
                    j = q // 2
                    act.wait_ge(landed[j % SLOTS], (it * (EXP_CHUNKS // SLOTS) + (j // SLOTS + 1)) * 16 + total[j % SLOTS])
                act.wait_ge(parts_used, it * PARTS + (q + 1))
                act.activation(WH[:, q % SPLITS, :], raw_part(q), ACT.Copy).then_inc(high_ready, 1)

            for c in range(2):
                half = slice(4 * c, 4 * c + 4)
                act.wait_ge(x1_ready, c + 1)
                act.activation(hT[:, half, :], xT[:, half, :], ACT.Square).then_inc(sq_ready, 1)
            for q in range(SPLITS):
                high_part(0, q)
            rstd(1)
            def softmax_exp():
                act.wait_ge(gl_ready, 1)
                for i in range(NT):
                    last = act.activation(gt4[:, i, :], m8[:, i, 0:TOPK], ACT.Exp, bias=ngm[:, i:i + 1], accum_out=gls[:, i:i + 1])
                last.then_inc(ge_ready, 1)

            for n in range(6):
                i, q = divmod(n, 2)
                m = TILES[i][1]
                act.wait_ge(rt_fill, n + 1)
                act.activation(h2n[0:m, i, 512 * q:512 * q + 512], PS[0:m, n, :], ACT.Copy).then_inc(rt_copy, 1)
            softmax_exp()

            def high_rows(it):
                act.wait_ge(gathered, it + 1)
                act.activation(XH.rearrange("p (b c) k -> p b (c k)", b=2), PS[:, 6:8, :], ACT.Copy).then_inc(xh_ready, 1)

            def high_hidden(it, h):
                act.wait_ge(hg_fill, 2 * it + (h + 1))
                act.activation(HH[:, 4 * h:4 * h + 4, :], c3(PS[:, h, :], P), ACT.Copy).then_inc(hh_ready, 1)

            def sigmoid(it, h):
                act.wait_ge(g1_ready, 2 * it + (h + 1))
                act.activation(e1, g1, ACT.Sigmoid, scale=ALPHA).then_inc(e_ready, 1)

            def expert_act(tp):
                def body(it, more):
                    sigmoid(it, 0)
                    for q in range(15, 21):
                        high_part(it, q)
                    high_hidden(it, 0)
                    sigmoid(it, 1)
                    high_part(it, 21)
                    if more:
                        high_rows(it + 1)
                    high_part(it, 22)
                    high_part(it, 23)
                    high_hidden(it, 1)
                    if more:
                        for q in range(6):
                            high_part(it + 1, q)
                    act.wait_ge(parts_used, (it + 1) * PARTS + SPLITS)
                    act.wait_ge(cur_ready, it + 1)
                    act.wait_ge(rows_out, it + 1)
                    act.activation(yb.rearrange("p (b c) -> p b c", b=2), PS[:, 4:6, :], ACT.Copy,
                                   scale=gcur).then_inc(y_scaled, 1)
                    if more:
                        for q in range(6, 15):
                            high_part(it + 1, q)

                if not isinstance(tp, int):
                    for q in range(SPLITS):
                        high_part(tp * NE, q)
                high_rows(tp * NE)
                for q in range(6, 15):
                    high_part(tp * NE, q)
                with act.Fori(0, NE - 1) as e:
                    body(tp * NE + e, True)
                body(tp * NE + (NE - 1), False)

            act.sem_inc(y_scaled, 1)
            act.preload_act_table_set("sigmoid_and_others")
            expert_act(0)
            most = act.value_load(cnt_i[0:1, 0:1], min_val=0, max_val=NTOK)
            with act.Fori(1, NT) as tp:
                with act.If(most > tp * CAP):
                    expert_act(tp)
                act.nop()
            act.nop()
            act.wait_ge(rt_fill, 7)
            act.activation(GT[:, :], PS[0:NE, TURNS[0][0], 0:NTOK], ACT.Copy).then_inc(rt_copy, 1)
            for n, (bank, kind, i, q, m) in enumerate(TURNS[1:]):
                act.wait_ge(rt_fill, 8 + n)
                dst = (acc if kind == "x1" else ga2n)[0:m, i, 512 * q:512 * q + 512]
                act.activation(dst, PS[0:m, bank, :], ACT.Copy).then_inc(rt_copy, 1)

        @block.vector
        def _(dve):
            V = nc.vector
            done = [0]

            def chain(ins):
                done[0] += 1
                ins.then_inc(dve_done, 1)
                dve.wait_ge(dve_done, done[0])

            TT, TS, STT = V.tensor_tensor, V.tensor_scalar, V.scalar_tensor_tensor

            dve.wait_ge(c_sig, 1)
            TT(cn[0:9, :], cn[0:9, :], ce[0:9, :], ALU.mult).then_inc(c_silu, 1)
            dve.wait_ge(set_fill, 1)
            V.tensor_copy(sT, c3(PS[:, 0, 0:DT * 9], 9)).then_inc(set_copy, 1)
            dve.wait_ge(set_fill, 2)
            V.tensor_copy(badaT, PS[:, 1, 0:NMOD * DT])
            V.tensor_copy(gT, PS[:, 1, NMOD * DT:NMOD * DT + 2 * DT]).then_inc(set_copy, 1)
            for n in range(6):
                i, q = divmod(n, 2)
                a, m = TILES[i]
                dve.wait_ge(set_fill, n + 3)
                V.tensor_copy(xT[:, 4 * q:4 * q + 4, a:a + m], c3(PS[:, n + 2, :], P)[:, :, 0:m]).then_inc(set_copy, 1)

            def modulation(c, bank):
                dve.wait_ge(mod_fill, c + 1)
                part = slice(16 * c, 16 * c + 16)
                chain(TT(modT[:, part, :], c3(PS[:, bank, 0:16 * 9], 9),
                         badaT[:, part].unsqueeze(2).to_broadcast([P, 16, 9]), ALU.add))
                dve.sem_inc(mod_ready, 1)

            def scaled_gain(q):
                chain(STT(gs[:, q], modT[:, (3 * q + 1) * DT:(3 * q + 2) * DT, :], 1.0,
                          gT[:, q * DT:(q + 1) * DT].unsqueeze(2).to_broadcast([P, DT, 9]), ALU.add, ALU.mult))

            def norm(k):
                dve.wait_ge(ssq_done, k + 1)
                chain(TS(rst, PS[:, 0, 0:NTOK], 1.0 / D, EPS, ALU.mult, ALU.add))
                V.reciprocal(rst, rst).then_inc(ms_ready, 1)
                if k == 0:
                    modulation(0, 4)
                    scaled_gain(0)
                dve.wait_ge(rstd_ready, k + 1)
                chain(TT(hT[:, :, :], xT[:, :, :], rst.unsqueeze(1).to_broadcast([P, DT, NTOK]), ALU.mult))
                sh = modT[:, 3 * k * DT:(3 * k + 1) * DT, :]
                for m in range(DT):
                    last = TS(hT[:, m, 0:NPR], hT[:, m, 0:NPR], gs[:, k, m, 0:1], sh[:, m, 0:1], ALU.mult, ALU.add)
                hs = hT[:, :, NPR:NTOK].rearrange("p m (b t) -> p m b t", t=NNEW)
                shape = [P, DT, NSEQ, NNEW]
                chain(TT(hs, hs, gs[:, k, :, 1:9].unsqueeze(3).to_broadcast(shape), ALU.mult))
                TT(hs, hs, sh[:, :, 1:9].unsqueeze(3).to_broadcast(shape), ALU.add).then_inc(h_ready, 1)

            norm(0)
            dve.wait_ge(hp_high, 1)
            TT(hP[1], hT[:, :, :], hP[0].bitcast(F32), ALU.subtract).then_inc(hp_low, 1)
            modulation(1, 0)
            modulation(2, 1)
            scaled_gain(1)

            chain(V.memset(small[:, ssh_at:ssh_at + 2 * NT * HEADS], 1.0))
            t3 = c3(T2[:, 0:BW], HD)
            for r in range(2):
                dve.wait_ge(proj_free, 1 + r)
                if r == 0:
                    dve.wait_ge(in_misc, 64)
                x = nat[r]
                for i, (a, m) in enumerate(TILES):
                    xi = x[0:m, i, :]
                    chain(TT(T2[0:m, 0:BW], xi, xi, ALU.mult))
                    chain(V.tensor_reduce(ssh[0:m, r, i, :], t3[0:m], AX.X, ALU.add))
                last = TS(ssh[:, r, 0:2, :], ssh[:, r, 0:2, :], 1.0 / HD, EPS, ALU.mult, ALU.add)
                chain(last)
                chain(TS(ssh[0:NSM, r, 2, :], ssh[0:NSM, r, 2, :], 1.0 / HD, EPS, ALU.mult, ALU.add))
                chain(V.reciprocal(ssh[:, r, :, :], ssh[:, r, :, :]))
                dve.sem_inc(nat_ms, 1)
                dve.wait_ge(nat_rs, r + 1)
                for i, (a, m) in enumerate(TILES):
                    xi = c3(x[0:m, i, :], HD)
                    full = [m, HEADS, HD]
                    chain(TT(xi, xi, ssh[0:m, r, i, :].unsqueeze(2).to_broadcast(full), ALU.mult))
                    chain(TT(xi, xi, qkg[0:m, r, :].unsqueeze(1).to_broadcast(full), ALU.mult))
                    hh = [m, HEADS, HD // 2]
                    co, si = (v[0:m, i, :].unsqueeze(1).to_broadcast(hh) for v in (cosv, sinv))
                    xa, xb = xi[:, :, 0:HD // 2], xi[:, :, HD // 2:HD]
                    ta = c3(T2[0:m, 0:BW // 2], HD // 2)
                    tb = c3(T2[0:m, BW // 2:BW], HD // 2)
                    tc = c3(T2[0:m, BW:BW + BW // 2], HD // 2)
                    TT(ta, xa, si, ALU.mult)
                    TT(tb, xb, si, ALU.mult)
                    TT(tc, xb, co, ALU.mult)
                    chain(TT(xa, xa, co, ALU.mult))
                    TT(xb, ta, tc, ALU.add)
                    chain(TT(xa, xa, tb, ALU.subtract))
                dve.sem_inc(nat_ready, 1)

            def zview(j):
                return PS[:, 2 * (j % 2):2 * (j % 2) + 2, 0:3 * P]

            def diag(ap):
                return ap.rearrange("p h (b k) -> p h b k", k=P)[:, :, 0:3:2, :]

            def over(m):
                return m.unsqueeze(1).unsqueeze(1).to_broadcast([P, 2, 2, P])

            dve.wait_ge(out_keys, 16 * 2)

            def exponents_of(j):
                a1, a2 = pt1[j % 2], pt2[j % 2]
                z = zview(j)
                if j >= 2:
                    dve.wait_ge(at_fill, j - 1)
                if j < 4:
                    dve.wait_ge(pl_ready, j + 1)
                    chain(STT(a2, z, 0.0, a1, ALU.max, ALU.add))
                    chain(TT(diag(a2), diag(a2), over(strict), ALU.mult))
                    for h in range(2):
                        for lo, hi in ((0, P), (P, 3 * P)):
                            rev = a2[:, h, lo:hi][:, ::-1]
                            last = V.tensor_tensor_scan(a1[:, h, lo:hi][:, ::-1], rev, rev, 0.0, ALU.add, ALU.bypass)
                            if h == 1 and lo:
                                chain(last)
                    chain(TT(a1, z, a1, ALU.subtract))
                    dve.sem_inc(pz_free, 1)
                else:
                    dve.wait_ge(pz_fill, j + 1)
                    TT(diag(a1), diag(z), over(causal), ALU.add)
                    chain(V.tensor_copy(a1[:, :, P:2 * P], z[:, :, P:2 * P]))
                    dve.sem_inc(pz_free, 1)
                    V.tensor_reduce(mx[j % 2][:, :, 0:1], a1[:, :, 0:P], AX.X, ALU.max, negate=True)
                    chain(V.tensor_reduce(mx[j % 2][:, :, 1:2], a1[:, :, P:3 * P], AX.X, ALU.max, negate=True))
                dve.sem_inc(pd_ready, 1)

            def weights_of(j):
                a2, sums = pt2[j % 2], ls[j % 2]
                dve.wait_ge(pe_ready, j + 1)
                if j < 4:
                    TT(diag(a2), diag(a2), over(strict), ALU.mult).then_inc(pw_ready, 1)
                else:
                    chain(V.reciprocal(sums, sums))
                    TT(a2[:, :, 0:P], a2[:, :, 0:P], sums[:, :, 0:1].to_broadcast([P, 2, P]), ALU.mult)
                    TT(a2[:, :, P:3 * P], a2[:, :, P:3 * P], sums[:, :, 1:2].to_broadcast([P, 2, 2 * P]),
                       ALU.mult).then_inc(pw_ready, 1)

            chain(V.memset(gt8, -3e38))
            def evacuate_keys(gi, a, b):
                for tp in range(32 * gi + HALF * a + 1, 32 * gi + HALF * b, 2):
                    dve.wait_ge(kt_fill, tp + 1)
                    V.tensor_copy(KT[:, (tp // HALF) % 2, :, (tp % HALF) * P:(tp % HALF + 1) * P],
                                  c3(PS[:, key_bank(tp), :], P)).then_inc(kt_dve, 1)

            def exponents(gi):
                g = gi % 2
                if gi:
                    dve.wait_ge(aw_fill, gi)
                if gi < 2:
                    dve.wait_ge(dl_ready, gi + 1)
                    chain(STT(T2, Z, 0.0, T1, ALU.max, ALU.add))
                    chain(TT(T2[:, PAST:ROWW], T2[:, PAST:ROWW], newsb[:, g, :], ALU.mult))
                    chain(V.tensor_tensor_scan(T1[:, ::-1], T2[:, ::-1], T2[:, ::-1], 0.0, ALU.add, ALU.bypass))
                    TT(T1, Z, T1, ALU.subtract).then_inc(dd_ready, 1)
                else:
                    dve.wait_ge(z_copy, gi + 1)
                    zb = c3(Z[:, 0:PAST], MOBA)
                    chain(V.tensor_reduce(gt8[:, 0:NMB], zb, AX.X, ALU.add))
                    chain(V.max(m8d, gt8))
                    chain(V.max_index(i8[:, 0, :], m8d, gt8))
                    chain(V.tensor_copy(f8d, i8[:, 0, :]))
                    chain(TS(sel8, iota[:, 0:8], f8d[:, 0:1], -1.0, ALU.is_equal, ALU.add))
                    for q in range(1, MTOP):
                        chain(STT(sel8, iota[:, 0:8], f8d[:, q:q + 1], sel8, ALU.is_equal, ALU.add))
                    chain(TS(sel8, sel8, -NEG, None, ALU.mult))
                    TT(c3(T1[:, 0:PAST], MOBA), zb, sel8[:, 0:NMB].unsqueeze(2).to_broadcast([P, NMB, MOBA]), ALU.add)
                    chain(TT(T1[:, PAST:ROWW], Z[:, PAST:ROWW], newmb[:, g, :], ALU.add))
                    V.tensor_reduce(dmx, T1, AX.X, ALU.max, negate=True).then_inc(dd_ready, 1)

            def weights(gi):
                dve.wait_ge(de_ready, gi + 1)
                if gi < 2:
                    TT(T2[:, PAST:ROWW], T2[:, PAST:ROWW], newsb[:, gi % 2, :], ALU.mult).then_inc(aw_ready, 1)
                else:
                    chain(V.reciprocal(dls, dls))
                    TS(T2, T2, dls, None, ALU.mult).then_inc(aw_ready, 1)

            evacuate_keys(0, 0, 8)
            exponents(0)
            evacuate_keys(1, 0, 2)
            weights(0)
            evacuate_keys(1, 2, 8)
            for gi in range(2):
                pair = (2 * gi, 2 * gi + 1)
                for j in pair:
                    exponents_of(j)
                for j in pair:
                    weights_of(j)
                exponents(gi + 1)
                weights(gi + 1)
                evacuate_keys(gi + 2, 0, 8)
            exponents(3)
            exponents_of(4)
            weights(3)
            for j in range(4, 8):
                if j + 1 < 8:
                    exponents_of(j + 1)
                weights_of(j)

            def low_parts(it, a, b):
                for q in range(a, b):
                    if not of_pool(q):
                        dve.wait_ge(high_ready, it * PARTS + (q + 1))
                        TT(WL[:, q % SPLITS, :], raw_part(q), WH[:, q % SPLITS, :].bitcast(F32),
                           ALU.subtract).then_inc(low_dve, 1)

            def branch_low(r):
                dve.wait_ge(op_high, r + 1)
                TT(oP[1], oT[r], oP[0].bitcast(F32), ALU.subtract).then_inc(op_low, 1)

            def merged_low(c):
                dve.wait_ge(up_high, c + 1)
                half = slice(4 * c, 4 * c + 4)
                TT(hP[1][:, half, :], uT[:, half, :], hP[0][:, half, :].bitcast(F32), ALU.subtract).then_inc(up_low, 1)

            branch_low(0)
            for h in range(24, 32):
                dve.wait_ge(mix_high, h + 1)
                high, low = mix_part(h)
                TT(low, raw_half(h), high.bitcast(F32), ALU.subtract).then_inc(mix_low, 1)
            for s in range(4):
                r, c = divmod(s, 2)
                dve.wait_ge(gate_ready, s + 1)
                dve.wait_ge(used, BRANCH_END[s])
                uc = uT[:, 4 * c:4 * c + 4, :]
                pb = PS[:, 4:8, 0:NTOK]
                if r == 0:
                    chain(TT(uc, pb, sg, ALU.mult))
                    dve.sem_inc(b_free, 1)
                else:
                    chain(TT(sg, pb, sg, ALU.mult))
                    chain(TT(uc, uc, sg, ALU.add))
                    dve.sem_inc(b_free, 1)
                    dve.sem_inc(u_ready, 1)
                if s == 1:
                    branch_low(1)
                if s >= 2:
                    merged_low(c)
            for c in range(2):
                dve.wait_ge(used, OUT_END[c])
                for m in range(4 * c, 4 * c + 4):
                    STT(xT[:, m, 0:NPR], PS[:, m, 0:NPR], modT[:, 2 * DT + m, 0:1], xT[:, m, 0:NPR], ALU.mult, ALU.add)
                shape = [P, 4, NSEQ, NNEW]
                tmp = sg[:, :, 0:NSM].rearrange("p m (b t) -> p m b t", t=NNEW)
                xs = xT[:, 4 * c:4 * c + 4, NPR:NTOK].rearrange("p m (b t) -> p m b t", t=NNEW)
                ps = PS[:, 4 * c:4 * c + 4, NPR:NTOK].rearrange("p m (b t) -> p m b t", t=NNEW)
                chain(TT(tmp, ps, modT[:, 2 * DT + 4 * c:2 * DT + 4 * c + 4, 1:9].unsqueeze(3).to_broadcast(shape), ALU.mult))
                chain(TT(xs, xs, tmp, ALU.add))
                dve.sem_inc(x1_ready, 1)
            norm(1)
            V.tensor_copy(gx.rearrange("p m (b t) -> p m b t", t=NNEW),
                          modT[:, 5 * DT:6 * DT, 1:9].unsqueeze(3).to_broadcast([P, DT, NSEQ, NNEW])).then_inc(gx_ready, 1)

            low_parts(0, 0, SPLITS)

            chain(V.memset(LG, 0.0))
            chain(V.memset(pos, -1.0))
            chain(V.memset(val, 0.0))
            dve.wait_ge(lg_fill, 1)
            TT(LG[:, 0:2, :], c3(PS[:, 6, 0:2 * NE], NE), brt.unsqueeze(1).to_broadcast([P, 2, NE]), ALU.add)
            chain(TT(LG[0:NSM, 2, :], PS[0:NSM, 6, 2 * NE:3 * NE], brt[0:NSM, :], ALU.add))
            for i in range(NT):
                last = V.max(m8[:, i, :], LG[:, i, :])
            chain(last)
            for i in range(NT):
                last = V.max_index(i8[:, i, :], m8[:, i, :], LG[:, i, :])
            chain(last)
            chain(TS(ngm, m8[:, :, 0], -1.0, None, ALU.mult))
            dve.sem_inc(gl_ready, 1)
            chain(V.tensor_copy(f8, i8[:, :, :]))
            full = [P, NT, TOPK, NE]
            chain(TT(choice, f8[:, :, 0:TOPK].unsqueeze(3).to_broadcast(full),
                     iota[:, 0:NE].unsqueeze(1).unsqueeze(1).to_broadcast(full), ALU.is_equal))
            chain(V.tensor_reduce(msk, choice.rearrange("p a q e -> p a e q"), AX.X, ALU.add))
            dve.sem_inc(mask_ready, 1)
            chain(TT(weighed, choice, iota[:, 0:TOPK].unsqueeze(1).unsqueeze(3).to_broadcast(full), ALU.mult))
            chain(V.tensor_reduce(val[:, :, 0:NE, 1], weighed.rearrange("p a q e -> p a e q"), AX.X, ALU.add))
            chain(TT(val[:, :, 0:NE, 1], val[:, :, 0:NE, 1], row4.unsqueeze(2).to_broadcast([P, NT, NE]), ALU.add))
            dve.wait_ge(rank_fill, 1)
            STT(pos[:, 0:2, 0:NE], c3(PS[:, 7, 0:2 * NE], NE), 1.0, msk[:, 0:2, :], ALU.add, ALU.mult)
            chain(STT(pos[0:NSM, 2, 0:NE], PS[0:NSM, 7, 2 * NE:3 * NE], 1.0, msk[0:NSM, 2, :], ALU.add, ALU.mult))
            TS(pos[:, :, 0:NE], pos[:, :, 0:NE], -1.0, None, ALU.add)
            chain(V.tensor_reduce(cnt, PS[:, 7, NT * NE:(NT + 1) * NE], AX.X, ALU.max))
            chain(V.tensor_copy(cnt_i[0:1, :], cnt[0:1, :]))
            dve.sem_inc(rank_read, 2)

            def gates():
                dve.wait_ge(ge_ready, 1)
                chain(V.reciprocal(gls, gls))
                chain(TT(gt4, gt4, gls.unsqueeze(2).to_broadcast([P, NT, TOPK]), ALU.mult))
                chain(TT(weighed, choice, gt4.unsqueeze(3).to_broadcast(full), ALU.mult))
                chain(V.tensor_reduce(gD, weighed.rearrange("p a q e -> p a e q"), AX.X, ALU.add))
                chain(V.tensor_copy(val[:, :, 0:NE, 0], gD))
                dve.sem_inc(val_ready, 1)
                dve.sem_inc(bb_used, 1)

            def lchain(base, k, ins):
                ins.then_inc(dve_loop, 1)
                dve.wait_ge(dve_loop, base + (k + 1))

            def place(n, e):
                for i, (a, m) in enumerate(TILES):
                    last = TS(onehot[0:m, i, :], iota[0:m, :], pos[0:m, i, bass.ds(e, 1)], None, ALU.is_equal)
                last.then_inc(oh_ready, 1)

            def info(n, e):
                dve.wait_ge(info_fill, n + 1)
                V.tensor_copy(infos[:, bass.ds(e, 1), :].rearrange("p a c -> p (a c)"), PS[:, 3, 0:2]).then_inc(info_ready, 1)

            def low_rows(it):
                dve.wait_ge(xh_ready, it + 1)
                halves = [v.rearrange("p (b c) k -> p b (c k)", b=2) for v in (XL, XH.bitcast(F32))]
                TT(halves[0], PS[:, 6:8, :], halves[1], ALU.subtract).then_inc(xl_ready, 1)

            def low_hidden(it, h):
                dve.wait_ge(hh_ready, 2 * it + (h + 1))
                part = slice(4 * h, 4 * h + 4)
                TT(HL[:, part, :], c3(PS[:, h, :], P), HH[:, part, :].bitcast(F32), ALU.subtract).then_inc(hl_ready, 1)

            LK = 10

            def expert_dve(tp):
                base = tp * NE
                if not isinstance(tp, int):
                    chain_tp = V.tensor_scalar(pos, pos, -float(CAP), None, ALU.add)
                    lchain(tp * (NE * LK + 1) - 1, 0, chain_tp)
                lb0 = tp * (NE * LK + 1)

                def glu_first(it, lb, h):
                    dve.wait_ge(parts_used, it * PARTS + (SPLITS + 8 * h + 8))
                    if h == 0:
                        dve.wait_ge(bb_ready, it + 1)
                    else:
                        dve.wait_ge(hb_ready, 2 * it + 1)
                    TT(u1, PS[:, 2 * h + 1, :], bb[:, FF + 512 * h:FF + 512 * h + 512], ALU.add)
                    lchain(lb, (0, 4)[h], TT(g1, PS[:, 2 * h, :], bb[:, 512 * h:512 * h + 512], ALU.add))
                    lchain(lb, (1, 5)[h], TS(g1, g1, LIMIT, None, ALU.min))
                    dve.sem_inc(g1_ready, 1)

                def glu_last(it, lb, h):
                    lchain(lb, (2, 8)[h], TS(u1, u1, LIMIT, -LIMIT, ALU.min, ALU.max))
                    lchain(lb, (3, 9)[h], STT(u1, u1, 1.0, g1, ALU.add, ALU.mult))
                    dve.wait_ge(e_ready, 2 * it + (h + 1))
                    TT(hb[:, 512 * h:512 * h + 512], u1, e1, ALU.mult).then_inc(hb_ready, 1)

                def body(it, e, more):
                    lb = lb0 + e * LK
                    low_parts(it, 6, 14)
                    glu_first(it, lb, 0)
                    if more:
                        place(it + 1, e + 1)
                    low_parts(it, 14, 15)
                    glu_last(it, lb, 0)
                    low_parts(it, 15, 20)
                    glu_first(it, lb, 1)
                    dve.sem_inc(bb_used, 1)
                    low_hidden(it, 0)
                    low_parts(it, 20, 21)
                    dve.wait_ge(rows_out, it + 1)
                    cur = infos[:, bass.ds(e, 1), :].rearrange("p a c -> p (a c)")
                    lchain(lb, 6, V.tensor_copy(gcur, cur[:, 0:1]))
                    lchain(lb, 7, TS(idx_cur[:, 0:1], cur[:, 1:2], OFF, None, ALU.add))
                    dve.sem_inc(cur_ready, 1)
                    glu_last(it, lb, 1)
                    low_parts(it, 21, 22)
                    if more:
                        low_rows(it + 1)
                    low_parts(it, 22, 24)
                    low_hidden(it, 1)
                    if more:
                        info(it + 1, e + 1)
                        dve.wait_ge(info_ready, it + 2)
                        low_parts(it + 1, 0, 6)

                place(base, 0)
                if isinstance(tp, int):
                    gates()
                else:
                    low_parts(base, 0, SPLITS)
                info(base, 0)
                dve.wait_ge(info_ready, base + 1)
                low_rows(base)
                with dve.Fori(0, NE - 1) as e:
                    body(tp * NE + e, e, True)
                body(tp * NE + (NE - 1), NE - 1, False)

            expert_dve(0)
            most = dve.value_load(cnt_i[0:1, 0:1], min_val=0, max_val=NTOK)
            with dve.Fori(1, NT) as tp:
                with dve.If(most > tp * CAP):
                    expert_dve(tp)
                dve.nop()
            dve.nop()
            dve.wait_ge(rt_copy, 6 + len(TURNS))
            for i, (a, m) in enumerate(TILES):
                biased = h2n[0:m, i, :]
                dve.wait_ge(bd_fill, i + 1)
                chain(TT(c3(biased, 512), PS[0:m, BIAS_BANKS[i]:BIAS_BANKS[i] + 2, :], c3(ga2n[0:m, i // 2, :], 512), ALU.mult))
                chain(TT(acc[0:m, i, :], acc[0:m, i, :], biased, ALU.add))
            dve.sem_inc(acc_ready, 1)
            for i in range(2):
                dve.wait_ge(back[i], 16)
                rows = ring[:, 2 * i:2 * i + 2, :].rearrange("p s (k n) -> p (s k) n", n=D)
                chain(TT(rows[:, 0:2, :], rows[:, 0:2, :], rows[:, 2:4, :], ALU.add))
                chain(TT(rows[:, 0, :], rows[:, 0, :], rows[:, 1, :], ALU.add))
                chain(TT(rows[:, 0, :], rows[:, 0, :], ga2n[:, 0, :], ALU.mult))
                chain(TT(acc[:, i, :], acc[:, i, :], rows[:, 0, :], ALU.add))
                dve.sem_inc(y_ready, 1)

        @block.tensor
        def _(pe):
            T = nc.tensor

            def mm(out, lhsT, rhs, start, stop):
                return T.matmul(out, lhsT, rhs, start=start, stop=stop, skip_group_check=True)

            pe.sem_inc(parts_used, SPLITS)
            pe.wait_ge(in_const, 16)
            pe.wait_ge(c_silu, 1)
            for k in range(DT):
                last = T.transpose(PS[:, 0, 9 * k:9 * k + 9], cn[0:9, k * P:(k + 1) * P], ident[0:9, 0:9])
            last.then_inc(set_fill, 1)
            T.transpose(PS[:, 1, 0:NMOD * DT], ban[0:NMOD * DT, :], ident[0:NMOD * DT, 0:NMOD * DT])
            T.transpose(PS[:, 1, NMOD * DT:NMOD * DT + 2 * DT], gn[0:2 * DT, :], ident[0:2 * DT, 0:2 * DT]).then_inc(set_fill, 1)
            pe.wait_ge(in_x, 32)
            for n in range(6):
                i, q = divmod(n, 2)
                m = TILES[i][1]
                for k in range(4):
                    last = T.transpose(PS[:, n + 2, k * P:k * P + m], xn[0:m, i, (4 * q + k) * P:(4 * q + k + 1) * P], ident[0:m, 0:m])
                last.then_inc(set_fill, 1)

            def sum_squares(k):
                pe.wait_ge(sq_ready, 2 * k + 1)
                for m in range(DT):
                    if k and m == 4:
                        pe.wait_ge(sq_ready, 3)
                    last = mm(PS[:, 0, 0:NTOK], ones, hT[:, m, :], m == 0, m == DT - 1)
                last.then_inc(ssq_done, 1)

            def modulation(c):
                for k in range(DT):
                    n = DT * c + k
                    if n == 6:
                        sum_squares(0)
                    await_chunk(pe, n)
                    for q in range(4):
                        last = mm(PS[0:9, 4 - 4 * (c % 2) + q, :], sT[:, k, :], slot4(n)[:, q, :], k == 0, k == DT - 1)
                    last.then_inc(used, 1)

            def turn_modulation(c, bank):
                pe.wait_ge(mod_copy, c + 1)
                for m in range(16):
                    last = T.transpose(PS[:, bank, 9 * m:9 * m + 9], mod_rows[0:9, c % 2, m * P:(m + 1) * P], ident[0:9, 0:9])
                last.then_inc(mod_fill, 1)

            pe.wait_ge(set_copy, 8)
            modulation(0)
            pe.wait_ge(ms_ready, 1)
            modulation(1)
            turn_modulation(0, 4)
            pe.wait_ge(mod_ready, 1)
            modulation(2)
            turn_modulation(1, 0)
            turn_modulation(2, 1)

            def three(out, xh, xl, wh, wl, start, stop):
                mm(out, xh, wh, start, False)
                mm(out, xh, wl, False, False)
                return mm(out, xl, wh, False, stop)

            halves = [0]

            def next_half():
                pe.wait_ge(mix_low, halves[0] + 1)
                halves[0] += 1
                return mix_part(halves[0] - 1)

            def turned(n0, parts, bank, kts, await_half=None, only=None):
                xh, xl = parts
                for q in only or range(kts // 2):
                    if await_half:
                        await_half(q)
                    wh, wl = next_half()
                    for m in range(4):
                        for k in range(2):
                            at, cols = 2 * q + k, slice(m * P, (m + 1) * P)
                            last = three(PS[:, bank + m, 0:NTOK], wh[:, k, cols], wl[:, k, cols], xh[:, at, :], xl[:, at, :],
                                         at == 0, at == kts - 1)
                    last.then_inc(used if q % 2 else halves_used, 1)
                return n0 + kts // 4

            def natural(n0, bank):
                xh, xl = hP
                for q in range(DT // 2):
                    wh, wl = next_half()
                    for i, (a, m) in enumerate(TILES):
                        for k in range(2):
                            at = 2 * q + k
                            last = three(PS[0:m, bank + i, :], xh[:, at, a:a + m], xl[:, at, a:a + m], wh[:, k, :], wl[:, k, :],
                                         at == 0, at == DT - 1)
                    last.then_inc(used if q % 2 else halves_used, 1)
                return n0 + 2

            pe.wait_ge(hp_low, 1)
            n = 3 * DT
            for at, c in enumerate(PROJ):
                if at >= 2:
                    pe.wait_ge(proj_free, at - 1)
                if at == 1:
                    pe.wait_ge(mod_ready, 3)
                n = turned(n, hP, proj_bank(at), DT) if c in (Q_SB, K_SB) else natural(n, proj_bank(at))
            pe.wait_ge(proj_free, 6)
            for q in range(9):
                kind, i = divmod(q, 3)
                a, m = TILES[i]
                if kind:
                    pe.wait_ge(nat_ready, kind)
                if q == 8:
                    pe.wait_ge(tr_free, 1)
                for p in range(PAIRS):
                    if kind == 0:
                        last = T.transpose(PS[0:m, q % 8, p * P:(p + 1) * P], kT[0][:, p, a:a + m], ident)
                    else:
                        last = T.transpose(PS[:, q % 8, p * P:p * P + m], nat[kind - 1][0:m, i, p * P:(p + 1) * P], ident[0:m, 0:m])
                last.then_inc(tr_fill, 1)

            pe.wait_ge(tr_free, 9)

            def prompt_scores(j):
                r, p = divmod(j, 4)
                if j >= 2:
                    pe.wait_ge(pz_free, j - 1)
                for h in range(2):
                    rows = slice(HD * h, HD * h + HD)
                    bank = 2 * (j % 2) + h
                    mm(PS[:, bank, 0:P], qT[r][rows, p, 0:P], kT[r][rows, p, 0:P], True, True)
                    last = mm(PS[:, bank, P:3 * P], qT[r][rows, p, P:2 * P], kT[r][rows, p, 0:2 * P], True, True)
                last.then_inc(pz_fill, 1)

            def turn_prompt(j):
                pe.wait_ge(pw_ready, j + 1)
                for h in range(2):
                    for b in range(3):
                        last = T.transpose(PS[:, 5 + h, b * P:(b + 1) * P], pt2[j % 2][:, h, b * P:(b + 1) * P], ident)
                last.then_inc(at_fill, 1)

            def prompt_values(j):
                r, p = divmod(j, 4)
                pe.wait_ge(at_copy, j + 1)
                if j:
                    pe.wait_ge(po_copy, j)
                for h in range(2):
                    v = [vn[r][:, i, (2 * p + h) * HD:(2 * p + h + 1) * HD] for i in range(2)]
                    out = PS[HD * h:HD * h + HD, 7, :]
                    mm(out[:, 0:2 * P], v[0], pAT[:, h, 0:2 * P], True, False)
                    last = mm(out[:, P:2 * P], v[1], pAT[:, h, 2 * P:3 * P], False, True)
                last.then_inc(po_fill, 1)

            def turn_keys(gi, hh):
                chunk = page_chunk["k", gi, hh]
                await_chunk(pe, chunk)
                for pg in range(HALF):
                    tp = 32 * gi + HALF * hh + pg
                    if tp >= 4:
                        pe.wait_ge(kt_act if tp % 2 == 0 else kt_dve, tp // 2 - 1)
                    for p in range(PAIRS):
                        last = T.transpose(PS[:, key_bank(tp), p * P:(p + 1) * P], slot4(chunk)[:, pg, p * P:(p + 1) * P], ident)
                    last.then_inc(kt_fill, 1)

            def row_scores(gi, hh):
                g = gi % 2
                b, hf = divmod(hh, 2)
                for s in (kt_act, kt_dve):
                    pe.wait_ge(s, 2 * (8 * gi + hh + 1))
                for p in range(PAIRS):
                    last = mm(PS[32 * b:32 * b + 32, 2 + hf, :], QP[:, 4 * g + b, p, :], KT[:, hh % 2, p, :], p == 0, p == PAIRS - 1)
                last.then_inc(used, 1)

            def scores(gi):
                r, g = divmod(gi, 2)
                turn_keys(gi, 0)
                if gi >= 2:
                    turn_product(gi - 2)
                pe.wait_ge(qp_ready, r + 1)
                if gi:
                    pe.wait_ge(z_copy, gi)
                for hh in range(8):
                    if hh < 7:
                        turn_keys(gi, hh + 1)
                    row_scores(gi, hh)
                for b in range(4):
                    for p in range(PAIRS):
                        last = mm(PS[32 * b:32 * b + 32, 4, 0:NSM], QP[:, 4 * g + b, p, :], kT[r][:, p, NPR:NTOK], p == 0, p == PAIRS - 1)
                last.then_inc(s_fill, 1)

            def turn_weights(gi):
                pe.wait_ge(aw_ready, gi + 1)
                if gi:
                    pe.wait_ge(oh_copy, gi)
                for pg in range(PAGES):
                    T.transpose(PS[:, 5 + pg // 4, (pg % 4) * P:(pg % 4 + 1) * P], T2[:, pg * P:(pg + 1) * P], ident)
                T.transpose(PS[0:NSM, 7, 0:P], T2[:, PAST:ROWW], ident).then_inc(aw_fill, 1)

            def new_values(gi):
                pe.wait_ge(aw_copy, gi + 1)
                pe.wait_ge(z_copy, min(gi + 2, 4))
                mm(PS[:, 4, :], AT[0:NSM, PAGES, :], vn[gi // 2][0:NSM, 2, :], True, False)

            def values(gi, hh):
                b, hf = divmod(hh, 2)
                chunk = page_chunk["v", gi, hh]
                await_chunk(pe, chunk)
                for pg in range(HALF):
                    last = mm(PS[32 * b:32 * b + 32, 4, :], AT[:, HALF * hf + pg, 32 * b:32 * b + 32], slot4(chunk)[:, pg, :],
                              False, hf == 1 and pg == HALF - 1)
                last.then_inc(used, 1)

            BESIDE = [{1: (turn_prompt, 2 * gi), 2: (prompt_values, 2 * gi),
                       4: (turn_prompt, 2 * gi + 1), 5: (prompt_values, 2 * gi + 1)} for gi in range(2)]
            BESIDE += [{hh: ((turn_prompt, prompt_values)[hh % 2], 4 + hh // 2) for hh in range(8)}]

            def turn_product(gi):
                pe.wait_ge(pv_copy, gi + 1)
                for p in range(PAIRS):
                    last = T.transpose(PS[:, 7, p * P:(p + 1) * P], pv_rows[:, p * P:(p + 1) * P], ident)
                last.then_inc(pt_fill, 1)

            scores(0)
            scores(1)
            for gi in range(3):
                turn_weights(gi)
                new_values(gi)
                first = min(2 * gi, 4)
                prompt_scores(first)
                prompt_scores(first + 1)
                for hh in range(8):
                    values(gi, hh)
                    step, j = BESIDE[gi].get(hh, (None, 0))
                    if step:
                        step(j)
                    if gi == 2 and hh in (0, 2):
                        prompt_scores(j + 2)
                if gi < 2:
                    scores(gi + 2)
                else:
                    turn_product(2)
            pe.wait_ge(po_copy, 8)
            turn_weights(3)
            new_values(3)
            for hh in range(8):
                values(3, hh)
                if hh % 2:
                    s, kh = hh // 4, hh // 2 % 2
                    if s:
                        pe.wait_ge(gate_ready, s)
                    turned(0, hP, 0, DT, only=(2 * kh, 2 * kh + 1))
            turn_product(3)
            pe.wait_ge(oh_copy, 4)
            for s in range(4):
                r = s // 2
                if s >= 2:
                    pe.wait_ge(gate_ready, s)
                    turned(0, hP, 0, DT)
                if s:
                    pe.wait_ge(b_free, s)
                pe.wait_ge(op_low, r + 1)
                turned(0, oP, 4, PAIRS)
            n = BRANCH_END[-1]
            pe.wait_ge(b_free, 4)
            for c in range(2):
                n = turned(n, hP, 4 * c, DT, lambda q: pe.wait_ge(up_low, q // 2 + 1))
            assert n == NSTREAM
            sum_squares(1)
            pe.wait_ge(h_ready, 2)
            for i, (a, m) in enumerate(TILES):
                for k in range(DT):
                    last = mm(PS[0:m, 6, NE * i:NE * i + NE], hT[:, k, a:a + m], wr[:, k, :], k == 0, k == DT - 1)
            last.then_inc(lg_fill, 1)
            for q in range(6):
                i, hf = divmod(q, 2)
                a, m = TILES[i]
                for k in range(4):
                    last = T.transpose(PS[0:m, q, k * P:(k + 1) * P], hT[:, 4 * hf + k, a:a + m], ident)
                last.then_inc(rt_fill, 1)
            pe.wait_ge(mask_ready, 1)
            for i, (a, m) in enumerate(TILES):
                out = PS[0:m, 7, NE * i:NE * i + NE]
                for k in range(i + 1):
                    mk = TILES[k][1]
                    mm(out, (below if k == i else ones)[0:mk, 0:m], msk[0:mk, k, :], k == 0, k == i)
            for k, (a, m) in enumerate(TILES):
                last = mm(PS[:, 7, NT * NE:(NT + 1) * NE], ones[0:m, :], msk[0:m, k, :], k == 0, k == NT - 1)
            last.then_inc(rank_fill, 1)
            pe.wait_ge(rt_copy, 6)

            def gather(it):
                pe.wait_ge(oh_ready, it + 1)
                for k in range(DT):
                    for i, (a, m) in enumerate(TILES):
                        last = mm(PS[:, 6 + k // 4, (k % 4) * P:(k % 4 + 1) * P], h2n[0:m, i, k * P:(k + 1) * P],
                                  onehot[0:m, i, :], i == 0, i == NT - 1)
                last.then_inc(gathered, 1)

            def gather_info(e):
                for i, (a, m) in enumerate(TILES):
                    last = mm(PS[:, 3, 0:2], onehot[0:m, i, :], val[0:m, i, bass.ds(e, 1), :].rearrange("p a c -> p (a c)"),
                              i == 0, i == NT - 1)
                last.then_inc(info_fill, 1)

            def parts(it, q):
                if of_pool(q):
                    pe.wait_ge(low_pool, pool_lows(it, q))
                else:
                    pe.wait_ge(low_dve, dve_lows(it, q))
                return WH[:, q % SPLITS, :], WL[:, q % SPLITS, :]

            def turn_hidden(it, h):
                pe.wait_ge(hb_ready, 2 * it + (h + 1))
                for k in range(4):
                    at = (4 * h + k) * P
                    last = T.transpose(PS[:, h, k * P:(k + 1) * P], hb[:, at:at + P], ident)
                last.then_inc(hg_fill, 1)

            def down(it, j):
                for k in range(2 * j, 2 * j + 2):
                    wh, wl = parts(it, 16 + k)
                    for hf in range(2):
                        cols = slice(512 * hf, 512 * hf + 512)
                        last = three(PS[:, 4 + hf, :], HH[:, k, :], HL[:, k, :], wh[:, cols], wl[:, cols], k == 0, k == DT - 1)
                    last.then_inc(parts_used, 1)

            def expert_pe(tp):
                def body(it, e, more):
                    pe.wait_ge(xl_ready, it + 1)
                    for j, (h, kh, gu) in enumerate(GU):
                        if j == 4:
                            pe.wait_ge(info_ready, it + 1)
                        for k in range(4 * kh, 4 * kh + 4):
                            if k % 2 == 0:
                                wh, wl = (c3(w, 512) for w in parts(it, 2 * j + k % 4 // 2))
                            last = three(PS[:, 2 * h + gu, :], XH[:, k, :], XL[:, k, :], wh[:, k % 2, :], wl[:, k % 2, :],
                                         k == 0, k == DT - 1)
                            if k % 2:
                                last.then_inc(parts_used, 1)
                    turn_hidden(it, 0)
                    if more:
                        gather(it + 1)
                    pe.wait_ge(hl_ready, 2 * it + 1)
                    pe.wait_ge(y_scaled, it + 1)
                    down(it, 0)
                    turn_hidden(it, 1)
                    if more:
                        gather_info(e + 1)
                    down(it, 1)
                    pe.wait_ge(hl_ready, 2 * it + 2)
                    down(it, 2)
                    down(it, 3)

                gather(tp * NE)
                if isinstance(tp, int):
                    pe.wait_ge(val_ready, 1)
                gather_info(0)
                with pe.Fori(0, NE - 1) as e:
                    body(tp * NE + e, e, True)
                body(tp * NE + (NE - 1), NE - 1, False)

            expert_pe(0)
            most = pe.value_load(cnt_i[0:1, 0:1], min_val=0, max_val=NTOK)
            with pe.Fori(1, NT) as tp:
                with pe.If(most > tp * CAP):
                    expert_pe(tp)
                pe.nop()
            pe.nop()
            pe.wait_ge(gx_ready, 1)
            pe.wait_ge(in_bd, 16)

            def weighted_biases(i):
                a, m = TILES[i]
                for hf in range(2):
                    last = mm(PS[0:m, BIAS_BANKS[i] + hf, :], GT[:, a:a + m], bdn[0:NE, 512 * hf:512 * hf + 512], True, True)
                last.then_inc(bd_fill, 1)

            for n, (bank, kind, i, hf, m) in enumerate(TURNS):
                if n >= len(banks):
                    pe.wait_ge(rt_copy, 6 + n - len(banks) + 1)
                if kind == "gates":
                    for i, (a, m) in enumerate(TILES):
                        last = T.transpose(PS[0:NE, bank, a:a + m], gD[0:m, i, :], ident[0:m, 0:m])
                else:
                    for k in range(4):
                        f = 4 * hf + k
                        if kind == "x1":
                            src = xT[:, f, TILES[i][0]:TILES[i][0] + m]
                        else:
                            src = modT[:, 5 * DT + f, 0:1].to_broadcast([P, P]) if i == 0 else gx[:, f, :]
                        last = T.transpose(PS[0:m, bank, k * P:(k + 1) * P], src, ident)
                last.then_inc(rt_fill, 1)
                if n == 6:
                    pe.wait_ge(rt_copy, 6 + 1)
                    weighted_biases(0)
            pe.wait_ge(rt_copy, 6 + len(TURNS))
            weighted_biases(1)
            weighted_biases(2)


_INS = ["x_prompt", "x_sample", "c_prompt", "c_sample", "cache_sb_k", "cache_sb_v", "cache_mb_k", "cache_mb_v",
        "page_table", "w_ada", "b_ada", "g_norm1", "g_norm2", "w_in", "q_norm_g", "k_norm_g", "w_br_sb", "w_br_mb",
        "w_out", "w_router", "b_router", "w_gu", "b_gu", "w_down", "b_down"]
_OUTS = [("y_prompt", (1, NPR, D)), ("y_sample", (NSEQ, NNEW, D))]
_OUTS += [(f"{r}_{x}_prompt", (1, 1, NPR, HEADS, HD)) for r in ("sb", "mb") for x in "kv"]
_OUTS += [(f"{r}_{x}_sample", (1, NSEQ, NNEW, HEADS, HD)) for r in ("sb", "mb") for x in "kv"]


def kernel(**inputs):
    import concourse.bacc as _bacc
    from concourse.bass_utils import run_bass_kernel_spmd as _run

    nc = _bacc.Bacc("TRN2", target_bir_lowering=False, num_devices=1)
    arrays, ins, outs = {}, {}, {}
    for name in _INS:
        a = np.ascontiguousarray(inputs[name])
        arrays[f"in_{name}"] = a
        ins[name] = nc.dram_tensor(f"in_{name}", a.shape, mybir.dt.from_np(a.dtype), kind="ExternalInput").ap()
    arrays["constants"] = constants()
    ins["constants"] = nc.dram_tensor("constants", (P, NCONST), F32, kind="ExternalInput").ap()
    for name, shape in _OUTS:
        outs[name] = nc.dram_tensor(f"out_{name}", shape, F32, kind="ExternalOutput").ap()
    build(nc, ins, outs)
    r = _run(nc, [arrays], core_ids=[0])
    return tuple(r.results[0][f"out_{name}"] for name, _ in _OUTS)
```
